# Optimizing a Trainium2 kernel written in Bass

```python
import jax, jax.numpy as jnp
from jax import lax
import numpy as np

D_MODEL = 1024
BATCH = 1
SEQ = 128
DEPTH = 1
DEC_BATCH = 1
DEC_SEQ = 128
PAST_LEN = 128

GRID_W = 64
MIX_WIDTH = D_MODEL
NA_HEADS = 8
NA_HEAD_DIM = 64
NA_WIDTH = NA_HEADS * NA_HEAD_DIM
NA_KH = 8
NA_KW = 16
NA_QBW = 16
NA_KSPAN = 2 * NA_QBW
HG_HEADS = 4
HG_DK = 64
HG_DV = 64
HG_WIDTH = HG_HEADS * HG_DV
HG_CHUNK = 32
F_FLOOR = 1e-30
GM_GROUPS = 4
GM_GDIM = 64
GM_WIDTH = GM_GROUPS * GM_GDIM
GM_CHUNK = 128
IN_COLS = 3 * NA_WIDTH + 5 * HG_WIDTH + 2 * GM_WIDTH
N_EXPERTS = 32
TOP_K = 4
D_EXPERT = D_MODEL
MOE_BLOCK = 128
SWIGLU_LIMIT = 7.0
SWIGLU_ALPHA = 1.702
RMS_EPS = 1e-6
NEG_INF = -1e30

kernel_name = 'hybrid_natten_hgrn2_gmlp_moe_dit_step'

def rmsnorm(x, g):
    xf = x.astype(jnp.float32)
    y = xf * lax.rsqrt(jnp.mean(xf * xf, axis=-1, keepdims=True) + RMS_EPS)
    return (y * g.astype(jnp.float32)).astype(x.dtype)

def ada_modulation(cond, w, b):
    m = (cond @ w + b)[:, None, :]
    return jnp.split(m, 6, axis=-1)

def modulate(h, shift, scale):
    return h * (1.0 + scale) + shift

def dense_attention(q, k, v):
    B, N, H, Dh = q.shape
    s = jnp.einsum('bqhd,bkhd->bhqk', q, k).astype(jnp.float32) * (Dh ** -0.5)
    p = jax.nn.softmax(s, axis=-1).astype(v.dtype)
    return jnp.einsum('bhqk,bkhd->bqhd', p, v).reshape(B, N, H * Dh)

def neighbourhood_attention(q, k, v, ck, cv, rel_bias):
    B, N, H, Dh = q.shape
    rows = N // GRID_W
    kh = min(NA_KH, rows)
    nb = GRID_W // NA_QBW
    r = np.arange(rows)
    row_idx = np.clip(r - kh // 2, 0, rows - kh)[:, None] + np.arange(kh)[None, :]
    dr_idx = row_idx - r[:, None] + NA_KH - 1
    qcol = (np.arange(nb) * NA_QBW)[:, None] + np.arange(NA_QBW)[None, :]
    col_idx = (np.clip(np.arange(nb) * NA_QBW - NA_KW // 2, 0, GRID_W - NA_KSPAN)[:, None]
               + np.arange(NA_KSPAN)[None, :])
    q_start = np.clip(qcol - NA_KW // 2, 0, GRID_W - NA_KW)
    kc = col_idx[:, None, :]
    in_win = (kc >= q_start[:, :, None]) & (kc < q_start[:, :, None] + NA_KW)
    dc_idx = np.clip(kc - qcol[:, :, None] + NA_KW - 1, 0, 2 * NA_KW - 2)
    bias = rel_bias[:, dr_idx[:, None, None, :, None], dc_idx[None, :, :, None, :]].astype(jnp.float32)
    ri = row_idx[:, None, :, None]
    ci = col_idx[None, :, None, :]
    kg = k.reshape(B, rows, GRID_W, H, Dh)[:, ri, ci]
    vg = v.reshape(B, rows, GRID_W, H, Dh)[:, ri, ci]
    qb = q.reshape(B, rows, nb, NA_QBW, H, Dh)
    scale = Dh ** -0.5
    s_loc = jnp.einsum('brnqhd,brnkjhd->bhrnqkj', qb, kg).astype(jnp.float32) * scale + bias[None]
    s_loc = jnp.where(in_win[:, :, None, :][None], s_loc, NEG_INF)
    nloc = kh * NA_KSPAN
    s_loc = s_loc.reshape(B, H, rows, nb, NA_QBW, nloc)
    s_ctx = jnp.einsum('brnqhd,blhd->bhrnql', qb, ck).astype(jnp.float32) * scale
    p = jax.nn.softmax(jnp.concatenate([s_loc, s_ctx], axis=-1), axis=-1)
    p_loc = p[..., :nloc].reshape(B, H, rows, nb, NA_QBW, kh, NA_KSPAN).astype(v.dtype)
    p_ctx = p[..., nloc:].astype(v.dtype)
    o = (jnp.einsum('bhrnqkj,brnkjhd->brnqhd', p_loc, vg)
         + jnp.einsum('bhrnql,blhd->brnqhd', p_ctx, cv))
    return o.reshape(B, N, H * Dh)

def chunk_scan(q, k, v, logf, s0):
    B, N, H, DK = q.shape
    DV = v.shape[-1]
    C = HG_CHUNK
    n = N // C
    q, k, v, logf = (t.reshape(B, n, C, H, t.shape[-1]) for t in (q, k, v, logf))
    b = jnp.cumsum(logf, axis=2)
    causal = np.tril(np.ones((C, C), dtype=bool))[None, None, :, :, None, None]
    diff = b[:, :, :, None] - b[:, :, None, :]
    decay = jnp.where(causal, jnp.exp(jnp.where(causal, diff, 0.0)), 0.0)
    a = jnp.einsum('bnthk,bnshk,bntshk->bnhts', q, k, decay)
    o_intra = jnp.einsum('bnhts,bnshv->bnthv', a, v)
    b_last = b[:, :, -1]
    q_in = q * jnp.exp(b)
    k_st = k * jnp.exp(b_last[:, :, None] - b)
    chunk_decay = jnp.exp(b_last)

    def step(S, xs):
        qc, kc, vc, dc = xs
        o = jnp.einsum('bthk,bhkv->bthv', qc, S)
        S = S * dc[..., None] + jnp.einsum('bthk,bthv->bhkv', kc, vc)
        return S, o

    xs = tuple(jnp.moveaxis(t, 1, 0) for t in (q_in, k_st, v, chunk_decay))
    S, o_inter = lax.scan(step, s0, xs)
    o = o_intra + jnp.moveaxis(o_inter, 0, 1)
    return o.reshape(B, N, H, DV), S

def hgrn2_mixer(q, zf, zb, i, g, lower_l, onorm_g, s0f, s0b):
    B, N, _ = q.shape
    f32 = jnp.float32

    def heads(t):
        return t.astype(f32).reshape(B, N, HG_HEADS, HG_DK)

    def gates(z, lb):
        z = heads(z)
        lb = lb.reshape(HG_HEADS, HG_DK)
        f = lb + (1.0 - lb) * jax.nn.sigmoid(z)
        logf = jnp.log(jnp.maximum(f, F_FLOOR))
        key = (1.0 - lb) * jax.nn.sigmoid(-z)
        return logf, key

    qh = heads(q)
    vh = i.astype(f32).reshape(B, N, HG_HEADS, HG_DV)
    logf_f, k_f = gates(zf, lower_l[0])
    logf_b, k_b = gates(zb, lower_l[1])
    o_f, sf = chunk_scan(qh, k_f, vh, logf_f, s0f.astype(f32))
    o_b, sb = chunk_scan(qh[:, ::-1], k_b[:, ::-1], vh[:, ::-1], logf_b[:, ::-1], s0b.astype(f32))
    o = o_f + o_b[:, ::-1]
    o = o * lax.rsqrt(jnp.mean(o * o, axis=-1, keepdims=True) + RMS_EPS) * onorm_g.astype(f32)
    o = o.reshape(B, N, HG_WIDTH) * jax.nn.silu(g.astype(f32))
    return o.astype(q.dtype), sf, sb

def chunk_mlp(u, v, vnorm_g, ws, bs):
    B, N, _ = u.shape
    nc = N // GM_CHUNK
    vg = rmsnorm(v, vnorm_g).reshape(B, nc, GM_CHUNK, GM_GROUPS, GM_GDIM)
    z = jnp.einsum('gts,bnsgc->bntgc', ws, vg) + bs.T[:, :, None]
    return u * z.reshape(B, N, GM_WIDTH)

def token_mixer(h, w_in_l, w_out_l, rel_bias_l, lower_l, onorm_g_l, vnorm_g_l, ws_l, bs_l, ctx):
    B, N, _ = h.shape
    sizes = [NA_WIDTH] * 3 + [HG_WIDTH] * 5 + [GM_WIDTH] * 2
    splits = np.cumsum(sizes)[:-1].tolist()
    aq, ak, av, hq, hzf, hzb, hi, hgate, gu, gv = jnp.split(h @ w_in_l, splits, axis=-1)
    aq, ak, av = (t.reshape(B, N, NA_HEADS, NA_HEAD_DIM) for t in (aq, ak, av))
    if ctx is None:
        att = dense_attention(aq, ak, av)
        s0f = jnp.zeros((B, HG_HEADS, HG_DK, HG_DV), jnp.float32)
        s0b = s0f
    else:
        ck, cv, s0f, s0b = ctx
        att = neighbourhood_attention(aq, ak, av, ck, cv, rel_bias_l)
    rec, sf, sb = hgrn2_mixer(hq, hzf, hzb, hi, hgate, lower_l, onorm_g_l, s0f, s0b)
    mlp = chunk_mlp(gu, gv, vnorm_g_l, ws_l, bs_l)
    out = jnp.concatenate([att, rec, mlp], axis=-1) @ w_out_l
    return out, (ak, av, sf, sb)

def swiglu_expert(xb, wg, bg, wu, bu, wd, bd):
    gate = jnp.minimum(xb @ wg + bg, SWIGLU_LIMIT)
    up = jnp.clip(xb @ wu + bu, -SWIGLU_LIMIT, SWIGLU_LIMIT)
    glu = gate * jax.nn.sigmoid(SWIGLU_ALPHA * gate)
    return ((up + 1.0) * glu) @ wd + bd

def routed_moe(h, wr, br, wg, bg, wu, bu, wd, bd):
    B, N, D = h.shape
    T = B * N
    A = T * TOP_K
    hf = h.reshape(T, D)
    logits = (hf @ wr + br).astype(jnp.float32)
    top_v, top_i = lax.top_k(logits, TOP_K)
    gates = jax.nn.softmax(top_v, axis=-1)
    flat_e = top_i.reshape(A)
    flat_t = jnp.repeat(jnp.arange(T, dtype=jnp.int32), TOP_K)
    flat_w = gates.reshape(A)
    order = jnp.argsort(flat_e)
    se, st, sw = flat_e[order], flat_t[order], flat_w[order]
    counts = jnp.bincount(flat_e, length=N_EXPERTS)
    padded = (counts + MOE_BLOCK - 1) // MOE_BLOCK * MOE_BLOCK
    pad_end = jnp.cumsum(padded)
    pad_start = pad_end - padded
    start = jnp.cumsum(counts) - counts
    dest = pad_start[se] + jnp.arange(A, dtype=jnp.int32) - start[se]
    n_blocks = (A + N_EXPERTS * (MOE_BLOCK - 1) + MOE_BLOCK - 1) // MOE_BLOCK
    n_slots = n_blocks * MOE_BLOCK
    slot_tok = jnp.zeros((n_slots,), jnp.int32).at[dest].set(st)
    slot_w = jnp.zeros((n_slots,), jnp.float32).at[dest].set(sw)
    blk_e = jnp.minimum(jnp.searchsorted(pad_end, jnp.arange(n_blocks) * MOE_BLOCK, side='right'),
                        N_EXPERTS - 1)

    def run_block(args):
        tok, w, e = args
        y = swiglu_expert(hf[tok], wg[e], bg[e], wu[e], bu[e], wd[e], bd[e])
        return y.astype(jnp.float32) * w[:, None]

    ys = lax.map(run_block, (slot_tok.reshape(n_blocks, MOE_BLOCK),
                             slot_w.reshape(n_blocks, MOE_BLOCK), blk_e))
    out = jnp.zeros((T, D), jnp.float32).at[slot_tok].add(ys.reshape(n_slots, D))
    return out.astype(h.dtype).reshape(B, N, D)

def setup_inputs(seed: int = 0) -> dict:
    key = jax.random.key(seed)
    k = jax.random.split(key, 30)
    D = D_MODEL

    def nrm(kk, shape, scale):
        return jax.random.normal(kk, shape, jnp.float32) * scale

    return {
        'x_prompt': nrm(k[0], (BATCH, SEQ, D), 1.0),
        'x_sample': nrm(k[1], (DEC_BATCH, DEC_SEQ, D), 1.0),
        'cache_k': nrm(k[2], (DEC_BATCH, DEPTH, PAST_LEN, NA_HEADS, NA_HEAD_DIM), 1.0),
        'cache_v': nrm(k[3], (DEC_BATCH, DEPTH, PAST_LEN, NA_HEADS, NA_HEAD_DIM), 1.0),
        'state_hgrn_fwd': nrm(k[4], (DEC_BATCH, DEPTH, HG_HEADS, HG_DK, HG_DV), 0.5),
        'state_hgrn_bwd': nrm(k[5], (DEC_BATCH, DEPTH, HG_HEADS, HG_DK, HG_DV), 0.5),
        'c': nrm(k[6], (DEC_BATCH, D), 1.0),
        'c_ctx': nrm(k[7], (D,), 1.0),
        'w_mod': nrm(k[8], (DEPTH, D, 6 * D), D ** -0.5),
        'b_mod': nrm(k[9], (DEPTH, 6 * D), 0.02),
        'norm1_g': 1.0 + nrm(k[10], (DEPTH, D), 0.02),
        'norm2_g': 1.0 + nrm(k[11], (DEPTH, D), 0.02),
        'w_in': nrm(k[12], (DEPTH, D, IN_COLS), D ** -0.5),
        'na_rel_bias': nrm(k[13], (DEPTH, NA_HEADS, 2 * NA_KH - 1, 2 * NA_KW - 1), 0.1),
        'hgrn_lb': nrm(k[14], (2, DEPTH, HG_WIDTH), 0.5),
        'hgrn_onorm_g': 1.0 + nrm(k[15], (DEPTH, HG_DV), 0.02),
        'gmlp_vnorm_g': 1.0 + nrm(k[16], (DEPTH, GM_WIDTH), 0.02),
        'gmlp_ws': nrm(k[17], (DEPTH, GM_GROUPS, GM_CHUNK, GM_CHUNK), GM_CHUNK ** -0.5),
        'gmlp_b': 1.0 + nrm(k[18], (DEPTH, GM_GROUPS, GM_CHUNK), 0.1),
        'w_out': nrm(k[19], (DEPTH, MIX_WIDTH, D), MIX_WIDTH ** -0.5),
        'router_w': nrm(k[20], (DEPTH, D, N_EXPERTS), D ** -0.5),
        'router_b': nrm(k[21], (DEPTH, N_EXPERTS), 0.01),
        'w_gate': nrm(k[22], (DEPTH, N_EXPERTS, D, D_EXPERT), D ** -0.5),
        'b_gate': nrm(k[23], (DEPTH, N_EXPERTS, D_EXPERT), 0.01),
        'w_up': nrm(k[24], (DEPTH, N_EXPERTS, D, D_EXPERT), D ** -0.5),
        'b_up': nrm(k[25], (DEPTH, N_EXPERTS, D_EXPERT), 0.01),
        'w_down': nrm(k[26], (DEPTH, N_EXPERTS, D_EXPERT, D), D_EXPERT ** -0.5),
        'b_down': nrm(k[27], (DEPTH, N_EXPERTS, D), 0.01),
        'final_g': 1.0 + nrm(k[28], (D,), 0.02),
    }

def reference(x_prompt, x_sample, cache_k, cache_v, state_hgrn_fwd, state_hgrn_bwd, c, c_ctx,
              w_mod, b_mod, norm1_g, norm2_g, w_in, na_rel_bias, hgrn_lb, hgrn_onorm_g,
              gmlp_vnorm_g, gmlp_ws, gmlp_b, w_out, router_w, router_b, w_gate, b_gate,
              w_up, b_up, w_down, b_down, final_g):
    cond_ctx = jax.nn.silu(c_ctx)[None, :]
    cond_lat = jax.nn.silu(c)
    lb_soft = jax.nn.softmax(hgrn_lb.astype(jnp.float32), axis=1)
    lower = jnp.cumsum(lb_soft, axis=1) - lb_soft[:, :1]
    xp, xs = x_prompt, x_sample
    k_list, v_list, sf_list, sb_list = [], [], [], []
    for l in range(DEPTH):
        mixer_w = (w_in[l], w_out[l], na_rel_bias[l], lower[:, l], hgrn_onorm_g[l],
                   gmlp_vnorm_g[l], gmlp_ws[l], gmlp_b[l])
        moe_w = (router_w[l], router_b[l], w_gate[l], b_gate[l], w_up[l], b_up[l],
                 w_down[l], b_down[l])
        sh1, sc1, g1, sh2, sc2, g2 = ada_modulation(cond_ctx, w_mod[l], b_mod[l])
        out, (kc, vc, sf, sb) = token_mixer(modulate(rmsnorm(xp, norm1_g[l]), sh1, sc1), *mixer_w, None)
        xp = xp + g1 * out
        xp = xp + g2 * routed_moe(modulate(rmsnorm(xp, norm2_g[l]), sh2, sc2), *moe_w)
        k_list.append(kc)
        v_list.append(vc)
        sf_list.append(sf.astype(xp.dtype))
        sb_list.append(sb.astype(xp.dtype))
        sh1, sc1, g1, sh2, sc2, g2 = ada_modulation(cond_lat, w_mod[l], b_mod[l])
        ctx = (cache_k[:, l], cache_v[:, l], state_hgrn_fwd[:, l], state_hgrn_bwd[:, l])
        out, _ = token_mixer(modulate(rmsnorm(xs, norm1_g[l]), sh1, sc1), *mixer_w, ctx)
        xs = xs + g1 * out
        xs = xs + g2 * routed_moe(modulate(rmsnorm(xs, norm2_g[l]), sh2, sc2), *moe_w)
    y_prompt = rmsnorm(xp, final_g)
    y_sample = rmsnorm(xs, final_g)
    new_cache_k = jnp.stack(k_list, axis=1)
    new_cache_v = jnp.stack(v_list, axis=1)
    new_state_hgrn_fwd = jnp.stack(sf_list, axis=1)
    new_state_hgrn_bwd = jnp.stack(sb_list, axis=1)
    return (y_prompt, y_sample, new_cache_k, new_cache_v, new_state_hgrn_fwd, new_state_hgrn_bwd)


_drawn_inputs = setup_inputs


def setup_inputs(seed=0):
    import zlib

    import numpy as np

    out = dict(_drawn_inputs(seed))
    spreads = {}
    factors = {'state_hgrn_fwd': 7.639,
     'state_hgrn_bwd': 3.867,
     'na_rel_bias': 10.409,
     'hgrn_onorm_g': 12.273,
     'gmlp_vnorm_g': 2.715,
     'router_b': 4.534,
     'b_gate': 28.208,
     'b_up': 36.88,
     'b_down': 31.416,
     'final_g': 7.338,
     'norm2_g': 2.803}
    for name, (base, spread) in spreads.items():
        noise = np.random.default_rng([zlib.crc32(name.encode()), seed]).standard_normal(out[name].shape)
        drawn = base * np.exp(spread * noise) if base else spread * noise
        out[name] = __import__('jax').numpy.asarray(drawn.astype(out[name].dtype))
    for name, factor in factors.items():
        out[name] = (out[name] * factor).astype(out[name].dtype)
    return out
```

```python
from contextlib import ExitStack

import numpy as np

import concourse.bass as bass
from concourse import mybir

F32 = mybir.dt.float32
I32 = mybir.dt.int32
U8 = mybir.dt.uint8
ALU = mybir.AluOpType
ACT = mybir.ActivationFunctionType
AX = mybir.AxisListType

P = 128
D = 1024
KT = D // P
G = 2
HALF = 64
HD = 64
NH = 8
HP = NH // 2
RH = 4
RP = RH // 2
GM = 4
GRID_W = 64
NA_KH, NA_KW = 8, 16
NE = 32
TOP_K = 4
CAP = 64
CHUNKS = G * P // CAP
MAX_OVER = (G * P * TOP_K - NE) // CAP
LIMIT, ALPHA = 7.0, 1.702
EPS = 1e-6
F_FLOOR = 1e-30
LN_SPLIT = 60
NEG = -1e30
SCALE = HD ** -0.5

RING = 12
SLOT = 2048
MODS = [1, 0, 2, 4, 3, 5]
WIN = [7, 8, 6, 9, 2, 0, 3, 1, 4, 5, 12, 11, 10]
Z_F, Z_B, H_Q, H_I, K_0, Q_0, K_1, Q_1, V_0, V_1, G_V, G_U, H_G = range(13)
AT_MODS1, AT_WIN = 0, 8
AT_MODS2 = AT_WIN + len(WIN)
AT_WOUT = AT_MODS2 + 16
AT_MOE = AT_WOUT + 4
LEVELS = [64, 32, 16, 8, 4, 2, 1]

C_IDENT, C_TRI, C_STRI, C_MODSEL, C_SLOTROW = 0, P, 2 * P, 3 * P, 4 * P
C_SLOTCOL = C_SLOTROW + CAP
C_THR, C_E, C_OFF = C_SLOTCOL + 1, C_SLOTCOL + 2, C_SLOTCOL + 3
C_IOTA = C_SLOTCOL + 4
C_END = C_IOTA + 16
M_DIAG, M_WINDOW = 14, 15


def shape_constants():
    f = np.zeros((P, C_END), np.float32)
    i = np.arange(P)
    f[:, C_IDENT:C_IDENT + P] = np.eye(P)
    f[:, C_TRI:C_TRI + P] = i[:, None] <= i[None, :]
    f[:, C_STRI:C_STRI + P] = i[:, None] < i[None, :]
    for j in range(4):
        for r in range(G):
            f[32 * j + r, C_MODSEL + HALF * r:C_MODSEL + HALF * (r + 1)] = 1
    f[:, C_SLOTROW:C_SLOTROW + CAP] = np.arange(1, CAP + 1)
    f[:, C_SLOTCOL] = i % CAP + 1
    f[:, C_THR] = np.where(i < NE, 1e9, CAP * (i // NE))
    f[:, C_E] = i % NE
    f[:, C_OFF] = CAP * (i // NE)
    f[:, C_IOTA:C_IOTA + 16] = np.arange(16)
    m = np.zeros((P, 16, P), np.float32)
    s, t = i[:, None], i[None, :]
    for n, w in enumerate(LEVELS):
        same = s // (2 * w) == t // (2 * w)
        first, second = s % (2 * w) < w, t % (2 * w) >= w
        m[:, n] = same & first & second
        m[:, 7 + n] = m[:, n].T
    m[:, M_DIAG] = s == t
    qc, kc = s % GRID_W, t % GRID_W
    start = np.clip(qc - NA_KW // 2, 0, GRID_W - NA_KW)
    m[:, M_WINDOW] = (kc >= start) & (kc < start + NA_KW)
    return f, m.reshape(P, 16 * P)


def hybrid_layer(nc, x_prompt, x_sample, cache_k, cache_v, state_hgrn_fwd, state_hgrn_bwd, c, c_ctx,
                 w_mod, b_mod, norm1_g, norm2_g, w_in, na_rel_bias, hgrn_lb, hgrn_onorm_g,
                 gmlp_vnorm_g, gmlp_ws, gmlp_b, w_out, router_w, router_b, w_gate, b_gate,
                 w_up, b_up, w_down, b_down, final_g, const_f32, const_masks,
                 y_prompt, y_sample, new_k, new_v, new_sf, new_sb):
    assert CHUNKS * NE == P and MAX_OVER <= 16
    ctx = ExitStack()
    with ctx:
        def sb(name, cols, dt=F32, parts=P):
            return ctx.enter_context(nc.sbuf_tensor(name, [parts, cols], dt))[:, :]

        events = {}

        def ev(name):
            if name not in events:
                events[name] = ctx.enter_context(nc.semaphore(name))
            return events[name]

        ring = sb("ring", RING * SLOT).rearrange("p (s w) -> p s w", s=RING)
        cst = sb("cst", C_END)
        masks = sb("masks", 16 * P, U8).rearrange("p (m t) -> p m t", m=16)
        xres = sb("xres", 2 * D).rearrange("p (t d) -> p t d", t=2)
        gain = sb("gain", D)
        gsc = sb("gsc", D)
        shf = sb("shf", D)
        rows = sb("rows", 2 * D).rearrange("p (t d) -> p t d", t=2)
        colsT = sb("colsT", 2 * D)
        kv_pool = sb("kv_pool", 3 * 1024)
        hq_hi = sb("hq_hi", 2 * 512)
        keyT = sb("keyT", 1024).rearrange("p (d n) -> p d n", d=2)
        cumT = sb("cumT", 1024).rearrange("p (d n) -> p d n", d=2)
        tmp = sb("tmp", 1024)
        q_pool = sb("q_pool", 2048)
        k_pool = sb("k_pool", 2048)
        d_pool = sb("d_pool", 1024)
        at_pool = sb("at_pool", 1024)
        biasN = sb("biasN", 1024).rearrange("p (h k) -> p h k", h=NH)
        cv = sb("cv", 512)
        ckT = sb("ckT", 512).rearrange("p (h l) -> p h l", h=HP)
        wsT = sb("wsT", 512).rearrange("p (g t) -> p g t", g=GM)
        condT = sb("condT", KT * 32).rearrange("p (k m) -> p k m", k=KT)
        bmod = sb("bmod", 512, parts=12)
        s0 = sb("s0", 2 * RP * HD).rearrange("p (d h v) -> p d h v", d=2, h=RP)
        rw = sb("rw", KT * NE).rearrange("p (k e) -> p k e", k=KT)
        vng = sb("vng", GM * HD)
        ong = sb("ong", HD)
        cond = sb("cond", P, parts=16)
        gb_rows = sb("gb_rows", P, parts=GM)
        small = sb("small", 120)
        ones = sb("ones", 8)
        small_i = sb("small_i", 18, I32, parts=1)
        ones_rows = ones[0:1, 0:1].to_broadcast([1, P])

        ident = cst[:, C_IDENT:C_IDENT + P]
        ck = d_pool[:, 0:512]
        ws = d_pool[:, 512:1024].rearrange("p (g s) -> p g s", g=GM)
        hT = colsT.rearrange("p (k g t) -> p k g t", k=KT, g=G)
        catT = colsT.rearrange("p (k t gt) -> p k t gt", k=KT, t=2)
        h2T = catT
        qT, kT = (kv_pool[:, 1024 * n:1024 * (n + 1)].rearrange("p (h g t) -> p h g t", h=HP, g=G)
                  for n in range(2))
        v = kv_pool[:, 2048:3072].rearrange("p (g n) -> p g n", g=G)
        hqT = hq_hi[:, 0:512]
        hi = hq_hi[:, 512:1024].rearrange("p (g n) -> p g n", g=G)
        sig = tmp.rearrange("p (d n) -> p d n", d=2)
        kout = tmp[:, 0:512]
        gtmp = tmp[:, 512:1024]
        part = [at_pool[:, 0:512], at_pool[:, 512:1024]]
        AT = at_pool.rearrange("p (q n) -> p q n", q=2)
        Qt = q_pool.rearrange("p (b d n) -> p b d n", b=2, d=2)
        Kt = k_pool.rearrange("p (b d n) -> p b d n", b=2, d=2)
        g1, g2 = q_pool[:, 0:D], q_pool[:, D:2 * D]
        Dl = d_pool.rearrange("p (d n) -> p d n", d=2)
        kstT = d_pool[:, 0:512].rearrange("p (d h k) -> p d h k", d=2, h=RP)
        state_out = d_pool[:, 512:1024]
        probs = k_pool[:, :].rearrange("p (h k) -> p h k", h=NH)
        probs_p = k_pool[:, 0:1024].rearrange("p (h k) -> p h k", h=NH)
        bias_raw = cumT.rearrange("p d n -> p (d n)").rearrange("p (h k) -> p h k", h=NH)
        flip = keyT[:, 1, 0:P]
        sT_lo = biasN.rearrange("p h k -> p (h k)")
        sT_hi = d_pool
        ss = small[:, 0:2]
        rstd = small[:, 2:4]
        lbT = small[:, 4:8]
        omlT = small[:, 8:12]
        lb_t = small[:, 12:20]
        gbT = small[:, 20:24]
        ssg = small[:, 24:26]
        rsg = small[:, 26:28]
        sso = small[:, 28:36]
        rso = small[:, 36:44]
        mx = small[:, 44:52]
        nmx = small[:, 52:60]
        rsum = small[:, 60:68]
        rinv = small[:, 68:76]
        mx_s = small[:, 76:84]
        nmx_s = small[:, 84:92]
        rsum_s = small[:, 92:100]
        rinv_s = small[:, 100:108]
        eps = small[:, 108:109]
        negc = small[:, 109:110]
        ssf = small[:, 110:112]
        rsf = small[:, 112:114]
        ss2 = small[:, 114:116]
        rs2 = small[:, 116:118]
        zcol = small[:, 118:119]

        moe_pool = kv_pool
        mbias = moe_pool[0:NE, :].rearrange("p (m n) -> p m n", m=3)
        actb = k_pool[:, 0:512]
        upb = k_pool[:, 512:1024]
        sigb = k_pool[:, 1024:1536]
        aT = k_pool[:, 1536:2048].rearrange("p (c s) -> p c s", c=4)
        ab = d_pool[:, 0:512]
        ysb = d_pool[:, 512:1024]
        xe = at_pool[:, 0:512].rearrange("p (k s) -> p k s", k=KT)
        gT = at_pool[:, 512:1024].rearrange("p (b t) -> p b t", b=2)
        pick = cumT[0:NE, 0, 0:256].rearrange("p (b m) -> p b m", b=2)
        Ptok = keyT[:, 0, 0:2 * CAP].rearrange("p (t s) -> p t s", t=2)
        rank = keyT[:, 0, 128:128 + 2 * (NE + 1)].rearrange("p (t e) -> p t e", t=2)
        gate = keyT[:, 0, 200:264].rearrange("p (t e) -> p t e", t=2)
        lg = keyT[:, 0, 264:328].rearrange("p (t e) -> p t e", t=2)
        msk = keyT[:, 0, 328:392].rearrange("p (t e) -> p t e", t=2)
        eqm = keyT[:, 0, 392:456].rearrange("p (t e) -> p t e", t=2)
        csm = keyT[:, 1, 0:64].rearrange("p (t e) -> p t e", t=2)
        ex = keyT[:, 1, 64:128].rearrange("p (t e) -> p t e", t=2)
        rsm = keyT[:, 1, 128:160]
        flag = keyT[:, 1, 160:161]
        posn = keyT[:, 1, 161:162]
        onehot = keyT[:, 1, 162:178]
        offb = keyT[:, 1, 178:194]
        mask4 = keyT[:, 1, 194:450].rearrange("p (t r e) -> p t r e", t=2, r=CHUNKS)
        rgT = cumT[0:NE, 1, :]
        zrow = tmp[:, 0:512]
        rbias = bmod[0:1, 0:NE]
        identE = wsT[0:NE, 0, 0:NE + 1]

        B = [ctx.enter_context(nc.psum_tensor(f"bank{n}", [P, 512], F32))[:, :] for n in range(8)]

        def mod_bank(n):
            return n % 2 if n < 4 else 0

        def bc_bank(n):
            return 2 + n % 2 if n < 4 else 1

        slot_loaded = [ctx.enter_context(nc.semaphore(f"slot{n}_loaded")) for n in range(RING)]
        chunks_used = ctx.enter_context(nc.semaphore("chunks_used"))

        def halves(ap):
            return ap.rearrange("(o p) d -> o p d", p=HALF)

        def expert_slot(cidx):
            return (AT_MOE + cidx) % RING

        def chunk_loads(cidx, e):
            return ((AT_MOE + cidx) // RING + 1 + e) * 16

        def used(cidx, e):
            return e * RING + (AT_MOE + cidx + 1)

        class Chain:

            def __init__(self, eng, name):
                self.eng, self.sem, self.n, self.at = eng, ev(name), 0, None

            def step(self, ins):
                ins.then_inc(self.sem, 1)
                self.n += 1
                self.eng.wait_ge(self.sem, self.n if self.at is None else self.at + self.n)

            def enter(self, reg, per):
                self.at, self.per, self.start = reg * per, per, self.n

            def leave(self, times):
                assert self.n - self.start == self.per, (self.n - self.start, self.per)
                self.at, self.n = None, self.start + self.per * times

        block = ctx.enter_context(nc.Block())

        @block.sync
        def _(sp):
            def slot_free(n):
                if n >= RING:
                    sp.wait_ge(chunks_used, n - RING + 1)

            def load(n, view, src):
                slot_free(n)
                sp.dma_start(view, src).then_inc(slot_loaded[n % RING], 16)

            n = 0
            sp.dma_start(cond[0:8, :], c_ctx.rearrange("(k p) -> k p", p=P)).then_inc(ev("cond_loaded"), 16)
            sp.dma_start(cond[8:16, :], c.rearrange("b (k p) -> (b k) p", p=P)).then_inc(ev("cond_loaded"), 16)

            def load_mod(m):
                nonlocal n
                for half in range(2):
                    for r in range(2):
                        src = w_mod[0, 512 * r:512 * (r + 1), m * D + 512 * half:m * D + 512 * (half + 1)]
                        load(n, ring[:, n % RING, :].rearrange("p (k n) -> p k n", k=4),
                             src.rearrange("(k p) n -> p k n", p=P))
                        n += 1

            for m in MODS[:2]:
                load_mod(m)
            for b in WIN:
                load(n, ring[:, n % RING, :].rearrange("p (k n) -> p k n", k=KT),
                     w_in[0, :, 256 * b:256 * (b + 1)].rearrange("(k p) n -> p k n", p=P))
                n += 1
            for m in MODS[2:]:
                load_mod(m)
            for r in range(4):
                load(n, ring[:, n % RING, :].rearrange("p (k n) -> p k n", k=2),
                     w_out[0, 256 * r:256 * (r + 1), :].rearrange("(k p) n -> p k n", p=P))
                n += 1
            assert n == AT_MOE

            def load_expert(e, count):
                for cidx in range(RING):
                    w = (w_gate, w_up, w_down)[cidx // 4]
                    sp.wait_ge(chunks_used, used(cidx - RING, count))
                    sp.dma_start(ring[:, expert_slot(cidx), :].rearrange("p (k n) -> p k n", k=2),
                                 w[0, bass.ds(e, 1), 256 * (cidx % 4):256 * (cidx % 4 + 1), :]
                                 .rearrange("a (k p) n -> p (a k) n", p=P)).then_inc(slot_loaded[expert_slot(cidx)], 16)

            with sp.Fori(0, NE) as e:
                load_expert(e, e)
            sp.wait_ge(ev("over_list"), 1)
            n_over = sp.value_load(small_i[0:1, 16:17], min_val=0, max_val=MAX_OVER)
            with sp.Fori(0, MAX_OVER) as j:
                with sp.If(n_over > j):
                    e = sp.value_load(small_i[0:1, bass.ds(j, 1)], min_val=0, max_val=NE - 1)
                    load_expert(e, j + NE)

            for t in range(2):
                sp.wait_ge(ev("y_ready"), t + 1)
                sp.dma_start(halves(y_prompt[0])[t], xres[0:HALF, t, :]).then_inc(ev("y_stored"), 16)
                sp.dma_start(halves(y_sample[0])[t], xres[HALF:P, t, :]).then_inc(ev("y_stored"), 16)
            sp.wait_ge(ev("y_stored"), 64)

        @block.gpsimd
        def _(pool):
            nc.gpsimd.memset(condT, 0.0).then_inc(ev("condT_zero"), 1)
            nc.gpsimd.memset(ones, 1.0).then_inc(ev("ones_set"), 1)
            nc.gpsimd.memset(eps, EPS).then_inc(ev("cols_set"), 1)
            nc.gpsimd.memset(zcol, 0.0).then_inc(ev("cols_set"), 1)
            nc.gpsimd.memset(q_pool, 0.0).then_inc(ev("qk_zero"), 1)
            pool.wait_ge(ev("masks_ready"), 1)
            nc.gpsimd.memset(k_pool, 0.0).then_inc(ev("qk_zero"), 1)

            pool.wait_ge(ev("mod_out"), 2)
            pool.dma_start(gain, norm2_g[0:1, :].partition_broadcast(P).rearrange("p a d -> p (a d)")).then_inc(ev("gain2_loaded"), 16)

            pool.wait_ge(ev("kout_ready"), 1)
            pool.dma_start(new_k.rearrange("b l s h d -> (b l s) (h d)"), kout).then_inc(ev("caches_stored"), 16)
            pool.wait_ge(ev("win_out"), V_1 + 1)
            pool.dma_start(new_v.rearrange("b l s h d -> (b l s) (h d)"), v[:, 0, :]).then_inc(ev("caches_stored"), 16)
            pool.wait_ge(ev("state_ready"), 1)
            for d, out in enumerate((new_sf, new_sb)):
                pool.dma_start(out.rearrange("b l h k v -> k (b l h) v"),
                               state_out[0:HD, 256 * d:256 * (d + 1)].rearrange("k (h v) -> k h v", h=RH)).then_inc(ev("caches_stored"), 16)
            pool.wait_ge(ev("caches_stored"), 64)
            pool.wait_ge(ev("cat_ps"), 4)
            for m, src in enumerate((b_gate, b_up, b_down)):
                pool.dma_start(mbias[:, m, :], src[0]).then_inc(ev("mbias_loaded"), 16)
            pool.wait_ge(ev("mod_out"), 8)
            pool.dma_start(gain, final_g.rearrange("(a d) -> a d", a=1).partition_broadcast(P).rearrange("p a d -> p (a d)")).then_inc(ev("gain3_loaded"), 16)
            pool.wait_ge(ev("mod_out"), 12)
            pool.dma_start(rbias, router_b).then_inc(ev("rbias_loaded"), 16)
            pool.wait_ge(ev("z_ps"), 1)
            nc.gpsimd.memset(identE, 0.0).then_inc(ev("idE_zero"), 1)
            pool.wait_ge(ev("idE_zero"), 1)
            nc.gpsimd.affine_select(out=identE, in_=identE, compare_op=ALU.not_equal, fill=1.0, base=0,
                                    pattern=[[-1, NE + 1]], channel_multiplier=1).then_inc(ev("idE_ready"), 1)
            pool.wait_ge(ev("mbias_loaded"), 48)
            pool.wait_ge(ev("gain3_loaded"), 16)
            pool.wait_ge(ev("rbias_loaded"), 16)

        @block.scalar
        def _(act):
            def small_load(name, dst, src, **kw):
                act.dma_start(dst, src, **kw).then_inc(ev(name), 16)

            small_load("consts_loaded", cst, const_f32)
            small_load("consts_loaded", bmod, b_mod.rearrange("a (c n) -> (a c) n", n=512))
            small_load("consts_loaded", gain, norm1_g[0:1, :].partition_broadcast(P).rearrange("p a d -> p (a d)"))
            for t in range(2):
                small_load("x_loaded", xres[0:HALF, t, :], halves(x_prompt[0])[t])
                small_load("x_loaded", xres[HALF:P, t, :], halves(x_sample[0])[t])
            act.wait_ge(ev("cond_loaded"), 32)
            act.wait_ge(ev("cond_loaded"), 32)
            nc.scalar.activation(gtmp[0:16, 0:P], cond, ACT.Sigmoid).then_inc(ev("cond_sig"), 1)
            small_load("early_loaded", ck, cache_k.rearrange("b l s h d -> (b l s) (h d)"))
            small_load("early_loaded", ws, gmlp_ws[0].rearrange("g t s -> t g s"))
            small_load("early_loaded", gb_rows, gmlp_b[0])
            small_load("lb_loaded", lb_t[:, 0:4], hgrn_lb.rearrange("d l (h p) -> p (d l h)", p=P),
                       allow_slow_non_contiguous=True)
            small_load("masks_loaded", k_pool, const_masks)
            for qr in range(2):
                for kr in range(2):
                    off = (NA_KH - 1 + kr - qr) * (2 * NA_KW - 1) + NA_KW - GRID_W
                    src = bass.AP(tensor=na_rel_bias.tensor, offset=na_rel_bias.offset + off,
                                  ap=[[1, GRID_W], [(2 * NA_KH - 1) * (2 * NA_KW - 1), NH], [1, GRID_W]])
                    small_load("bias_raw_loaded", bias_raw[64 * (1 - qr):64 * (2 - qr), :, 64 * kr:64 * (kr + 1)], src)
            small_load("mixer_loaded", cv, cache_v.rearrange("b l s h d -> (b l s) (h d)"))
            for d, src in enumerate((state_hgrn_fwd, state_hgrn_bwd)):
                small_load("mixer_loaded", s0[:, d], src[0, 0].rearrange("(h q) k v -> (q k) h v", q=2))
            small_load("mixer_loaded", vng, gmlp_vnorm_g[0:1, :].partition_broadcast(P).rearrange("p a d -> p (a d)"))
            small_load("mixer_loaded", ong, hgrn_onorm_g[0:1, :].partition_broadcast(P).rearrange("p a d -> p (a d)"))
            small_load("mixer_loaded", rw, router_w[0].rearrange("(k p) e -> p k e", p=P))

            act.wait_ge(ev("x_loaded"), 64)
            for t in range(2):
                nc.scalar.activation(rows[:, t, :], xres[:, t, :], ACT.Square, accum_out=ss[:, t:t + 1]).then_inc(ev("ss1"), 1)
            act.wait_ge(ev("ss1"), 2)
            act.wait_ge(ev("cols_set"), 2)
            nc.scalar.activation(rstd, ss, ACT.Sqrt, bias=eps, scale=1.0 / D).then_inc(ev("rms1"), 1)

            act.wait_ge(ev("lb_shift"), 1)
            nc.scalar.activation(lb_t[:, 0:4], lb_t[:, 4:8], ACT.Exp).then_inc(ev("lb_exp"), 1)

            for t in range(2):
                for q in range(2):
                    act.wait_ge(ev("hT_ps"), 2 * t + q + 1)
                    nc.scalar.copy(hT[:, 4 * q:4 * q + 4, :, HALF * t:HALF * (t + 1)],
                                   B[4 + 2 * t + q].rearrange("p (k g u) -> p k g u", k=4, g=G)).then_inc(ev("hT_ready"), 1)

            def win_wait(i):
                act.wait_ge(chunks_used, AT_WIN + i + 1)

            for d, i in enumerate((Z_F, Z_B)):
                win_wait(i)
                if d == 0:
                    act.wait_ge(ev("cond_silu"), 1)
                nc.scalar.activation(sig[:, d, :], B[i % 2], ACT.Sigmoid).then_inc(ev("sig_z"), 1)
                nc.scalar.activation(keyT[:, d, :], B[i % 2], ACT.Sigmoid, scale=-1.0).then_inc(ev("win_out"), 1)
            win_wait(H_Q)
            nc.scalar.copy(hqT, B[H_Q % 2]).then_inc(ev("win_out"), 1)
            win_wait(H_I)
            nc.scalar.copy(hi.rearrange("p g n -> p (g n)"), B[H_I % 2]).then_inc(ev("win_out"), 1)
            act.wait_ge(ev("f_parts"), 1)
            nc.scalar.activation(cumT, cumT, ACT.Ln).then_inc(ev("ln_parts"), 1)
            nc.scalar.activation(sig, sig, ACT.Ln, scale=2.0 ** LN_SPLIT).then_inc(ev("ln_parts"), 1)

            def copy_win(i):
                win_wait(i)
                if i in (K_0, Q_0, K_1, Q_1):
                    dst = (kT if i in (K_0, K_1) else qT)[:, 2 * (i >= K_1):2 * (i >= K_1) + 2]
                    nc.scalar.copy(dst, B[i % 2].rearrange("p (h g t) -> p h g t", h=2, g=G)).then_inc(ev("win_out"), 1)
                else:
                    dst = v[:, :, 256 * (i - V_0):256 * (i - V_0 + 1)] if i in (V_0, V_1) else rows[:, :, 768:1024]
                    nc.scalar.copy(dst, B[i % 2].rearrange("p (g n) -> p g n", g=G)).then_inc(ev("win_out"), 1)

            def level_exp(n):
                w = LEVELS[n]
                act.wait_ge(ev("lvl_diff"), n + 1)
                for d in range(2):
                    x = Dl[:, d, :].rearrange("p (n h m) -> p n h m", h=2, m=w)
                    for h in range(2):
                        query = h == 1 - d
                        nc.scalar.activation(x[:, :, h, :], x[:, :, h, :], ACT.Exp,
                                             scale=1.0 if query else -1.0).then_inc(ev("lvl_exp"), 1)

            copy_win(K_0)
            copy_win(Q_0)
            level_exp(0)
            copy_win(K_1)
            level_exp(1)
            copy_win(Q_1)
            act.wait_ge(ev("kout_ps"), 1)
            act.wait_ge(ev("logf_used"), 2)
            nc.scalar.copy(kout, B[6]).then_inc(ev("kout_ready"), 1)
            level_exp(2)
            copy_win(V_0)
            level_exp(3)
            copy_win(V_1)
            level_exp(4)
            copy_win(G_V)
            level_exp(5)
            act.wait_ge(ev("win_out"), G_V + 1)
            for g in range(G):
                nc.scalar.activation(gtmp[:, 256 * g:256 * (g + 1)], rows[:, g, 768:1024], ACT.Square,
                                     accum_out=ssg[:, g:g + 1]).then_inc(ev("ssg"), 1)
            act.wait_ge(ev("ssg"), 2)
            level_exp(6)
            nc.scalar.activation(rsg, ssg, ACT.Sqrt, bias=eps, scale=1.0 / (GM * HD)).then_inc(ev("rmsg"), 1)
            act.wait_ge(ev("end_diff"), 1)
            nc.scalar.activation(Qt[:, 0, :, :], cumT, ACT.Exp).then_inc(ev("end_exp"), 1)
            nc.scalar.activation(Dl, Dl, ACT.Exp, scale=-1.0).then_inc(ev("end_exp"), 1)
            win_wait(H_G)
            act.wait_ge(ev("vg_ready"), 1)
            nc.scalar.activation(gtmp, B[H_G % 2], ACT.Sigmoid).then_inc(ev("sig_g"), 1)

            act.wait_ge(ev("kst_ps"), 1)
            nc.scalar.copy(kstT.rearrange("p d h k -> p (d h k)"), B[6]).then_inc(ev("kst_ready"), 1)
            act.wait_ge(ev("state_ps"), 1)
            nc.scalar.copy(state_out[0:HD, :], B[4][0:HD, :]).then_inc(ev("state_ready"), 1)

            act.wait_ge(ev("ms_o"), 1)
            nc.scalar.activation(rso, sso, ACT.Sqrt).then_inc(ev("rms_o"), 1)

            act.wait_ge(ev("nmx_p"), 1)
            act.wait_ge(ev("state_ps"), 1)
            for q in range(2):
                for h in range(HP):
                    n = HP * q + h
                    nc.scalar.activation(probs_p[:, n, :], B[2 + q][:, P * h:P * (h + 1)], ACT.Exp, scale=SCALE,
                                         bias=nmx[:, n:n + 1], accum_out=rsum[:, n:n + 1]).then_inc(ev("exp_p"), 1)
            act.wait_ge(ev("pT_ps"), 2)
            for q in range(2):
                nc.scalar.copy(k_pool[:, D + 512 * q:D + 512 * (q + 1)], B[4 + q]).then_inc(ev("pT_ready"), 1)
            act.wait_ge(ev("att_p_ps"), 1)
            act.wait_ge(ev("sc_ps"), 1)
            for q in range(2):
                nc.scalar.mul(probs[:, q:NH:2, P:2 * P], B[4 + q].rearrange("p (h k) -> p h k", h=HP), SCALE).then_inc(ev("ctx_sc"), 1)
            act.wait_ge(ev("nmx_s"), 1)
            for h in range(NH):
                nc.scalar.activation(probs[:, h, :], probs[:, h, :], ACT.Exp, bias=nmx_s[:, h:h + 1],
                                     accum_out=rsum_s[:, h:h + 1]).then_inc(ev("exp_s"), 1)
            act.wait_ge(ev("caches_stored"), 64)
            for q in range(4):
                act.wait_ge(ev("sT_ps"), q + 1)
                dst = (sT_lo if q < 2 else sT_hi)[:, 512 * (q % 2):512 * (q % 2 + 1)]
                nc.scalar.copy(dst, B[2 + q]).then_inc(ev("sT_ready"), 1)

            for q in range(4):
                g, kh = q // 2, q % 2
                act.wait_ge(ev("cat_ps"), q + 1)
                nc.scalar.copy(catT[:, 4 * kh:4 * kh + 4, :, HALF * g:HALF * (g + 1)],
                               B[2 + q].rearrange("p (k t u) -> p k t u", k=4, t=2)).then_inc(ev("catT_ready"), 1)

            for t in range(2):
                act.wait_ge(ev("x1_ready"), 2 * t + 2)
                nc.scalar.activation(k_pool[:, D * t:D * (t + 1)], xres[:, t, :], ACT.Square, accum_out=ss2[:, t:t + 1]).then_inc(ev("ss2"), 1)
            act.wait_ge(ev("ss2"), 2)
            nc.scalar.activation(rs2, ss2, ACT.Sqrt, bias=eps, scale=1.0 / D).then_inc(ev("rms2"), 1)
            for t in range(2):
                for q in range(2):
                    act.wait_ge(ev("h2T_ps"), 2 * t + q + 1)
                    nc.scalar.copy(h2T[:, 4 * q:4 * q + 4, t, :],
                                   B[2 + (2 * t + q) % 2].rearrange("p (k u) -> p k u", k=4)).then_inc(ev("h2T_ready"), 1)
            act.wait_ge(ev("nv1"), 1)
            for t in range(2):
                nc.scalar.activation(ex[:, t, :], lg[:, t, :], ACT.Exp, bias=rsm[:, 16 + t:17 + t]).then_inc(ev("r_exp"), 1)
            act.wait_ge(ev("rgT_ps"), 1)
            nc.scalar.copy(rgT, B[1][0:NE, :]).then_inc(ev("rgT_ready"), 1)

            def tokens_out(count):
                act.wait_ge(ev("xe_ps"), count + 1)
                nc.scalar.copy(xe.rearrange("p k s -> p (k s)"), B[3]).then_inc(ev("xe_ready"), 1)

            def sigmoid_step(count):
                act.wait_ge(ev("gate_min"), count + 1)
                nc.scalar.activation(sigb, actb, ACT.Sigmoid, scale=ALPHA).then_inc(ev("gate_sig"), 1)

            def down_steps(count):
                act.wait_ge(ev("aT_ps"), count + 1)
                nc.scalar.copy(aT.rearrange("p c s -> p (c s)"), B[2]).then_inc(ev("aT_ready"), 1)
                act.wait_ge(chunks_used, used(11, count))
                nc.scalar.copy(ysb, B[2]).then_inc(ev("y_sb"), 1)

            act.wait_ge(ev("mixer_freed"), 1)
            tokens_out(0)
            with act.Fori(0, NE) as e:
                sigmoid_step(e)
                tokens_out(e + 1)
                down_steps(e)
            act.wait_ge(ev("over_list"), 1)
            n_over = act.value_load(small_i[0:1, 16:17], min_val=0, max_val=MAX_OVER)
            with act.Fori(0, MAX_OVER) as j:
                with act.If(n_over > j):
                    tokens_out(j + (NE + 1))
                    sigmoid_step(j + NE)
                    down_steps(j + NE)

            for t in range(2):
                act.wait_ge(ev("x2_ready"), 2 * t + 2)
                nc.scalar.activation(rows[:, t, :], xres[:, t, :], ACT.Square, accum_out=ssf[:, t:t + 1]).then_inc(ev("ssf"), 1)
            act.wait_ge(ev("ssf"), 2)
            nc.scalar.activation(rsf, ssf, ACT.Sqrt, bias=eps, scale=1.0 / D).then_inc(ev("rmsf"), 1)

        @block.vector
        def _(dve):
            ch = Chain(dve, "dve_steps")
            V = nc.vector

            dve.wait_ge(ev("consts_loaded"), 48)
            V.tensor_copy(flip, ident[:, ::-1]).then_inc(ev("flip_ready"), 1)
            dve.wait_ge(ev("cond_sig"), 1)
            V.tensor_tensor(cond, cond, gtmp[0:16, 0:P], ALU.mult).then_inc(ev("cond_silu"), 1)
            dve.wait_ge(ev("condT_ps"), 1)
            dve.wait_ge(ev("condT_zero"), 1)
            V.tensor_copy(condT[:, :, 0:G], B[4][:, 0:16].rearrange("p (r k) -> p k r", r=G)).then_inc(ev("condT_ready"), 1)

            def mod_part(n):
                dve.wait_ge(chunks_used, (AT_MODS1 if n < 4 else AT_MODS2 - 8) + 2 * n + 2)
                if n >= 2:
                    dve.wait_ge(ev("mod_bc"), n - 1)
                V.tensor_copy(part[n % 2], B[mod_bank(n)]).then_inc(ev("mod_part"), 1)

            def mod_out(n):
                dve.wait_ge(ev("mod_bc"), n + 1)
                m, cols = MODS[n // 2], slice(512 * (n % 2), 512 * (n % 2 + 1))
                src = B[bc_bank(n)]
                if m in (1, 4):
                    if m == 4:
                        dve.wait_ge(ev("gain2_loaded"), 16)
                    V.scalar_tensor_tensor(gsc[:, cols], src, 1.0, gain[:, cols], ALU.add, ALU.mult).then_inc(ev("mod_out"), 1)
                else:
                    dst = {0: shf, 3: shf, 2: g1, 5: g2}[m]
                    V.tensor_copy(dst[:, cols], src).then_inc(ev("mod_out"), 1)

            mod_part(0)
            mod_part(1)
            mod_out(0)
            mod_part(2)
            mod_out(1)
            dve.wait_ge(ev("rms1"), 1)
            ch.step(V.reciprocal(rstd, rstd))
            mod_part(3)
            for t in range(2):
                dve.wait_ge(ev("mod_out"), 2)
                ch.step(V.scalar_tensor_tensor(rows[:, t, :], xres[:, t, :], rstd[:, t:t + 1], gsc, ALU.mult, ALU.mult))
            mod_out(2)
            mod_out(3)
            dve.wait_ge(ev("mod_out"), 4)
            for t in range(2):
                V.tensor_tensor(rows[:, t, :], rows[:, t, :], shf, ALU.add).then_inc(ev("h_ready"), 1)

            dve.wait_ge(ev("early_ps"), 3)
            V.tensor_copy(ckT.rearrange("p h l -> p (h l)"), B[6]).then_inc(ev("early_out"), 1)
            V.tensor_copy(wsT.rearrange("p g t -> p (g t)"), B[7]).then_inc(ev("early_out"), 1)
            V.tensor_copy(gbT, B[3][:, 0:GM]).then_inc(ev("early_out"), 1)

            dve.wait_ge(ev("lb_loaded"), 16)
            ch.step(V.tensor_tensor(lb_t[:, 4:8], lb_t[:, 0:4], lb_t[:, 0:4], ALU.max))
            V.tensor_tensor(lb_t[:, 4:8], lb_t[:, 0:4], lb_t[:, 4:8], ALU.subtract).then_inc(ev("lb_shift"), 1)
            dve.wait_ge(ev("lb_exp"), 1)
            ch.step(V.reciprocal(lb_t[:, 4:8], lb_t[:, 0:4]))
            ch.step(V.tensor_tensor(lb_t[:, 4:8], lb_t[:, 0:4], lb_t[:, 4:8], ALU.mult))
            ch.step(V.tensor_tensor(lbT, lb_t[:, 4:8], lb_t[:, 4:8], ALU.subtract))
            ch.step(V.tensor_scalar(omlT, lbT, -1.0, 1.0, ALU.mult, ALU.add))
            dve.wait_ge(ev("masks_loaded"), 16)
            V.tensor_copy(masks.rearrange("p m t -> p (m t)"), k_pool).then_inc(ev("masks_ready"), 1)
            ch.step(V.memset(biasN, NEG))
            for q in range(2):
                dve.wait_ge(ev("flip_ps"), 1)
                dve.wait_ge(ev("masks_ready"), 1)
                V.copy_predicated(biasN[:, HP * q:HP * (q + 1), :], masks[:, M_WINDOW, :].unsqueeze(1).to_broadcast([P, HP, P]),
                                  B[2 + q].rearrange("p (h k) -> p h k", h=HP)).then_inc(ev("biasN_ready"), 1)

            dve.wait_ge(ev("win_out"), 2)
            dve.wait_ge(ev("sig_z"), 2)
            for d in range(2):
                for h in range(RP):
                    n, cols = 2 * d + h, slice(256 * h, 256 * (h + 1))
                    V.tensor_scalar(sig[:, d, cols], sig[:, d, cols], omlT[:, n:n + 1], lbT[:, n:n + 1],
                                    ALU.mult, ALU.add).then_inc(ev("f_ready"), 1)
                    V.tensor_scalar(keyT[:, d, cols], keyT[:, d, cols], omlT[:, n:n + 1], None, ALU.mult).then_inc(ev("key_ready"), 1)
            dve.wait_ge(ev("f_ready"), 4)
            ch.step(V.tensor_scalar(cumT, sig, 2.0 ** -LN_SPLIT, None, ALU.max))
            V.tensor_scalar(sig, sig, F_FLOOR, 2.0 ** -LN_SPLIT, ALU.max, ALU.min).then_inc(ev("f_parts"), 1)
            dve.wait_ge(ev("ln_parts"), 2)
            ch.step(V.tensor_tensor(sig, sig, cumT, ALU.add))
            ch.step(V.memset(Dl[:, 0, :], 1.0))
            ch.step(V.memset(Dl[:, 0, 0:512:P], 0.0))
            V.tensor_tensor_scan(cumT[:, 0, :], Dl[:, 0, :], sig[:, 0, :], 0.0, ALU.mult, ALU.add).then_inc(ev("logf_used"), 1)
            V.tensor_tensor_scan(cumT[:, 1, ::-1], Dl[:, 0, :], sig[:, 1, ::-1], 0.0, ALU.mult, ALU.add).then_inc(ev("logf_used"), 1)
            dve.wait_ge(ev("logf_used"), 2)
            dve.wait_ge(ev("key_ready"), 4)
            dve.wait_ge(ev("qk_zero"), 2)
            V.tensor_tensor(Kt[:, 1, 0, :], keyT[:, 0, :], keyT[:, 1, :], ALU.add).then_inc(ev("ksum_ready"), 1)

            def level_diff(n):
                w = LEVELS[n]
                for d in range(2):
                    b = cumT[:, d, :].rearrange("p (n m) -> p n m", m=2 * w)
                    edge = b[:, :, w - 1:w] if d == 0 else b[:, :, w:w + 1]
                    ins = V.tensor_tensor(Dl[:, d, :].rearrange("p (n m) -> p n m", m=2 * w), b,
                                          edge.to_broadcast([P, 256 // w, 2 * w]), ALU.subtract)
                    if d:
                        ins.then_inc(ev("lvl_diff"), 1)
                    else:
                        ch.step(ins)

            def level_qk(n):
                w, buf = LEVELS[n], n % 2
                dve.wait_ge(ev("lvl_exp"), 4 * (n + 1))
                if n >= 1:
                    dve.wait_ge(ev("lvl_mm"), n)
                for d in range(2):
                    ex_ = Dl[:, d, :].rearrange("p (n h m) -> p n h m", h=2, m=w)
                    for h in range(2):
                        query = h == 1 - d
                        dst = (Qt if query else Kt)[:, buf, d, :].rearrange("p (n h m) -> p n h m", h=2, m=w)
                        src = (hqT if query else keyT[:, d, :]).rearrange("p (n h m) -> p n h m", h=2, m=w)
                        V.tensor_tensor(dst[:, :, h, :], ex_[:, :, h, :], src[:, :, h, :], ALU.mult).then_inc(ev("lvl_qk"), 1)

            def level_store(n):
                dve.wait_ge(ev("lvl_mm"), n + 2)
                if n < 0:
                    for q in range(2):
                        V.tensor_copy(AT[:, q, :], B[2 + q]).then_inc(ev("lvl_store"), 1)
                    return
                for d in range(2):
                    dve.wait_ge(ev("lvl_store"), 4 * n + 2 * d + 2)
                    for q in range(2):
                        V.copy_predicated(AT[:, q, :].rearrange("p (n t) -> p n t", n=4),
                                          masks[:, 7 * d + n, :].unsqueeze(1).to_broadcast([P, 4, P]),
                                          B[2 + 2 * d + q].rearrange("p (n t) -> p n t", n=4)).then_inc(ev("lvl_store"), 1)

            level_diff(0)
            for n in range(len(LEVELS)):
                level_qk(n)
                if n + 1 < len(LEVELS):
                    dve.wait_ge(ev("lvl_qk"), 4 * (n + 1))
                    level_diff(n + 1)
                level_store(n - 1)
            level_store(6)
            dve.wait_ge(ev("lvl_qk"), 28)
            for d in range(2):
                b = cumT[:, d, :].rearrange("p (n m) -> p n m", m=P)
                edge = b[:, :, P - 1:P] if d == 0 else b[:, :, 0:1]
                ins = V.tensor_tensor(Dl[:, d, :].rearrange("p (n m) -> p n m", m=P), b, edge.to_broadcast([P, 4, P]), ALU.subtract)
                if d:
                    dve.wait_ge(ev("lvl_mm"), 8)
                    ins.then_inc(ev("end_diff"), 1)
                else:
                    ch.step(ins)
            dve.wait_ge(ev("rmsg"), 1)
            ch.step(V.reciprocal(rsg, rsg))
            dve.wait_ge(ev("mixer_loaded"), 96)
            for g in range(G):
                V.scalar_tensor_tensor(rows[:, g, 768:1024], rows[:, g, 768:1024], rsg[:, g:g + 1], vng,
                                       ALU.mult, ALU.mult).then_inc(ev("vg_ready"), 1)
            dve.wait_ge(ev("end_exp"), 2)
            for d in range(2):
                V.tensor_tensor(Qt[:, 0, d, :], Qt[:, 0, d, :], hqT, ALU.mult).then_inc(ev("end_ready"), 1)
                V.tensor_tensor(Kt[:, 0, d, :], Dl[:, d, :], keyT[:, d, :], ALU.mult).then_inc(ev("end_ready"), 1)
            dve.wait_ge(ev("z_ps"), 1)
            for g in range(GM):
                V.tensor_scalar(rows[:, :, 768 + HD * g:768 + HD * (g + 1)], B[7][:, P * g:P * (g + 1)].rearrange("p (r n) -> p r n", r=G),
                                gbT[:, g:g + 1], None, ALU.add).then_inc(ev("zb_ready"), 1)
            dve.wait_ge(ev("zb_ready"), 4)
            dve.wait_ge(chunks_used, AT_WIN + G_U + 1)
            V.tensor_tensor(rows[:, :, 768:1024], rows[:, :, 768:1024], B[G_U % 2].rearrange("p (g n) -> p g n", g=G),
                            ALU.mult).then_inc(ev("gmlp_ready"), 1)
            dve.wait_ge(ev("sig_g"), 1)
            V.tensor_tensor(rows[:, :, 512:768], gtmp.rearrange("p (g n) -> p g n", g=G),
                            B[H_G % 2].rearrange("p (g n) -> p g n", g=G), ALU.mult).then_inc(ev("silu_g"), 1)

            dve.wait_ge(ev("o_ps"), 1)
            o_sb = gtmp.rearrange("p (g h n) -> p g h n", g=G, h=RH)
            dve.wait_ge(ev("silu_g"), 1)
            for q in range(2):
                src = B[2 + q].rearrange("p (g h n) -> p g h n", g=G, h=4)[:, :, 0:RP, :]
                V.tensor_copy(o_sb[:, :, q:RH:2, :], src).then_inc(ev("o_out"), 1)
            dve.wait_ge(ev("o_out"), 2)
            o_rows = gtmp.rearrange("p (n v) -> p n v", v=HD)
            o_sq = keyT[:, 0, :].rearrange("p (n v) -> p n v", v=HD)
            ch.step(V.tensor_tensor(o_sq, o_rows, o_rows, ALU.mult))
            ch.step(V.tensor_reduce(sso, o_sq, AX.X, ALU.add))
            V.tensor_scalar(sso, sso, 1.0 / HD, EPS, ALU.mult, ALU.add).then_inc(ev("ms_o"), 1)
            dve.wait_ge(ev("rms_o"), 1)
            ch.step(V.reciprocal(rso, rso))
            ch.step(V.tensor_tensor(o_rows, o_rows, rso.unsqueeze(2).to_broadcast([P, 8, HD]), ALU.mult))
            dve.wait_ge(ev("mixer_loaded"), 96)
            ch.step(V.tensor_tensor(o_rows, o_rows, ong.unsqueeze(1).to_broadcast([P, 8, HD]), ALU.mult))
            V.tensor_tensor(rows[:, :, 512:768], rows[:, :, 512:768], gtmp.rearrange("p (g n) -> p g n", g=G),
                            ALU.mult).then_inc(ev("hgrn_ready"), 1)

            def late_mod(n):
                mod_part(n)
                mod_out(n)

            dve.wait_ge(ev("state_ps"), 1)
            late_mod(4)
            late_mod(5)

            dve.wait_ge(ev("score_p"), 1)
            for q in range(2):
                V.tensor_reduce(mx[:, HP * q:HP * (q + 1)], B[2 + q].rearrange("p (h k) -> p h k", h=HP), AX.X, ALU.max).then_inc(ev("mx_p"), 1)
            dve.wait_ge(ev("mx_p"), 2)
            V.tensor_scalar(nmx, mx, -SCALE, None, ALU.mult).then_inc(ev("nmx_p"), 1)
            late_mod(6)
            late_mod(7)
            dve.wait_ge(ev("exp_p"), NH)
            ch.step(V.reciprocal(rinv, rsum))
            dve.wait_ge(ev("att_p_ps"), 1)
            V.tensor_tensor(rows[:, 0, 0:512].rearrange("p (h q d) -> p h q d", h=HP, q=2), B[6].rearrange("p (h q d) -> p h q d", h=HP, q=2),
                            rinv.rearrange("p (q h) -> p h q", q=2).unsqueeze(3).to_broadcast([P, HP, 2, HD]), ALU.mult).then_inc(ev("att_p"), 1)
            dve.wait_ge(ev("sl_ps"), 1)
            dve.wait_ge(ev("biasN_ready"), 2)
            for q in range(2):
                V.scalar_tensor_tensor(probs[:, q:NH:2, 0:P], B[2 + q].rearrange("p (h k) -> p h k", h=HP), SCALE,
                                       biasN[:, q:NH:2, :], ALU.mult, ALU.add).then_inc(ev("local_sc"), 1)
            dve.wait_ge(ev("local_sc"), 2)
            dve.wait_ge(ev("ctx_sc"), 2)
            ch.step(V.tensor_reduce(mx_s, probs, AX.X, ALU.max))
            V.tensor_scalar(nmx_s, mx_s, -1.0, None, ALU.mult).then_inc(ev("nmx_s"), 1)
            for n in range(8, 12):
                late_mod(n)
            dve.wait_ge(ev("exp_s"), NH)
            ch.step(V.reciprocal(rinv_s, rsum_s))
            dve.wait_ge(ev("att_s_ps"), 1)
            V.tensor_tensor(rows[:, 1, 0:512].rearrange("p (h d) -> p h d", h=NH), B[7].rearrange("p (h d) -> p h d", h=NH),
                            rinv_s.unsqueeze(2).to_broadcast([P, NH, HD]), ALU.mult).then_inc(ev("att_s"), 1)

            dve.wait_ge(chunks_used, AT_MOE)
            dve.wait_ge(ev("caches_stored"), 64)
            out_bank = (0, 1, 6, 7)
            for t in range(2):
                for half in range(2):
                    cols = slice(512 * half, 512 * (half + 1))
                    ch.step(V.tensor_tensor(gtmp if half else kout, B[out_bank[2 * t + half]], g1[:, cols], ALU.mult))
                    V.tensor_tensor(xres[:, t, cols], xres[:, t, cols], gtmp if half else kout, ALU.add).then_inc(ev("x1_ready"), 1)
            dve.wait_ge(ev("rms2"), 1)
            ch.step(V.reciprocal(rs2, rs2))
            dve.wait_ge(ev("x1_ready"), 4)
            dve.wait_ge(ev("mod_out"), 12)
            for t in range(2):
                ch.step(V.scalar_tensor_tensor(rows[:, t, :], xres[:, t, :], rs2[:, t:t + 1], gsc, ALU.mult, ALU.mult))
                V.tensor_tensor(rows[:, t, :], rows[:, t, :], shf, ALU.add).then_inc(ev("h2_ready"), 1)

            dve.wait_ge(ev("logits_ps"), 1)
            ch.step(V.tensor_copy(lg, B[0][:, 0:2 * NE].rearrange("p (t e) -> p t e", t=2)))
            for t in range(2):
                ch.step(V.max(rsm[:, 8 * t:8 * t + 8], lg[:, t, :]))
            V.tensor_scalar(rsm[:, 16:18], rsm[:, 0:16:8], -1.0, None, ALU.mult).then_inc(ev("nv1"), 1)
            ch.step(V.memset(csm, 1.0))
            for t in range(2):
                v4 = rsm[:, 8 * t + 3:8 * t + 4]
                ch.step(V.tensor_scalar(msk[:, t, :], lg[:, t, :], v4, None, ALU.is_gt))
                ch.step(V.tensor_reduce(rsm[:, 18 + t:19 + t], msk[:, t, :], AX.X, ALU.add))
                ch.step(V.tensor_scalar(rsm[:, 20 + t:21 + t], rsm[:, 18 + t:19 + t], -1.0, float(TOP_K), ALU.mult, ALU.add))
                ch.step(V.tensor_scalar(eqm[:, t, :], lg[:, t, :], v4, None, ALU.is_equal))
                ch.step(V.tensor_tensor_scan(mask4[:, 0, 0, :], csm[:, t, :], eqm[:, t, :], 0.0, ALU.mult, ALU.add))
                ch.step(V.scalar_tensor_tensor(eqm[:, t, :], mask4[:, 0, 0, :], rsm[:, 20 + t:21 + t], eqm[:, t, :], ALU.is_le, ALU.mult))
                ch.step(V.tensor_tensor(msk[:, t, :], msk[:, t, :], eqm[:, t, :], ALU.add))
            V.tensor_copy(mask4, msk.unsqueeze(2).to_broadcast([P, 2, CHUNKS, NE])).then_inc(ev("mask_ready"), 1)
            dve.wait_ge(ev("r_exp"), 2)
            ch.step(V.tensor_tensor(ex, ex, msk, ALU.mult))
            ch.step(V.tensor_reduce(rsm[:, 22:24], ex, AX.X, ALU.add))
            ch.step(V.reciprocal(rsm[:, 24:26], rsm[:, 22:24]))
            for t in range(2):
                V.tensor_scalar(gate[:, t, :], ex[:, t, :], rsm[:, 24 + t:25 + t], None, ALU.mult).then_inc(ev("gate_ready"), 1)
            ch.step(V.memset(rank, 0.0))
            dve.wait_ge(ev("rank_ps"), 1)
            for t in range(2):
                V.tensor_tensor(rank[:, t, 0:NE], B[1][:, NE * t:NE * (t + 1)], msk[:, t, :], ALU.mult).then_inc(ev("rank_ready"), 1)
            ch.step(V.tensor_tensor(flag, B[1][:, 64:65], cst[:, C_THR:C_THR + 1], ALU.is_gt))
            V.tensor_copy(zrow, zcol.to_broadcast([P, 512])).then_inc(ev("flag_ready"), 1)
            dve.wait_ge(ev("pos_ps"), 1)
            ch.step(V.tensor_copy(posn, B[0][:, 64:65]))
            V.tensor_scalar(onehot, cst[:, C_IOTA:C_IOTA + 16], posn, flag, ALU.is_equal, ALU.mult).then_inc(ev("onehot_ready"), 1)
            dve.wait_ge(ev("list_ps"), 1)
            V.tensor_copy(offb, B[0][:, 128:144]).then_inc(ev("offb_ready"), 1)
            ch.step(V.tensor_copy(small_i[0:1, 0:16], B[0][0:1, 144:160]))
            V.tensor_copy(small_i[0:1, 16:17], B[0][0:1, 160:161]).then_inc(ev("over_list"), 1)

            def route(e, buf, off=None):
                V.tensor_copy(pick[:, buf, :], identE[:, bass.ds(e, 1)].to_broadcast([NE, P]))
                for t in range(2):
                    r = rank[:, t, bass.ds(e, 1)]
                    if off is None:
                        ins = V.tensor_scalar(Ptok[:, t, :], cst[:, C_SLOTROW:C_SLOTROW + CAP], r, None, ALU.is_equal)
                    else:
                        ins = V.tensor_scalar(Ptok[:, t, :], cst[:, C_SLOTROW:C_SLOTROW + CAP], off, r, ALU.add, ALU.is_equal)
                ins.then_inc(ev("route_ready"), 1)

            def slot_gates(count, buf, off=None):
                dve.wait_ge(ev("bc_ps"), count + 1)
                scol = cst[:, C_SLOTCOL:C_SLOTCOL + 1]
                if off is None:
                    ch.step(V.tensor_scalar(gT[:, buf, :], B[3][:, 0:256], scol, None, ALU.is_equal))
                else:
                    ch.step(V.tensor_scalar(gT[:, buf, :], B[3][:, 0:256], off, scol, ALU.subtract, ALU.is_equal))
                V.tensor_tensor(gT[:, buf, :], gT[:, buf, :], B[3][:, 256:512], ALU.mult).then_inc(ev("gT_ready"), 1)

            def gate_step(count):
                dve.wait_ge(chunks_used, used(3, count))
                V.tensor_scalar(actb, B[0], LIMIT, None, ALU.min).then_inc(ev("gate_min"), 1)

            def up_step(count):
                dve.wait_ge(chunks_used, used(7, count))
                V.tensor_scalar(upb, B[1], -LIMIT, LIMIT, ALU.max, ALU.min).then_inc(ev("up_clip"), 1)
                dve.wait_ge(ev("up_clip"), count + 1)
                ch.step(V.scalar_tensor_tensor(upb, upb, 1.0, actb, ALU.add, ALU.mult))
                dve.wait_ge(ev("gate_sig"), count + 1)
                V.tensor_tensor(ab, upb, sigb, ALU.mult).then_inc(ev("a_ready"), 1)

            dve.wait_ge(ev("idE_ready"), 1)
            dve.wait_ge(ev("rank_ready"), 2)
            V.memset(gT[:, 1, :], 0.0).then_inc(ev("mixer_freed"), 1)
            V.memset(ysb, 0.0).then_inc(ev("y_sb"), 1)
            route(0, 0)
            slot_gates(0, 0)
            with dve.Fori(0, NE // 2) as i:
                ch.enter(i, 4)
                for u in range(2):
                    e = i * 2 + u
                    gate_step(e)
                    dve.wait_ge(ev("xe_ps"), e + 1)
                    route(e + 1, 1 - u)
                    slot_gates(e + 1, 1 - u)
                    up_step(e)
            ch.leave(NE // 2)
            dve.wait_ge(ev("over_list"), 1)
            n_over = dve.value_load(small_i[0:1, 16:17], min_val=0, max_val=MAX_OVER)
            with dve.Fori(0, MAX_OVER) as j:
                with dve.If(n_over > j):
                    ch.enter(j, 2)
                    e = dve.value_load(small_i[0:1, bass.ds(j, 1)], min_val=0, max_val=NE - 1)
                    off = offb[:, bass.ds(j, 1)]
                    dve.wait_ge(ev("combined"), j + (NE + 1))
                    route(e, 0, off)
                    slot_gates(j + (NE + 1), 0, off)
                    gate_step(j + NE)
                    up_step(j + NE)

            fin = Chain(dve, "dve_last_steps")
            dve.wait_ge(ev("moe_done"), 1)
            acc = [B[4 + n] for n in range(4)]
            for t in range(2):
                for half in range(2):
                    cols = slice(512 * half, 512 * (half + 1))
                    buf = k_pool[:, 512 * (2 * t + half):512 * (2 * t + half + 1)]
                    fin.step(V.tensor_tensor(buf, acc[2 * t + half], g2[:, cols], ALU.mult))
                    V.tensor_tensor(xres[:, t, cols], xres[:, t, cols], buf, ALU.add).then_inc(ev("x2_ready"), 1)
            dve.wait_ge(ev("rmsf"), 1)
            dve.wait_ge(ev("gain3_loaded"), 16)
            fin.step(V.reciprocal(rsf, rsf))
            for t in range(2):
                V.scalar_tensor_tensor(xres[:, t, :], xres[:, t, :], rsf[:, t:t + 1], gain, ALU.mult, ALU.mult).then_inc(ev("y_ready"), 1)

        @block.tensor
        def _(pe):
            mm, tr = nc.tensor.matmul, nc.tensor.transpose
            pe.wait_ge(ev("consts_loaded"), 48)
            pe.wait_ge(ev("cond_silu"), 1)
            tr(B[4][:, 0:16], cond, ident[0:16, 0:16]).then_inc(ev("condT_ps"), 1)
            pe.wait_ge(ev("condT_ready"), 1)
            pe.wait_ge(ev("ones_set"), 1)
            pe.wait_ge(ev("consts_loaded"), 48)

            def slot_wait(n):
                pe.wait_ge(slot_loaded[n % RING], 16 * (n // RING + 1))

            def mod_sums(n):
                if n >= 2:
                    pe.wait_ge(ev("mod_part"), n - 1 if n < 4 else n)
                at = (AT_MODS1 if n < 4 else AT_MODS2 - 8) + 2 * n
                for r in range(2):
                    slot_wait(at + r)
                    w = ring[:, (at + r) % RING, :].rearrange("p (k n) -> p k n", k=4)
                    for j in range(4):
                        ins = mm(B[mod_bank(n)][32 * j:32 * (j + 1), :], condT[:, 4 * r + j, :], w[:, j, :],
                                 start=r == 0, stop=r == 1, tile_position=(0, 32 * j))
                    ins.then_inc(chunks_used, 1)

            def mod_spread(n):
                if n >= 2:
                    pe.wait_ge(ev("mod_out"), n - 1 if n < 5 else n)
                pe.wait_ge(ev("mod_part"), n + 1)
                m, half = MODS[n // 2], n % 2
                row = 2 * m + half
                mm(B[bc_bank(n)], cst[:, C_MODSEL:C_MODSEL + P], part[n % 2], start=True, stop=False)
                mm(B[bc_bank(n)], ident[0:12, row:row + 1].to_broadcast([12, P]), bmod, start=False, stop=True).then_inc(ev("mod_bc"), 1)

            mod_sums(0)
            mod_sums(1)
            mod_spread(0)
            mod_sums(2)
            mod_spread(1)
            mod_sums(3)
            mod_spread(2)
            mod_spread(3)
            pe.wait_ge(ev("early_loaded"), 48)
            for h in range(HP):
                ins = tr(B[6][:, P * h:P * (h + 1)], ck[:, P * h:P * (h + 1)], ident)
            ins.then_inc(ev("early_ps"), 1)
            pe.wait_ge(ev("early_loaded"), 48)
            for g in range(GM):
                ins = tr(B[7][:, P * g:P * (g + 1)], ws[:, g, :], ident)
            ins.then_inc(ev("early_ps"), 1)
            pe.wait_ge(ev("early_loaded"), 48)
            pe.wait_ge(ev("mod_out"), 4)
            tr(B[3][:, 0:GM], gb_rows, ident[0:GM, 0:GM]).then_inc(ev("early_ps"), 1)
            pe.wait_ge(ev("early_out"), 3)
            for t in range(2):
                pe.wait_ge(ev("h_ready"), t + 1)
                for q in range(2):
                    for k in range(4):
                        ins = tr(B[4 + 2 * t + q][:, P * k:P * (k + 1)], rows[:, t, P * (4 * q + k):P * (4 * q + k + 1)], ident)
                    ins.then_inc(ev("hT_ps"), 1)

            def project(i):
                if i >= 2:
                    pe.wait_ge(ev("win_out"), min(i - 1, G_V + 1))
                n = AT_WIN + i
                slot_wait(n)
                w = ring[:, n % RING, :].rearrange("p (k n) -> p k n", k=KT)
                bank = B[i % 2]
                for r in range(2):
                    for k in range(KT):
                        if i in (Z_F, Z_B, H_Q, K_0, K_1, Q_0, Q_1):
                            ins = mm(bank[:, 256 * r:256 * (r + 1)], w[:, k, P * r:P * (r + 1)],
                                     hT[:, k, :, :], start=k == 0, stop=k == KT - 1)
                        else:
                            ins = mm(bank[:, 256 * r:256 * (r + 1)], hT[:, k, r, :], w[:, k, :],
                                     start=k == 0, stop=k == KT - 1)
                ins.then_inc(chunks_used, 1)

            def level_mm(n):
                buf = n % 2
                if n < 0:
                    pe.wait_ge(ev("ksum_ready"), 1)
                    pe.wait_ge(ev("win_out"), H_Q + 1)
                else:
                    pe.wait_ge(ev("lvl_qk"), 4 * (n + 1))
                    pe.wait_ge(ev("lvl_store"), 4 * n + 2)
                for d in range(1 if n < 0 else 2):
                    keys = Kt[:, 1, 0, :] if n < 0 else Kt[:, buf, d, :]
                    queries = hqT if n < 0 else Qt[:, buf, d, :]
                    for m in range(4):
                        for q in range(2):
                            part_, cols = slice(HD * q, HD * (q + 1)), slice(P * m, P * (m + 1))
                            ins = mm(B[2 + 2 * d + q][:, cols], keys[part_, cols], queries[part_, cols], start=True, stop=True)
                ins.then_inc(ev("lvl_mm"), 1)

            pe.wait_ge(ev("hT_ready"), 4)
            pe.wait_ge(ev("bias_raw_loaded"), 64)
            pe.wait_ge(ev("flip_ready"), 1)
            for q in range(2):
                ins = mm(B[2 + q], flip,
                         bias_raw[:, HP * q:HP * (q + 1), :], start=True, stop=True)
            ins.then_inc(ev("flip_ps"), 1)
            for i in (Z_F, Z_B, H_Q, H_I, K_0, Q_0):
                project(i)
            pe.wait_ge(ev("biasN_ready"), 2)
            level_mm(-1)
            project(K_1)
            level_mm(0)
            pe.wait_ge(ev("win_out"), K_1 + 1)
            for h in range(HP):
                ins = tr(B[6][:, P * h:P * (h + 1)], kT[:, h, 0, :], ident)
            ins.then_inc(ev("kout_ps"), 1)
            project(Q_1)
            level_mm(1)
            project(V_0)
            level_mm(2)
            project(V_1)
            level_mm(3)
            project(G_V)
            level_mm(4)
            project(G_U)
            level_mm(5)
            project(H_G)
            level_mm(6)

            pe.wait_ge(ev("vg_ready"), 2)
            for g in range(GM):
                ins = mm(B[7][:, P * g:P * (g + 1)], wsT[:, g, :],
                         rows[:, :, 768 + HD * g:768 + HD * (g + 1)], start=True, stop=True)
            ins.then_inc(ev("z_ps"), 1)

            pe.wait_ge(ev("end_ready"), 4)
            pe.wait_ge(ev("kout_ready"), 1)
            for d in range(2):
                for h in range(RP):
                    ins = tr(B[6][:, P * (2 * d + h):P * (2 * d + h + 1)], Kt[:, 0, d, 256 * h:256 * h + P], ident)
            ins.then_inc(ev("kst_ps"), 1)
            pe.wait_ge(ev("lvl_store"), 30)
            pe.wait_ge(ev("mixer_loaded"), 96)
            for q in range(2):
                for g in range(G):
                    for h in range(RP):
                        out = B[2 + q][:, 256 * g + HD * h:256 * g + HD * (h + 1)]
                        m = 2 * h + g
                        ins = mm(out, AT[:, q, P * m:P * (m + 1)], hi[:, g, HD * (2 * h + q):HD * (2 * h + q + 1)],
                                 start=True, stop=g == 0)
                        for d in range(2 if g else 0):
                            ins = mm(out, Qt[HD * q:HD * (q + 1), 0, d, P * m:P * (m + 1)], s0[HD * q:HD * (q + 1), d, h, :],
                                     start=False, stop=d == 1)
            ins.then_inc(ev("o_ps"), 1)
            pe.wait_ge(ev("kst_ready"), 1)
            for d in range(2):
                for h in range(RH):
                    ins = mm(B[4][0:HD, 256 * d + HD * h:256 * d + HD * (h + 1)],
                             kstT[:, d, h // 2, HD * (h % 2):HD * (h % 2 + 1)], hi[:, 0, HD * h:HD * (h + 1)], start=True, stop=True)
            ins.then_inc(ev("state_ps"), 1)

            def late_mod(n):
                mod_sums(n)
                mod_spread(n)

            pe.wait_ge(ev("gmlp_ready"), 1)
            pe.wait_ge(ev("silu_g"), 1)
            late_mod(4)
            pe.wait_ge(ev("o_out"), 2)
            for h in range(HP):
                for q in range(2):
                    hd = slice(HD * q, HD * (q + 1))
                    ins = mm(B[2 + q][:, P * h:P * (h + 1)], qT[hd, h, 0, :], kT[hd, h, 0, :], start=True, stop=True)
            ins.then_inc(ev("score_p"), 1)
            late_mod(5)
            late_mod(6)
            pe.wait_ge(ev("exp_p"), NH)
            pe.wait_ge(ev("state_ready"), 1)
            for q in range(2):
                for h in range(HP):
                    ins = tr(B[4 + q][:, P * h:P * (h + 1)], probs_p[:, HP * q + h, :], ident)
                ins.then_inc(ev("pT_ps"), 1)
            for h in range(HP):
                for q in range(2):
                    hd = slice(HD * q, HD * (q + 1))
                    ins = mm(B[2 + q][:, P * h:P * (h + 1)], qT[hd, h, 1, :], kT[hd, h, 1, :], start=True, stop=True)
            ins.then_inc(ev("sl_ps"), 1)
            pe.wait_ge(ev("pT_ready"), 2)
            for h in range(HP):
                for q in range(2):
                    head = 2 * h + q
                    ins = mm(B[6][:, HD * head:HD * (head + 1)], k_pool[:, D + 512 * q + P * h:D + 512 * q + P * (h + 1)],
                             v[:, 0, HD * head:HD * (head + 1)], start=True, stop=True)
            ins.then_inc(ev("att_p_ps"), 1)
            for h in range(HP):
                for q in range(2):
                    hd = slice(HD * q, HD * (q + 1))
                    ins = mm(B[4 + q][:, P * h:P * (h + 1)], qT[hd, h, 1, :], ckT[hd, h, :], start=True, stop=True)
            ins.then_inc(ev("sc_ps"), 1)
            late_mod(7)
            for n in range(8, 12):
                late_mod(n)
            pe.wait_ge(ev("exp_s"), NH)
            for n in range(16):
                ins = tr(B[2 + n // 4][:, P * (n % 4):P * (n % 4 + 1)], probs[:, n // 2, P * (n % 2):P * (n % 2 + 1)], ident)
                if n % 4 == 3:
                    ins.then_inc(ev("sT_ps"), 1)
            pe.wait_ge(ev("mixer_loaded"), 96)
            for n in range(16):
                if n % 4 == 0:
                    pe.wait_ge(ev("sT_ready"), n // 4 + 1)
                head = n // 2
                src = (sT_lo if n < 8 else sT_hi)[:, P * (n % 8):P * (n % 8 + 1)]
                val = (cv if n % 2 else v[:, 1, :])[:, HD * head:HD * (head + 1)]
                ins = mm(B[7][:, HD * head:HD * (head + 1)], src, val, start=n % 2 == 0, stop=n % 2 == 1)
            ins.then_inc(ev("att_s_ps"), 1)

            for g in range(G):
                pe.wait_ge(ev("att_p" if g == 0 else "att_s"), 1)
                pe.wait_ge(ev("gmlp_ready"), 1)
                pe.wait_ge(ev("hgrn_ready"), 1)
                for kh in range(2):
                    for k in range(4):
                        ins = tr(B[2 + 2 * g + kh][:, P * k:P * (k + 1)], rows[:, g, P * (4 * kh + k):P * (4 * kh + k + 1)], ident)
                    ins.then_inc(ev("cat_ps"), 1)
            pe.wait_ge(ev("catT_ready"), 4)
            pe.wait_ge(ev("mod_out"), 12)
            out_bank = (0, 1, 6, 7)
            for r in range(4):
                slot_wait(AT_WOUT + r)
                w = ring[:, (AT_WOUT + r) % RING, :].rearrange("p (k n) -> p k n", k=2)
                for kk in range(2):
                    k = 2 * r + kk
                    for t in range(2):
                        for half in range(2):
                            ins = mm(B[out_bank[2 * t + half]], catT[:, k, t, :], w[:, kk, 512 * half:512 * (half + 1)],
                                     start=k == 0, stop=k == KT - 1)
                ins.then_inc(chunks_used, 1)

            for t in range(2):
                pe.wait_ge(ev("h2_ready"), t + 1)
                for q in range(2):
                    if t:
                        pe.wait_ge(ev("h2T_ready"), q + 1)
                    for k in range(4):
                        ins = tr(B[2 + (2 * t + q) % 2][:, P * k:P * (k + 1)], rows[:, t, P * (4 * q + k):P * (4 * q + k + 1)], ident)
                    ins.then_inc(ev("h2T_ps"), 1)
            pe.wait_ge(ev("mixer_loaded"), 96)
            pe.wait_ge(ev("rbias_loaded"), 16)
            pe.wait_ge(ev("h2T_ready"), 4)
            for t in range(2):
                out = B[0][:, NE * t:NE * (t + 1)]
                mm(out, ones_rows, rbias, start=True, stop=False)
                for k in range(KT):
                    ins = mm(out, h2T[:, k, t, :], rw[:, k, :], start=False, stop=k == KT - 1)
            ins.then_inc(ev("logits_ps"), 1)
            pe.wait_ge(ev("mask_ready"), 1)
            tri = cst[:, C_TRI:C_TRI + P]
            mm(B[1][:, 0:NE], tri, msk[:, 0, :], start=True, stop=True)
            mm(B[1][:, NE:2 * NE], tri, msk[:, 1, :], start=True, stop=False)
            mm(B[1][:, NE:2 * NE], ones[:, 0:1].to_broadcast([P, P]), msk[:, 0, :], start=False, stop=True)
            for t in range(2):
                ins = mm(B[1][:, 64:65], mask4[:, t].rearrange("p r e -> p (r e)"), ones[:, 0:1], start=t == 0, stop=t == 1)
            ins.then_inc(ev("rank_ps"), 1)
            pe.wait_ge(ev("flag_ready"), 1)
            mm(B[0][:, 64:65], cst[:, C_STRI:C_STRI + P], flag, start=True, stop=True).then_inc(ev("pos_ps"), 1)
            pe.wait_ge(ev("onehot_ready"), 1)
            mm(B[0][:, 128:144], cst[:, C_OFF:C_OFF + 1].to_broadcast([P, P]), onehot, start=True, stop=True)
            mm(B[0][:, 144:160], cst[:, C_E:C_E + 1].to_broadcast([P, P]), onehot, start=True, stop=True)
            mm(B[0][:, 160:161], ones[:, 0:1].to_broadcast([P, P]), flag, start=True, stop=True).then_inc(ev("list_ps"), 1)
            pe.wait_ge(ev("rank_ready"), 2)
            pe.wait_ge(ev("gate_ready"), 2)
            for t in range(2):
                tr(B[1][0:NE, P * t:P * (t + 1)], rank[:, t, 0:NE], ident)
                ins = tr(B[1][0:NE, 256 + P * t:256 + P * (t + 1)], gate[:, t, :], ident)
            ins.then_inc(ev("rgT_ps"), 1)

            def spread(buf, count):
                pe.wait_ge(ev("route_ready"), count + 1)
                mm(B[3], pick[:, buf, :], rgT, start=True, stop=True).then_inc(ev("bc_ps"), 1)

            def gather(count):
                pe.wait_ge(ev("gT_ready"), count + 1)
                for k in range(KT):
                    for t in range(2):
                        ins = mm(B[3][:, CAP * k:CAP * (k + 1)], rows[:, t, P * k:P * (k + 1)], Ptok[:, t, :],
                                 start=t == 0, stop=t == 1)
                ins.then_inc(ev("xe_ps"), 1)

            def product(bank, m, buf, lhsT, count):
                for half in range(2):
                    cols = slice(512 * half, 512 * (half + 1))
                    mm(bank[CAP * half:CAP * (half + 1), :], pick[:, buf, 0:CAP], mbias[:, m, cols], start=True, stop=False)
                for r in range(4):
                    cidx = 4 * m + r
                    pe.wait_ge(slot_loaded[expert_slot(cidx)], chunk_loads(cidx, count))
                    w = ring[:, expert_slot(cidx), :].rearrange("p (k n) -> p k n", k=2)
                    for kk in range(2):
                        for half in range(2):
                            ins = mm(bank[CAP * half:CAP * (half + 1), :], lhsT(2 * r + kk), w[:, kk, 512 * half:512 * (half + 1)],
                                     start=False, stop=r == 3 and kk == 1)
                    ins.then_inc(chunks_used, 1)

            def combine(buf, stored):
                pe.wait_ge(ev("y_sb"), stored)
                for t in range(2):
                    for half in range(2):
                        r = slice(CAP * half, CAP * (half + 1))
                        ins = mm(B[4 + 2 * t + half], gT[r, buf, P * t:P * (t + 1)], ysb[r, :], start=False, stop=False)
                ins.then_inc(ev("combined"), 1)

            def xe_tile(k):
                return xe[:, k, :]

            def a_tile(k):
                return aT[:, k % 4, CAP * (k // 4):CAP * (k // 4 + 1)]

            def down(buf, count):
                pe.wait_ge(ev("a_ready"), count + 1)
                for q in range(4):
                    ins = tr(B[2][:, P * q:P * (q + 1)], ab[:, P * q:P * (q + 1)], ident)
                ins.then_inc(ev("aT_ps"), 1)
                pe.wait_ge(ev("aT_ready"), count + 1)
                product(B[2], 2, buf, a_tile, count)

            pe.wait_ge(ev("flag_ready"), 1)
            pe.wait_ge(ev("x1_ready"), 4)
            for n in range(4):
                mm(B[4 + n], zrow[:, 0:P], zrow, start=True, stop=False)
            pe.wait_ge(ev("rgT_ready"), 1)
            pe.wait_ge(ev("mbias_loaded"), 48)
            spread(0, 0)
            gather(0)
            with pe.Fori(0, NE // 2) as i:
                for u in range(2):
                    e = i * 2 + u
                    pe.wait_ge(ev("xe_ready"), e + 1)
                    product(B[0], 0, u, xe_tile, e)
                    combine(1 - u, e + 1)
                    spread(1 - u, e + 1)
                    product(B[1], 1, u, xe_tile, e)
                    gather(e + 1)
                    down(u, e)
            combine(1, NE + 1)
            pe.wait_ge(ev("over_list"), 1)
            n_over = pe.value_load(small_i[0:1, 16:17], min_val=0, max_val=MAX_OVER)
            with pe.Fori(0, MAX_OVER) as j:
                with pe.If(n_over > j):
                    spread(0, j + (NE + 1))
                    gather(j + (NE + 1))
                    pe.wait_ge(ev("xe_ready"), j + (NE + 2))
                    product(B[0], 0, 0, xe_tile, j + NE)
                    product(B[1], 1, 0, xe_tile, j + NE)
                    down(0, j + NE)
                    combine(0, j + (NE + 2))
            for n in range(4):
                ins = mm(B[4 + n], zrow[:, 0:P], zrow, start=False, stop=True)
            ins.then_inc(ev("moe_done"), 1)


_INS = ['x_prompt', 'x_sample', 'cache_k', 'cache_v', 'state_hgrn_fwd', 'state_hgrn_bwd', 'c', 'c_ctx',
        'w_mod', 'b_mod', 'norm1_g', 'norm2_g', 'w_in', 'na_rel_bias', 'hgrn_lb', 'hgrn_onorm_g',
        'gmlp_vnorm_g', 'gmlp_ws', 'gmlp_b', 'w_out', 'router_w', 'router_b', 'w_gate', 'b_gate',
        'w_up', 'b_up', 'w_down', 'b_down', 'final_g']
_OUTS = [(1, P, D), (1, P, D), (1, 1, P, NH, HD), (1, 1, P, NH, HD), (1, 1, RH, HD, HD), (1, 1, RH, HD, HD)]


def kernel(**inputs):
    import concourse.bacc as bacc
    from concourse.bass_utils import run_bass_kernel_spmd

    nc = bacc.Bacc("TRN2", target_bir_lowering=False, num_devices=1)
    arrays, args = {}, []
    const_f32, const_masks = shape_constants()
    given = [(name, inputs[name]) for name in _INS] + [("const_f32", const_f32), ("const_masks", const_masks)]
    for name, array in given:
        array = np.ascontiguousarray(array)
        arrays[f"in_{name}"] = array
        args.append(nc.dram_tensor(f"in_{name}", array.shape, mybir.dt.from_np(array.dtype), kind="ExternalInput").ap())
    for i, shape in enumerate(_OUTS):
        args.append(nc.dram_tensor(f"out_{i}", shape, F32, kind="ExternalOutput").ap())
    hybrid_layer(nc, *args)
    r = run_bass_kernel_spmd(nc, [arrays], core_ids=[0])
    return tuple(r.results[0][f"out_{i}"] for i in range(len(_OUTS)))
```

```python
from contextlib import ExitStack

import numpy as np

import concourse.bass as bass
from concourse import mybir

F32 = mybir.dt.float32
I32 = mybir.dt.int32
U8 = mybir.dt.uint8
ALU = mybir.AluOpType
ACT = mybir.ActivationFunctionType
AX = mybir.AxisListType

P = 128
D = 1024
KT = D // P
G = 2
HALF = 64
HD = 64
NH = 8
HP = NH // 2
RH = 4
RP = RH // 2
GM = 4
GRID_W = 64
NA_KH, NA_KW = 8, 16
NE = 32
TOP_K = 4
CAP = 64
CHUNKS = G * P // CAP
MAX_OVER = (G * P * TOP_K - NE) // CAP
LIMIT, ALPHA = 7.0, 1.702
EPS = 1e-6
F_FLOOR = 1e-30
LN_SPLIT = 60
NEG = -1e30
SCALE = HD ** -0.5

RING = 12
SLOT = 2048
MODS = [1, 0, 2, 4, 3, 5]
WIN = [7, 8, 6, 9, 2, 0, 3, 1, 4, 5, 12, 11, 10]
Z_F, Z_B, H_Q, H_I, K_0, Q_0, K_1, Q_1, V_0, V_1, G_V, G_U, H_G = range(13)
AT_WIN = 8
AT_MODS2 = AT_WIN + len(WIN)
AT_WOUT = AT_MODS2 + 12
AT_MODG2 = AT_WOUT + 4
AT_MOE = AT_MODG2 + 4
WOUT = [2, 3, 0, 1]
LEVELS = [64, 32, 16, 8, 4, 2, 1]

C_IDENT, C_TRI, C_STRI, C_MODSEL, C_SLOTROW = 0, P, 2 * P, 3 * P, 4 * P
C_SLOTCOL = C_SLOTROW + CAP
C_THR, C_E, C_OFF = C_SLOTCOL + 1, C_SLOTCOL + 2, C_SLOTCOL + 3
C_IOTA = C_SLOTCOL + 4
C_END = C_IOTA + 16
M_DIAG, M_WINDOW = 14, 15


def shape_constants():
    f = np.zeros((P, C_END), np.float32)
    i = np.arange(P)
    f[:, C_IDENT:C_IDENT + P] = np.eye(P)
    f[:, C_TRI:C_TRI + P] = i[:, None] <= i[None, :]
    f[:, C_STRI:C_STRI + P] = i[:, None] < i[None, :]
    for j in range(4):
        for r in range(G):
            f[32 * j + r, C_MODSEL + HALF * r:C_MODSEL + HALF * (r + 1)] = 1
    f[:, C_SLOTROW:C_SLOTROW + CAP] = np.arange(1, CAP + 1)
    f[:, C_SLOTCOL] = i % CAP + 1
    f[:, C_THR] = np.where(i < NE, 1e9, CAP * (i // NE))
    f[:, C_E] = i % NE
    f[:, C_OFF] = CAP * (i // NE)
    f[:, C_IOTA:C_IOTA + 16] = np.arange(16)
    m = np.zeros((P, 16, P), np.float32)
    s, t = i[:, None], i[None, :]
    for n, w in enumerate(LEVELS):
        same = s // (2 * w) == t // (2 * w)
        first, second = s % (2 * w) < w, t % (2 * w) >= w
        m[:, n] = same & first & second
        m[:, 7 + n] = m[:, n].T
    m[:, M_DIAG] = s == t
    qc, kc = s % GRID_W, t % GRID_W
    start = np.clip(qc - NA_KW // 2, 0, GRID_W - NA_KW)
    m[:, M_WINDOW] = (kc >= start) & (kc < start + NA_KW)
    return f, m.reshape(P, 16 * P)


def hybrid_layer(nc, x_prompt, x_sample, cache_k, cache_v, state_hgrn_fwd, state_hgrn_bwd, c, c_ctx,
                 w_mod, b_mod, norm1_g, norm2_g, w_in, na_rel_bias, hgrn_lb, hgrn_onorm_g,
                 gmlp_vnorm_g, gmlp_ws, gmlp_b, w_out, router_w, router_b, w_gate, b_gate,
                 w_up, b_up, w_down, b_down, final_g, const_f32, const_masks,
                 y_prompt, y_sample, new_k, new_v, new_sf, new_sb):
    assert CHUNKS * NE == P and MAX_OVER <= 16
    ctx = ExitStack()
    with ctx:
        def sb(name, cols, dt=F32, parts=P):
            return ctx.enter_context(nc.sbuf_tensor(name, [parts, cols], dt))[:, :]

        events = {}

        def ev(name):
            if name not in events:
                events[name] = ctx.enter_context(nc.semaphore(name))
            return events[name]

        ring = sb("ring", RING * SLOT).rearrange("p (s w) -> p s w", s=RING)
        cst = sb("cst", C_END)
        masks = sb("masks", 16 * P, U8).rearrange("p (m t) -> p m t", m=16)
        xres = sb("xres", 2 * D).rearrange("p (t d) -> p t d", t=2)
        gain = sb("gain", D)
        gsc = sb("gsc", D)
        shf = sb("shf", D)
        rows = sb("rows", 2 * D).rearrange("p (t d) -> p t d", t=2)
        colsT = sb("colsT", 2 * D)
        kv_pool = sb("kv_pool", 3 * 1024)
        hq_hi = sb("hq_hi", 2 * 512)
        keyT = sb("keyT", 1024).rearrange("p (d n) -> p d n", d=2)
        cumT = sb("cumT", 1024).rearrange("p (d n) -> p d n", d=2)
        tmp = sb("tmp", 1024)
        g12 = sb("g12", 2 * D)
        qc = sb("qc", 512)
        k_pool = sb("k_pool", 2048)
        d_pool = sb("d_pool", 1024)
        at_pool = sb("at_pool", 1024)
        biasN = sb("biasN", 1024).rearrange("p (h k) -> p h k", h=NH)
        cv = sb("cv", 512)
        ckT = sb("ckT", 512).rearrange("p (h l) -> p h l", h=HP)
        wsT = sb("wsT", 512).rearrange("p (g t) -> p g t", g=GM)
        condT = sb("condT", KT * 32).rearrange("p (k m) -> p k m", k=KT)
        rbias = sb("rbias", NE, parts=1)
        s0 = sb("s0", 2 * RP * HD).rearrange("p (d h v) -> p d h v", d=2, h=RP)
        rw = sb("rw", KT * NE).rearrange("p (k e) -> p k e", k=KT)
        vng = sb("vng", GM * HD)
        ong = sb("ong", HD)
        cond = sb("cond", P, parts=16)
        gb_rows = sb("gb_rows", P, parts=GM)
        small = sb("small", 120)
        ones = sb("ones", 8)
        small_i = sb("small_i", 18, I32, parts=1)
        ones_rows = ones[0:1, 0:1].to_broadcast([1, P])

        ident = cst[:, C_IDENT:C_IDENT + P]
        ck = d_pool[:, 0:512]
        ws = d_pool[:, 512:1024].rearrange("p (g s) -> p g s", g=GM)
        hT = colsT.rearrange("p (k g t) -> p k g t", k=KT, g=G)
        catT = colsT.rearrange("p (k t gt) -> p k t gt", k=KT, t=2)
        h2T = catT
        qT, kT = (kv_pool[:, 1024 * n:1024 * (n + 1)].rearrange("p (h g t) -> p h g t", h=HP, g=G)
                  for n in range(2))
        v = kv_pool[:, 2048:3072].rearrange("p (g n) -> p g n", g=G)
        hqT = hq_hi[:, 0:512]
        hi = hq_hi[:, 512:1024].rearrange("p (g n) -> p g n", g=G)
        sig = tmp.rearrange("p (d n) -> p d n", d=2)
        kout = rows[:, :, 512:768]
        state_out = tmp[:, 0:512]
        xtmp = [tmp[:, 0:512], tmp[:, 512:1024]]
        gtmp = tmp[:, 512:1024]
        part = [at_pool[:, 0:512], at_pool[:, 512:1024]]
        AT = at_pool.rearrange("p (q n) -> p q n", q=2)
        Kl = k_pool[:, 0:1024].rearrange("p (d n) -> p d n", d=2)
        Qc = qc.rearrange("p (d n) -> p d n", d=2)
        Qend = qc.rearrange("p (d h t) -> p d h t", d=2, h=RP)
        Kend = k_pool[:, 0:512].rearrange("p (d h t) -> p d h t", d=2, h=RP)
        g1, g2 = g12[:, 0:D], g12[:, D:2 * D]
        Dl = d_pool.rearrange("p (d n) -> p d n", d=2)
        Dk = Dl[:, :, 0:256].rearrange("p d (h t) -> p d h t", h=RP)
        Dq = Dl[:, :, 256:512].rearrange("p d (h t) -> p d h t", h=RP)
        cum4 = cumT.rearrange("p d (h g t) -> p d h g t", h=RP, g=G)
        key4 = keyT.rearrange("p d (h g t) -> p d h g t", h=RP, g=G)
        hq4 = hqT.rearrange("p (h g t) -> p h g t", h=RP, g=G)
        kstT = d_pool[:, 0:512].rearrange("p (d h k) -> p d h k", d=2, h=RP)
        probs = k_pool[:, :].rearrange("p (h k) -> p h k", h=NH)
        probs_p = rows[:, :, 0:512].rearrange("p q (h k) -> p q h k", h=HP)
        pT_p = k_pool[:, 1024:2048].rearrange("p (q n) -> p q n", q=2)
        bias_raw = kv_pool[:, 2048:3072].rearrange("p (h k) -> p h k", h=NH)
        flip = kv_pool[:, 0:P]
        sT_lo = biasN.rearrange("p h k -> p (h k)")
        sT_hi = d_pool
        ss = small[:, 0:2]
        rstd = small[:, 2:4]
        lbT = small[:, 4:8]
        omlT = small[:, 8:12]
        lb_t = small[:, 12:20]
        gbT = small[:, 20:24]
        ssg = small[:, 24:26]
        rsg = small[:, 26:28]
        sso = small[:, 28:36]
        rso = small[:, 36:44]
        mx = small[:, 44:52]
        nmx = small[:, 52:60]
        rsum = small[:, 60:68]
        rinv = small[:, 68:76]
        mx_s = small[:, 76:84]
        nmx_s = small[:, 84:92]
        rsum_s = small[:, 92:100]
        rinv_s = small[:, 100:108]
        eps = small[:, 108:109]
        ssf = small[:, 110:112]
        rsf = small[:, 112:114]
        ss2 = small[:, 114:116]
        rs2 = small[:, 116:118]
        zcol = small[:, 118:119]

        moe_pool = kv_pool
        mbias = moe_pool[0:NE, :].rearrange("p (m n) -> p m n", m=3)
        actb = k_pool[:, 0:512]
        upb = k_pool[:, 512:1024]
        sigb = k_pool[:, 1024:1536]
        aT = k_pool[:, 1536:2048].rearrange("p (c s) -> p c s", c=4)
        ab = d_pool[:, 0:512]
        ysb = d_pool[:, 512:1024]
        xe = at_pool[:, 0:512].rearrange("p (k s) -> p k s", k=KT)
        gT = at_pool[:, 512:1024].rearrange("p (b t) -> p b t", b=2)
        pick = cumT[0:NE, 0, 0:256].rearrange("p (b m) -> p b m", b=2)
        Ptok = keyT[:, 0, 0:2 * CAP].rearrange("p (t s) -> p t s", t=2)
        rank = keyT[:, 0, 128:128 + 2 * (NE + 1)].rearrange("p (t e) -> p t e", t=2)
        gate = keyT[:, 0, 200:264].rearrange("p (t e) -> p t e", t=2)
        lg = keyT[:, 0, 264:328].rearrange("p (t e) -> p t e", t=2)
        msk = keyT[:, 0, 328:392].rearrange("p (t e) -> p t e", t=2)
        eqm = keyT[:, 0, 392:456].rearrange("p (t e) -> p t e", t=2)
        csm = keyT[:, 1, 0:64].rearrange("p (t e) -> p t e", t=2)
        ex = keyT[:, 1, 64:128].rearrange("p (t e) -> p t e", t=2)
        rsm = keyT[:, 1, 128:160]
        flag = keyT[:, 1, 160:161]
        posn = keyT[:, 1, 161:162]
        onehot = keyT[:, 1, 162:178]
        offb = keyT[:, 1, 178:194]
        mask4 = keyT[:, 1, 194:450].rearrange("p (t r e) -> p t r e", t=2, r=CHUNKS)
        rgT = cumT[0:NE, 1, :]
        zeros = zcol.to_broadcast([P, P])
        identE = wsT[0:NE, 0, 0:NE + 1]

        B = [ctx.enter_context(nc.psum_tensor(f"bank{n}", [P, 512], F32))[:, :] for n in range(8)]

        def mod_at(n):
            return 2 * n if n < 4 else AT_MODS2 + 2 * (n - 4) if n < 10 else AT_MODG2 + 2 * (n - 10)

        def mod_bank(n):
            return n % 2 if n < 4 else 0 if n < 10 else 6

        def bc_bank(n):
            return 2 + n % 2 if n < 4 else 1 if n < 10 else 7

        def bcast_row(ap):
            return ap.partition_broadcast(P).rearrange("p a d -> p (a d)")

        def level_view(ap, w):
            return ap.rearrange("p (n h m) -> p n h m", h=2, m=w)

        slot_loaded = [ctx.enter_context(nc.semaphore(f"slot{n}_loaded")) for n in range(RING)]
        chunks_used = ctx.enter_context(nc.semaphore("chunks_used"))

        def halves(ap):
            return ap.rearrange("(o p) d -> o p d", p=HALF)

        def expert_slot(cidx):
            return (AT_MOE + cidx) % RING

        def chunk_loads(cidx, e):
            return ((AT_MOE + cidx) // RING + 1 + e) * 16

        def used(cidx, e):
            return e * RING + (AT_MOE + cidx + 1)

        class Chain:

            def __init__(self, eng, name):
                self.eng, self.sem, self.n, self.at = eng, ev(name), 0, None

            def step(self, ins):
                ins.then_inc(self.sem, 1)
                self.n += 1
                self.eng.wait_ge(self.sem, self.n if self.at is None else self.at + self.n)

            def enter(self, reg, per):
                self.at, self.per, self.start = reg * per, per, self.n

            def leave(self, times):
                assert self.n - self.start == self.per, (self.n - self.start, self.per)
                self.at, self.n = None, self.start + self.per * times

        block = ctx.enter_context(nc.Block())

        @block.sync
        def _(sp):
            def slot_free(n):
                if n >= RING:
                    sp.wait_ge(chunks_used, n - RING + 1)

            def load(n, view, src):
                slot_free(n)
                sp.dma_start(view, src).then_inc(slot_loaded[n % RING], 16)

            n = 0
            sp.dma_start(cond[0:8, :], c_ctx.rearrange("(k p) -> k p", p=P)).then_inc(ev("cond_loaded"), 16)
            sp.dma_start(cond[8:16, :], c.rearrange("b (k p) -> (b k) p", p=P)).then_inc(ev("cond_loaded"), 16)

            def load_mod(m):
                nonlocal n
                for half in range(2):
                    for r in range(2):
                        src = w_mod[0, 512 * r:512 * (r + 1), m * D + 512 * half:m * D + 512 * (half + 1)]
                        load(n, ring[:, n % RING, :].rearrange("p (k n) -> p k n", k=4),
                             src.rearrange("(k p) n -> p k n", p=P))
                        n += 1

            for m in MODS[:2]:
                load_mod(m)
            for b in WIN:
                load(n, ring[:, n % RING, :].rearrange("p (k n) -> p k n", k=KT),
                     w_in[0, :, 256 * b:256 * (b + 1)].rearrange("(k p) n -> p k n", p=P))
                n += 1
            for m in MODS[2:5]:
                load_mod(m)
            for r in WOUT:
                load(n, ring[:, n % RING, :].rearrange("p (k n) -> p k n", k=2),
                     w_out[0, 256 * r:256 * (r + 1), :].rearrange("(k p) n -> p k n", p=P))
                n += 1
            load_mod(MODS[5])
            assert n == AT_MOE

            def load_expert(e, count):
                for cidx in range(RING):
                    w = (w_gate, w_up, w_down)[cidx // 4]
                    sp.wait_ge(chunks_used, used(cidx - RING, count))
                    sp.dma_start(ring[:, expert_slot(cidx), :].rearrange("p (k n) -> p k n", k=2),
                                 w[0, bass.ds(e, 1), 256 * (cidx % 4):256 * (cidx % 4 + 1), :]
                                 .rearrange("a (k p) n -> p (a k) n", p=P)).then_inc(slot_loaded[expert_slot(cidx)], 16)

            with sp.Fori(0, NE) as e:
                load_expert(e, e)
            sp.wait_ge(ev("over_list"), 1)
            n_over = sp.value_load(small_i[0:1, 16:17], min_val=0, max_val=MAX_OVER)
            with sp.If(n_over > 0):
                with sp.Fori(0, MAX_OVER) as j:
                    with sp.If(n_over > j):
                        e = sp.value_load(small_i[0:1, bass.ds(j, 1)], min_val=0, max_val=NE - 1)
                        load_expert(e, j + NE)

            for t in range(2):
                sp.wait_ge(ev("y_ready"), t + 1)
                sp.dma_start(halves(y_prompt[0])[t], xres[0:HALF, t, :]).then_inc(ev("y_stored"), 16)
                sp.dma_start(halves(y_sample[0])[t], xres[HALF:P, t, :]).then_inc(ev("y_stored"), 16)
            sp.wait_ge(ev("y_stored"), 64)

        @block.gpsimd
        def _(pool):
            nc.gpsimd.memset(condT, 0.0).then_inc(ev("cols_set"), 1)
            nc.gpsimd.memset(ones, 1.0).then_inc(ev("cols_set"), 1)
            nc.gpsimd.memset(eps, EPS).then_inc(ev("cols_set"), 1)
            nc.gpsimd.memset(zcol, 0.0).then_inc(ev("cols_set"), 1)

            def small_load(name, dst, src):
                pool.dma_start(dst, src).then_inc(ev(name), 16)

            pool.wait_ge(chunks_used, 1)
            small_load("masks_loaded", k_pool, const_masks)
            small_load("early_loaded", ck, cache_k.rearrange("b l s h d -> (b l s) (h d)"))
            small_load("early_loaded", ws, gmlp_ws[0].rearrange("g t s -> t g s"))
            small_load("early_loaded", gb_rows, gmlp_b[0])
            for qr in range(2):
                for kr in range(2):
                    off = (NA_KH - 1 + kr - qr) * (2 * NA_KW - 1) + NA_KW - GRID_W
                    src = bass.AP(tensor=na_rel_bias.tensor, offset=na_rel_bias.offset + off,
                                  ap=[[1, GRID_W], [(2 * NA_KH - 1) * (2 * NA_KW - 1), NH], [1, GRID_W]])
                    small_load("bias_raw_loaded", bias_raw[64 * (1 - qr):64 * (2 - qr), :, 64 * kr:64 * (kr + 1)], src)
            small_load("mixer_loaded", cv, cache_v.rearrange("b l s h d -> (b l s) (h d)"))
            for d, src in enumerate((state_hgrn_fwd, state_hgrn_bwd)):
                small_load("mixer_loaded", s0[:, d], src[0, 0].rearrange("(h q) k v -> (q k) h v", q=2))
            small_load("mixer_loaded", vng, bcast_row(gmlp_vnorm_g[0:1, :]))
            small_load("mixer_loaded", ong, bcast_row(hgrn_onorm_g[0:1, :]))
            small_load("mixer_loaded", rw, router_w[0].rearrange("(k p) e -> p k e", p=P))
            small_load("mixer_loaded", rbias, router_b)
            small_load("mixer_loaded", g1, bcast_row(b_mod[0:1, 2 * D:3 * D]))
            small_load("mixer_loaded", g2, bcast_row(b_mod[0:1, 5 * D:6 * D]))
            pool.wait_ge(ev("masks_ready"), 1)
            nc.gpsimd.memset(Kl, 0.0).then_inc(ev("k_zero"), 1)
            pool.wait_ge(ev("h_ready"), 2)
            small_load("norm2_loaded", gain, bcast_row(norm2_g[0:1, :]))
            small_load("norm2_loaded", gsc, bcast_row(b_mod[0:1, 4 * D:5 * D]))
            small_load("norm2_loaded", shf, bcast_row(b_mod[0:1, 3 * D:4 * D]))

            pool.wait_ge(ev("kout_ready"), 1)
            pool.dma_start(new_k.rearrange("b l s (g h) d -> (b l s) g (h d)", g=2), kout).then_inc(ev("kout_stored"), 16)
            pool.wait_ge(ev("win_out"), V_1 + 1)
            pool.dma_start(new_v.rearrange("b l s h d -> (b l s) (h d)"), v[:, 0, :]).then_inc(ev("caches_stored"), 16)
            pool.wait_ge(ev("state_ready"), 1)
            for d, out in enumerate((new_sf, new_sb)):
                pool.dma_start(out.rearrange("b l h k v -> k (b l h) v"),
                               state_out[0:HD, 256 * d:256 * (d + 1)].rearrange("k (h v) -> k h v", h=RH)).then_inc(ev("caches_stored"), 16)
            nc.gpsimd.memset(identE, 0.0).then_inc(ev("idE_zero"), 1)
            pool.wait_ge(ev("idE_zero"), 1)
            nc.gpsimd.affine_select(out=identE, in_=identE, compare_op=ALU.not_equal, fill=1.0, base=0,
                                    pattern=[[-1, NE + 1]], channel_multiplier=1).then_inc(ev("idE_ready"), 1)
            pool.wait_ge(ev("mod_out"), 8)
            small_load("gain3_loaded", gain, bcast_row(final_g.rearrange("(a d) -> a d", a=1)))
            pool.wait_ge(ev("kout_stored"), 16)
            pool.wait_ge(ev("caches_stored"), 48)
            pool.wait_ge(ev("cat_ps"), 4)
            for m, src in enumerate((b_gate, b_up, b_down)):
                small_load("mbias_loaded", mbias[:, m, :], src[0])
            pool.wait_ge(ev("mbias_loaded"), 48)
            pool.wait_ge(ev("gain3_loaded"), 16)

        @block.scalar
        def _(act):
            def small_load(name, dst, src, **kw):
                act.dma_start(dst, src, **kw).then_inc(ev(name), 16)

            small_load("consts_loaded", cst, const_f32)
            small_load("consts_loaded", gsc, bcast_row(b_mod[0:1, D:2 * D]))
            small_load("consts_loaded", shf, bcast_row(b_mod[0:1, 0:D]))
            small_load("consts_loaded", gain, bcast_row(norm1_g[0:1, :]))
            for t in range(2):
                small_load("x_loaded", xres[0:HALF, t, :], halves(x_prompt[0])[t])
                small_load("x_loaded", xres[HALF:P, t, :], halves(x_sample[0])[t])
            small_load("lb_loaded", lb_t[:, 0:4], hgrn_lb.rearrange("d l (h p) -> p (d l h)", p=P),
                       allow_slow_non_contiguous=True)
            act.wait_ge(ev("cond_loaded"), 32)
            nc.scalar.activation(gtmp[0:16, 0:P], cond, ACT.Sigmoid).then_inc(ev("cond_sig"), 1)

            act.wait_ge(ev("x_loaded"), 64)
            for t in range(2):
                nc.scalar.activation(rows[:, t, :], xres[:, t, :], ACT.Square, accum_out=ss[:, t:t + 1]).then_inc(ev("ss1"), 1)
            act.wait_ge(ev("ss1"), 2)
            act.wait_ge(ev("cols_set"), 4)
            nc.scalar.activation(rstd, ss, ACT.Sqrt, bias=eps, scale=1.0 / D).then_inc(ev("rms1"), 1)
            act.wait_ge(ev("lb_shift"), 1)
            nc.scalar.activation(lb_t[:, 0:4], lb_t[:, 4:8], ACT.Exp).then_inc(ev("lb_exp"), 1)

            for t, q in ((0, 0), (0, 1), (1, 0)):
                act.wait_ge(ev("hT_ps"), 2 * t + q + 1)
                nc.scalar.copy(hT[:, 4 * q:4 * q + 4, :, HALF * t:HALF * (t + 1)],
                               B[4 + 2 * t + q].rearrange("p (k g u) -> p k g u", k=4, g=G)).then_inc(ev("hT_ready"), 1)

            def win_wait(i):
                act.wait_ge(chunks_used, AT_WIN + i + 1)

            for d, i in enumerate((Z_F, Z_B)):
                win_wait(i)
                if d == 0:
                    act.wait_ge(ev("cond_silu"), 1)
                nc.scalar.activation(sig[:, d, :], B[i % 2], ACT.Sigmoid).then_inc(ev("sig_z"), 1)
                nc.scalar.activation(keyT[:, d, :], B[i % 2], ACT.Sigmoid, scale=-1.0).then_inc(ev("win_out"), 1)
            win_wait(H_Q)
            nc.scalar.copy(hqT, B[H_Q % 2]).then_inc(ev("win_out"), 1)
            act.wait_ge(ev("f_parts"), 1)
            nc.scalar.activation(cumT, cumT, ACT.Ln).then_inc(ev("ln_parts"), 1)
            nc.scalar.activation(sig, sig, ACT.Ln, scale=2.0 ** LN_SPLIT).then_inc(ev("ln_parts"), 1)
            win_wait(H_I)
            nc.scalar.copy(hi.rearrange("p g n -> p (g n)"), B[H_I % 2]).then_inc(ev("win_out"), 1)

            def copy_win(i):
                win_wait(i)
                if i in (K_0, Q_0, K_1, Q_1):
                    dst = (kT if i in (K_0, K_1) else qT)[:, 2 * (i >= K_1):2 * (i >= K_1) + 2]
                    nc.scalar.copy(dst, B[i % 2].rearrange("p (h g t) -> p h g t", h=2, g=G)).then_inc(ev("win_out"), 1)
                else:
                    dst = v[:, :, 256 * (i - V_0):256 * (i - V_0 + 1)]
                    nc.scalar.copy(dst, B[i % 2].rearrange("p (g n) -> p g n", g=G)).then_inc(ev("win_out"), 1)

            def level_exp(n):
                act.wait_ge(ev("lvl_diff"), n + 1)
                for d in range(2):
                    x = level_view(Dl[:, d, :], LEVELS[n])
                    for h in range(2):
                        query = h == 1 - d
                        nc.scalar.activation(x[:, :, h, :], x[:, :, h, :], ACT.Exp,
                                             scale=1.0 if query else -1.0).then_inc(ev("lvl_exp"), 1)

            copy_win(K_0)
            copy_win(Q_0)
            level_exp(0)
            copy_win(K_1)
            level_exp(1)
            copy_win(Q_1)
            act.wait_ge(ev("kout_ps"), 1)
            nc.scalar.copy(kout, B[6].rearrange("p (g n) -> p g n", g=2)).then_inc(ev("kout_ready"), 1)
            level_exp(2)
            copy_win(V_0)
            act.wait_ge(ev("nmx_p"), 1)
            for q in range(2):
                for h in range(HP):
                    n = HP * q + h
                    nc.scalar.activation(probs_p[:, q, h, :], B[4 + q][:, P * h:P * (h + 1)], ACT.Exp, scale=SCALE,
                                         bias=nmx[:, n:n + 1], accum_out=rsum[:, n:n + 1]).then_inc(ev("exp_p"), 1)
            level_exp(3)
            copy_win(V_1)
            level_exp(4)
            win_wait(G_V)
            gv = B[G_V % 2].rearrange("p (g n) -> p g n", g=G)
            nc.scalar.copy(rows[:, :, 768:1024], gv).then_inc(ev("gv_out"), 1)
            act.wait_ge(ev("gv_out"), 1)
            for g in range(G):
                nc.scalar.activation(gv[:, g, :], gv[:, g, :], ACT.Square, accum_out=ssg[:, g:g + 1]).then_inc(ev("ssg"), 1)
            act.wait_ge(ev("ssg"), 2)
            nc.scalar.activation(rsg, ssg, ACT.Sqrt, bias=eps, scale=1.0 / (GM * HD)).then_inc(ev("rmsg"), 1)
            for q in range(2):
                act.wait_ge(ev("pT_ps"), q + 1)
                nc.scalar.copy(pT_p[:, q, :], B[6 + q]).then_inc(ev("pT_ready"), 1)
            level_exp(5)
            level_exp(6)
            act.wait_ge(ev("end_diff"), 2)
            nc.scalar.activation(Dk, Dk, ACT.Exp, scale=-1.0).then_inc(ev("end_exp"), 1)
            for d in range(2):
                nc.scalar.activation(Dq[:, d], cum4[:, d, :, 1, :], ACT.Exp).then_inc(ev("end_exp"), 1)
            win_wait(H_G)
            nc.scalar.activation(gtmp, B[H_G % 2], ACT.Sigmoid).then_inc(ev("sig_g"), 1)

            act.wait_ge(ev("kst_ps"), 1)
            nc.scalar.copy(kstT.rearrange("p d h k -> p (d h k)"), B[1]).then_inc(ev("kst_ready"), 1)
            act.wait_ge(ev("score_s"), 1)
            for q in range(2):
                nc.scalar.mul(probs[:, q:NH:2, P:2 * P], B[6 + q].rearrange("p (h k) -> p h k", h=HP), SCALE).then_inc(ev("ctx_sc"), 1)
            act.wait_ge(ev("state_ps"), 1)
            nc.scalar.copy(state_out[0:HD, :], B[0][0:HD, :]).then_inc(ev("state_ready"), 1)
            act.wait_ge(ev("nmx_s"), 1)
            for h in range(NH):
                nc.scalar.activation(probs[:, h, :], probs[:, h, :], ACT.Exp, bias=nmx_s[:, h:h + 1],
                                     accum_out=rsum_s[:, h:h + 1]).then_inc(ev("exp_s"), 1)
            act.wait_ge(ev("ms_o"), 1)
            nc.scalar.activation(rso, sso, ACT.Sqrt).then_inc(ev("rms_o"), 1)

            def cat_out(n, bank):
                g, kh = n % 2, 1 - n // 2
                act.wait_ge(ev("cat_ps"), n + 1)
                nc.scalar.copy(catT[:, 4 * kh:4 * kh + 4, :, HALF * g:HALF * (g + 1)],
                               B[bank].rearrange("p (k t u) -> p k t u", k=4, t=2)).then_inc(ev("catT_ready"), 1)

            def probs_out(q):
                act.wait_ge(ev("sT_ps"), q + 1)
                dst = (sT_lo if q < 2 else sT_hi)[:, 512 * (q % 2):512 * (q % 2 + 1)]
                nc.scalar.copy(dst, B[4 + q % 2]).then_inc(ev("sT_ready"), 1)

            cat_out(0, 6)
            cat_out(1, 7)
            for q in range(4):
                probs_out(q)
            cat_out(2, 7)
            cat_out(3, 5)

            for t in range(2):
                act.wait_ge(ev("x1_ready"), 2 * t + 2)
                nc.scalar.activation(k_pool[:, D * t:D * (t + 1)], xres[:, t, :], ACT.Square, accum_out=ss2[:, t:t + 1]).then_inc(ev("ss2"), 1)
                act.wait_ge(ev("ss2"), t + 1)
                nc.scalar.activation(rs2[:, t:t + 1], ss2[:, t:t + 1], ACT.Sqrt, bias=eps, scale=1.0 / D).then_inc(ev("rms2"), 1)
            for t in range(2):
                for q in range(2):
                    act.wait_ge(ev("h2T_ps"), 2 * t + q + 1)
                    nc.scalar.copy(h2T[:, 4 * q:4 * q + 4, t, :],
                                   B[2 + q].rearrange("p (k u) -> p k u", k=4)).then_inc(ev("h2T_ready"), 1)
            act.wait_ge(ev("nv1"), 1)
            for t in range(2):
                nc.scalar.activation(ex[:, t, :], lg[:, t, :], ACT.Exp, bias=rsm[:, 16 + t:17 + t]).then_inc(ev("r_exp"), 1)
            act.wait_ge(ev("rgT_ps"), 1)
            nc.scalar.copy(rgT, B[1][0:NE, :]).then_inc(ev("rgT_ready"), 1)

            def tokens_out(count):
                act.wait_ge(ev("xe_ps"), count + 1)
                nc.scalar.copy(xe.rearrange("p k s -> p (k s)"), B[3]).then_inc(ev("xe_ready"), 1)

            def sigmoid_step(count):
                act.wait_ge(ev("gate_min"), count + 1)
                nc.scalar.activation(sigb, actb, ACT.Sigmoid, scale=ALPHA).then_inc(ev("gate_sig"), 1)

            def down_steps(count):
                act.wait_ge(ev("aT_ps"), count + 1)
                nc.scalar.copy(aT.rearrange("p c s -> p (c s)"), B[2]).then_inc(ev("aT_ready"), 1)
                act.wait_ge(chunks_used, used(11, count))
                nc.scalar.copy(ysb, B[2]).then_inc(ev("y_sb"), 1)

            act.wait_ge(ev("mixer_freed"), 1)
            tokens_out(0)
            with act.Fori(0, NE) as e:
                sigmoid_step(e)
                tokens_out(e + 1)
                down_steps(e)
            act.wait_ge(ev("over_list"), 1)
            n_over = act.value_load(small_i[0:1, 16:17], min_val=0, max_val=MAX_OVER)
            with act.If(n_over > 0):
                with act.Fori(0, MAX_OVER) as j:
                    with act.If(n_over > j):
                        tokens_out(j + (NE + 1))
                        sigmoid_step(j + NE)
                        down_steps(j + NE)

            nc.scalar.activation(rsf[:, 0:1], eps, ACT.Sqrt).then_inc(ev("root_table"), 1)
            act.wait_ge(ev("root_table"), 1)
            for t in range(2):
                act.wait_ge(ev("x2_ready"), 2 * t + 2)
                nc.scalar.activation(rows[:, t, :], xres[:, t, :], ACT.Square, accum_out=ssf[:, t:t + 1]).then_inc(ev("ssf"), 1)
                act.wait_ge(ev("ssf"), t + 1)
                nc.scalar.activation(rsf[:, t:t + 1], ssf[:, t:t + 1], ACT.Sqrt, bias=eps, scale=1.0 / D).then_inc(ev("rmsf"), 1)

        @block.vector
        def _(dve):
            ch = Chain(dve, "dve_steps")
            V = nc.vector

            dve.wait_ge(ev("cond_sig"), 1)
            V.tensor_tensor(cond, cond, gtmp[0:16, 0:P], ALU.mult).then_inc(ev("cond_silu"), 1)
            dve.wait_ge(ev("consts_loaded"), 64)
            V.tensor_copy(flip, ident[:, ::-1]).then_inc(ev("flip_ready"), 1)
            dve.wait_ge(ev("condT_ps"), 1)
            dve.wait_ge(ev("cols_set"), 4)
            V.tensor_copy(condT[:, :, 0:G], B[4][:, 0:16].rearrange("p (r k) -> p k r", r=G)).then_inc(ev("condT_ready"), 1)

            def mod_part(n):
                dve.wait_ge(chunks_used, mod_at(n) + 2)
                if n >= 2:
                    dve.wait_ge(ev("mod_bc"), n - 1)
                V.tensor_copy(part[n % 2], B[mod_bank(n)]).then_inc(ev("mod_part"), 1)

            def mod_out(n):
                dve.wait_ge(ev("mod_bc"), n + 1)
                m, cols = MODS[n // 2], slice(512 * (n % 2), 512 * (n % 2 + 1))
                src = B[bc_bank(n)]
                if m in (1, 4):
                    ch.step(V.scalar_tensor_tensor(gsc[:, cols], src, 1.0, gsc[:, cols], ALU.add, ALU.add))
                    V.tensor_tensor(gsc[:, cols], gsc[:, cols], gain[:, cols], ALU.mult).then_inc(ev("mod_out"), 1)
                else:
                    dst = {0: shf, 3: shf, 2: g1, 5: g2}[m]
                    V.tensor_tensor(dst[:, cols], src, dst[:, cols], ALU.add).then_inc(ev("mod_out"), 1)

            dve.wait_ge(ev("lb_loaded"), 16)
            ch.step(V.tensor_tensor(lb_t[:, 4:8], lb_t[:, 0:4], lb_t[:, 0:4], ALU.max))
            V.tensor_tensor(lb_t[:, 4:8], lb_t[:, 0:4], lb_t[:, 4:8], ALU.subtract).then_inc(ev("lb_shift"), 1)

            mod_part(0)
            mod_part(1)
            mod_out(0)
            dve.wait_ge(ev("rms1"), 1)
            ch.step(V.reciprocal(rstd, rstd))
            mod_part(2)
            mod_out(1)
            dve.wait_ge(ev("mod_out"), 2)
            ch.step(V.scalar_tensor_tensor(rows[:, 0, :], xres[:, 0, :], rstd[:, 0:1], gsc, ALU.mult, ALU.mult))
            mod_part(3)
            mod_out(2)
            V.scalar_tensor_tensor(rows[:, 1, :], xres[:, 1, :], rstd[:, 1:2], gsc, ALU.mult, ALU.mult).then_inc(ev("h_scaled"), 1)
            mod_out(3)
            dve.wait_ge(ev("mod_out"), 4)
            dve.wait_ge(ev("h_scaled"), 1)
            for t in range(2):
                V.tensor_tensor(rows[:, t, :], rows[:, t, :], shf, ALU.add).then_inc(ev("h_ready"), 1)

            dve.wait_ge(ev("lb_exp"), 1)
            ch.step(V.reciprocal(lb_t[:, 4:8], lb_t[:, 0:4]))
            ch.step(V.tensor_tensor(lb_t[:, 4:8], lb_t[:, 0:4], lb_t[:, 4:8], ALU.mult))
            ch.step(V.tensor_tensor(lbT, lb_t[:, 4:8], lb_t[:, 4:8], ALU.subtract))
            ch.step(V.tensor_scalar(omlT, lbT, -1.0, 1.0, ALU.mult, ALU.add))
            dve.wait_ge(ev("hT_ps"), 4)
            V.tensor_copy(hT[:, 4:8, :, HALF:P], B[7].rearrange("p (k g u) -> p k g u", k=4, g=G)).then_inc(ev("hT_ready"), 1)
            dve.wait_ge(ev("masks_loaded"), 16)
            V.tensor_copy(masks.rearrange("p m t -> p (m t)"), k_pool).then_inc(ev("masks_ready"), 1)
            V.memset(biasN, NEG).then_inc(ev("biasN_neg"), 1)

            for d in range(2):
                dve.wait_ge(ev("win_out"), d + 1)
                dve.wait_ge(ev("sig_z"), d + 1)
                for h in range(RP):
                    n, cols = 2 * d + h, slice(256 * h, 256 * (h + 1))
                    V.tensor_scalar(sig[:, d, cols], sig[:, d, cols], omlT[:, n:n + 1], lbT[:, n:n + 1],
                                    ALU.mult, ALU.add).then_inc(ev("f_ready"), 1)
                    V.tensor_scalar(keyT[:, d, cols], keyT[:, d, cols], omlT[:, n:n + 1], None, ALU.mult).then_inc(ev("key_ready"), 1)
            dve.wait_ge(ev("f_ready"), 4)
            ch.step(V.tensor_scalar(cumT, sig, 2.0 ** -LN_SPLIT, None, ALU.max))
            V.tensor_scalar(sig, sig, F_FLOOR, 2.0 ** -LN_SPLIT, ALU.max, ALU.min).then_inc(ev("f_parts"), 1)
            dve.wait_ge(ev("early_ps"), 3)
            V.tensor_copy(ckT.rearrange("p h l -> p (h l)"), B[6]).then_inc(ev("early_out"), 1)
            V.tensor_copy(wsT.rearrange("p g t -> p (g t)"), B[7]).then_inc(ev("early_out"), 1)
            V.tensor_copy(gbT, B[2][:, 0:GM]).then_inc(ev("early_out"), 1)
            dve.wait_ge(ev("flip_ps"), 1)
            dve.wait_ge(ev("masks_ready"), 1)
            dve.wait_ge(ev("biasN_neg"), 1)
            for q in range(2):
                V.copy_predicated(biasN[:, HP * q:HP * (q + 1), :], masks[:, M_WINDOW, :].unsqueeze(1).to_broadcast([P, HP, P]),
                                  B[4 + q].rearrange("p (h k) -> p h k", h=HP)).then_inc(ev("biasN_ready"), 1)
            ch.step(V.memset(Dl[:, 0, :], 1.0))
            ch.step(V.memset(Dl[:, 0, 0:512:P], 0.0))
            dve.wait_ge(ev("ln_parts"), 2)
            ch.step(V.tensor_tensor(sig, sig, cumT, ALU.add))
            V.tensor_tensor_scan(cumT[:, 0, :], Dl[:, 0, :], sig[:, 0, :], 0.0, ALU.mult, ALU.add).then_inc(ev("scan_done"), 1)
            V.tensor_tensor_scan(cumT[:, 1, ::-1], Dl[:, 0, :], sig[:, 1, ::-1], 0.0, ALU.mult, ALU.add).then_inc(ev("scan_done"), 1)
            dve.wait_ge(ev("key_ready"), 4)
            dve.wait_ge(ev("k_zero"), 1)
            V.tensor_tensor(Kl[:, 0, :], keyT[:, 0, :], keyT[:, 1, :], ALU.add).then_inc(ev("ksum_ready"), 1)
            dve.wait_ge(ev("scan_done"), 2)

            def level_diff(n):
                w = LEVELS[n]
                for d in range(2):
                    b = cumT[:, d, :].rearrange("p (n m) -> p n m", m=2 * w)
                    edge = b[:, :, w - 1:w] if d == 0 else b[:, :, w:w + 1]
                    ins = V.tensor_tensor(Dl[:, d, :].rearrange("p (n m) -> p n m", m=2 * w), b,
                                          edge.to_broadcast([P, 256 // w, 2 * w]), ALU.subtract)
                ins.then_inc(ev("lvl_diff"), 1)

            def level_qk(n):
                w = LEVELS[n]
                dve.wait_ge(ev("lvl_exp"), 4 * (n + 1))
                dve.wait_ge(ev("lvl_mm"), n + 1)
                for d in range(2):
                    ex_ = level_view(Dl[:, d, :], w)
                    qh = 1 - d
                    V.tensor_tensor(Qc[:, d, :].rearrange("p (n m) -> p n m", m=w), ex_[:, :, qh, :],
                                    level_view(hqT, w)[:, :, qh, :], ALU.mult).then_inc(ev("lvl_qk"), 1)
                    V.tensor_tensor(level_view(Kl[:, d, :], w)[:, :, d, :], ex_[:, :, d, :],
                                    level_view(keyT[:, d, :], w)[:, :, d, :], ALU.mult).then_inc(ev("lvl_qk"), 1)

            def level_store(n):
                dve.wait_ge(ev("lvl_mm"), n + 2)
                if n < 0:
                    for q in range(2):
                        V.tensor_copy(AT[:, q, :], B[2 + q]).then_inc(ev("lvl_store"), 1)
                    return
                w = LEVELS[n]
                for d in range(2):
                    dve.wait_ge(ev("lvl_store"), 4 * n + 2 * d + 2)
                    for q in range(2):
                        V.copy_predicated(AT[:, q, :].rearrange("p (a n h m) -> p a n h m", a=4, h=2, m=w)[:, :, :, 1 - d, :],
                                          level_view(masks[:, 7 * d + n, :], w)[:, :, 1 - d, :].unsqueeze(1).to_broadcast([P, 4, 64 // w, w]),
                                          B[2 + q][:, 256 * d:256 * (d + 1)].rearrange("p (a n m) -> p a n m", a=4, m=w)).then_inc(ev("lvl_store"), 1)

            level_diff(0)
            for n in range(len(LEVELS)):
                level_qk(n)
                dve.wait_ge(ev("lvl_qk"), 4 * (n + 1))
                if n + 1 < len(LEVELS):
                    level_diff(n + 1)
                else:
                    for d in range(2):
                        edge = cum4[:, d, :, 0, P - 1:P] if d == 0 else cum4[:, d, :, 0, 0:1]
                        V.tensor_tensor(Dk[:, d], cum4[:, d, :, 0, :], edge.to_broadcast([P, RP, P]), ALU.subtract).then_inc(ev("end_diff"), 1)
                level_store(n - 1)
                if n == 2:
                    dve.wait_ge(ev("score_p"), 1)
                    for q in range(2):
                        V.tensor_reduce(mx[:, HP * q:HP * (q + 1)], B[4 + q].rearrange("p (h k) -> p h k", h=HP), AX.X, ALU.max).then_inc(ev("mx_p"), 1)
                    dve.wait_ge(ev("mx_p"), 2)
                    V.tensor_scalar(nmx, mx, -SCALE, None, ALU.mult).then_inc(ev("nmx_p"), 1)
                if n == 4:
                    dve.wait_ge(ev("exp_p"), NH)
                    ch.step(V.reciprocal(rinv, rsum))
                if n == 5:
                    dve.wait_ge(ev("rmsg"), 1)
                    ch.step(V.reciprocal(rsg, rsg))
                    dve.wait_ge(ev("mixer_loaded"), 144)
                    for g in range(G):
                        V.scalar_tensor_tensor(rows[:, g, 768:1024], rows[:, g, 768:1024], rsg[:, g:g + 1], vng,
                                               ALU.mult, ALU.mult).then_inc(ev("vg_ready"), 1)
                    dve.wait_ge(ev("att_p_ps"), 1)
                    V.tensor_tensor(rows[:, 0, 0:512].rearrange("p (h q d) -> p h q d", h=HP, q=2), B[4].rearrange("p (h q d) -> p h q d", h=HP, q=2),
                                    rinv.rearrange("p (q h) -> p h q", q=2).unsqueeze(3).to_broadcast([P, HP, 2, HD]), ALU.mult).then_inc(ev("att_p"), 1)
                    dve.wait_ge(ev("z_ps"), 1)
                    for g in range(GM):
                        V.tensor_scalar(rows[:, :, 768 + HD * g:768 + HD * (g + 1)], B[5][:, P * g:P * (g + 1)].rearrange("p (r n) -> p r n", r=G),
                                        gbT[:, g:g + 1], None, ALU.add).then_inc(ev("zb_ready"), 1)
                    dve.wait_ge(ev("zb_ready"), 4)
                    V.tensor_tensor(rows[:, :, 768:1024], rows[:, :, 768:1024], B[G_U % 2].rearrange("p (g n) -> p g n", g=G),
                                    ALU.mult).then_inc(ev("gmlp_ready"), 1)
            dve.wait_ge(ev("end_exp"), 3)
            dve.wait_ge(ev("lvl_mm"), 8)
            for d in range(2):
                V.tensor_tensor(Kend[:, d], Dk[:, d], key4[:, d, :, 0, :], ALU.mult).then_inc(ev("end_ready"), 1)
            for d in range(2):
                V.tensor_tensor(Qend[:, d], Dq[:, d], hq4[:, :, 1, :], ALU.mult).then_inc(ev("end_ready"), 1)
            level_store(6)
            dve.wait_ge(ev("score_s"), 1)
            dve.wait_ge(ev("kst_ps"), 1)
            dve.wait_ge(ev("biasN_ready"), 2)
            for q in range(2):
                V.scalar_tensor_tensor(probs[:, q:NH:2, 0:P], B[4 + q].rearrange("p (h k) -> p h k", h=HP), SCALE,
                                       biasN[:, q:NH:2, :], ALU.mult, ALU.add).then_inc(ev("local_sc"), 1)
            dve.wait_ge(ev("sig_g"), 1)
            dve.wait_ge(ev("kout_stored"), 16)
            V.tensor_tensor(rows[:, :, 512:768], gtmp.rearrange("p (g n) -> p g n", g=G),
                            B[H_G % 2].rearrange("p (g n) -> p g n", g=G), ALU.mult).then_inc(ev("silu_g"), 1)
            dve.wait_ge(ev("local_sc"), 2)
            dve.wait_ge(ev("ctx_sc"), 2)
            ch.step(V.tensor_reduce(mx_s, probs, AX.X, ALU.max))
            V.tensor_scalar(nmx_s, mx_s, -1.0, None, ALU.mult).then_inc(ev("nmx_s"), 1)

            dve.wait_ge(ev("o_ps"), 1)
            o_sb = gtmp.rearrange("p (g h n) -> p g h n", g=G, h=RH)
            dve.wait_ge(ev("silu_g"), 1)
            for q in range(2):
                src = B[2 + q].rearrange("p (g h n) -> p g h n", g=G, h=4)[:, :, 0:RP, :]
                V.tensor_copy(o_sb[:, :, q:RH:2, :], src).then_inc(ev("o_out"), 1)
            dve.wait_ge(ev("o_out"), 2)
            o_rows = gtmp.rearrange("p (n v) -> p n v", v=HD)
            o_sq = keyT[:, 0, :].rearrange("p (n v) -> p n v", v=HD)
            ch.step(V.tensor_tensor(o_sq, o_rows, o_rows, ALU.mult))
            ch.step(V.tensor_reduce(sso, o_sq, AX.X, ALU.add))
            V.tensor_scalar(sso, sso, 1.0 / HD, EPS, ALU.mult, ALU.add).then_inc(ev("ms_o"), 1)
            mod_part(4)
            mod_out(4)
            mod_part(5)
            mod_out(5)
            dve.wait_ge(ev("norm2_loaded"), 48)
            mod_part(6)
            dve.wait_ge(ev("rms_o"), 1)
            ch.step(V.reciprocal(rso, rso))
            ch.step(V.tensor_tensor(o_rows, o_rows, rso.unsqueeze(2).to_broadcast([P, 8, HD]), ALU.mult))
            ch.step(V.tensor_tensor(o_rows, o_rows, ong.unsqueeze(1).to_broadcast([P, 8, HD]), ALU.mult))
            V.tensor_tensor(rows[:, :, 512:768], rows[:, :, 512:768], gtmp.rearrange("p (g n) -> p g n", g=G),
                            ALU.mult).then_inc(ev("hgrn_ready"), 1)
            mod_out(6)
            mod_part(7)
            mod_out(7)
            dve.wait_ge(ev("exp_s"), NH)
            ch.step(V.reciprocal(rinv_s, rsum_s))
            for n in (8, 9):
                mod_part(n)
                mod_out(n)
            dve.wait_ge(ev("att_s_ps"), 1)
            V.tensor_tensor(rows[:, 1, 0:512].rearrange("p (h d) -> p h d", h=NH), B[6].rearrange("p (h d) -> p h d", h=NH),
                            rinv_s.unsqueeze(2).to_broadcast([P, NH, HD]), ALU.mult).then_inc(ev("att_s"), 1)

            dve.wait_ge(ev("caches_stored"), 48)
            for t in range(2):
                if t == 0:
                    dve.wait_ge(ev("wout_ps"), 1)
                else:
                    dve.wait_ge(chunks_used, AT_MODG2)
                for half in range(2):
                    cols = slice(512 * half, 512 * (half + 1))
                    ch.step(V.tensor_tensor(xtmp[half], B[2 * t + half], g1[:, cols], ALU.mult))
                    V.tensor_tensor(xres[:, t, cols], xres[:, t, cols], xtmp[half], ALU.add).then_inc(ev("x1_ready"), 1)
            dve.wait_ge(ev("mod_out"), 10)
            for t in range(2):
                dve.wait_ge(ev("rms2"), t + 1)
                ch.step(V.reciprocal(rs2[:, t:t + 1], rs2[:, t:t + 1]))
                ch.step(V.scalar_tensor_tensor(rows[:, t, :], xres[:, t, :], rs2[:, t:t + 1], gsc, ALU.mult, ALU.mult))
                V.tensor_tensor(rows[:, t, :], rows[:, t, :], shf, ALU.add).then_inc(ev("h2_ready"), 1)
            for n in (10, 11):
                mod_part(n)
                mod_out(n)
            V.memset(rank, 0.0).then_inc(ev("rank_zero"), 1)
            V.memset(csm, 1.0).then_inc(ev("csm_set"), 1)
            dve.wait_ge(ev("csm_set"), 1)
            ch.step(V.memset(csm[:, 1, 0:1], 0.0))
            V.memset(gT[:, 1, :], 0.0).then_inc(ev("mixer_freed"), 1)
            V.memset(ysb, 0.0).then_inc(ev("y_sb"), 1)

            both = [P, 2, NE]
            dve.wait_ge(ev("logits_ps"), 1)
            logits = B[0][:, 0:2 * NE].rearrange("p (t e) -> p t e", t=2)
            V.tensor_copy(lg, logits).then_inc(ev("lg_ready"), 1)
            for t in range(2):
                V.max(rsm[:, 8 * t:8 * t + 8], logits[:, t, :]).then_inc(ev("lg_ready"), 1)
            dve.wait_ge(ev("lg_ready"), 3)
            V.tensor_scalar(rsm[:, 16:18], rsm[:, 0:16:8], -1.0, None, ALU.mult).then_inc(ev("nv1"), 1)
            v4 = rsm[:, 3:16:8].unsqueeze(2).to_broadcast(both)
            ch.step(V.tensor_tensor(eqm, lg, v4, ALU.is_equal))
            ch.step(V.tensor_tensor(msk, lg, v4, ALU.is_gt))
            V.tensor_tensor_scan(mask4[:, 0, 0:2, :].rearrange("p r e -> p (r e)"), csm.rearrange("p t e -> p (t e)"),
                                 eqm.rearrange("p t e -> p (t e)"), 0.0, ALU.mult, ALU.add).then_inc(ev("ties"), 1)
            ch.step(V.tensor_reduce(rsm[:, 18:20], msk, AX.X, ALU.add))
            dve.wait_ge(ev("ties"), 1)
            ch.step(V.tensor_tensor(csm, mask4[:, 0, 0:2, :], rsm[:, 18:20].unsqueeze(2).to_broadcast(both), ALU.add))
            ch.step(V.scalar_tensor_tensor(eqm, csm, float(TOP_K), eqm, ALU.is_le, ALU.mult))
            ch.step(V.tensor_tensor(msk, msk, eqm, ALU.add))
            V.tensor_copy(mask4, msk.unsqueeze(2).to_broadcast([P, 2, CHUNKS, NE])).then_inc(ev("mask_ready"), 1)
            dve.wait_ge(ev("r_exp"), 2)
            ch.step(V.tensor_tensor(ex, ex, msk, ALU.mult))
            ch.step(V.tensor_reduce(rsm[:, 22:24], ex, AX.X, ALU.add))
            ch.step(V.reciprocal(rsm[:, 24:26], rsm[:, 22:24]))
            V.tensor_tensor(gate, ex, rsm[:, 24:26].unsqueeze(2).to_broadcast(both), ALU.mult).then_inc(ev("gate_ready"), 1)
            dve.wait_ge(ev("rank_zero"), 1)
            dve.wait_ge(ev("rank_ps"), 1)
            V.tensor_tensor(rank[:, :, 0:NE], B[1][:, 0:2 * NE].rearrange("p (t e) -> p t e", t=2), msk, ALU.mult).then_inc(ev("rank_ready"), 1)
            V.tensor_tensor(flag, B[1][:, 64:65], cst[:, C_THR:C_THR + 1], ALU.is_gt).then_inc(ev("flag_ready"), 1)

            def route(e, buf, off=None):
                V.tensor_copy(pick[:, buf, :], identE[:, bass.ds(e, 1)].to_broadcast([NE, P]))
                for t in range(2):
                    r = rank[:, t, bass.ds(e, 1)]
                    if off is None:
                        ins = V.tensor_scalar(Ptok[:, t, :], cst[:, C_SLOTROW:C_SLOTROW + CAP], r, None, ALU.is_equal)
                    else:
                        ins = V.tensor_scalar(Ptok[:, t, :], cst[:, C_SLOTROW:C_SLOTROW + CAP], off, r, ALU.add, ALU.is_equal)
                ins.then_inc(ev("route_ready"), 1)

            def slot_gates(count, buf, off=None):
                dve.wait_ge(ev("bc_ps"), count + 1)
                scol = cst[:, C_SLOTCOL:C_SLOTCOL + 1]
                if off is None:
                    ch.step(V.tensor_scalar(gT[:, buf, :], B[3][:, 0:256], scol, None, ALU.is_equal))
                else:
                    ch.step(V.tensor_scalar(gT[:, buf, :], B[3][:, 0:256], off, scol, ALU.subtract, ALU.is_equal))
                V.tensor_tensor(gT[:, buf, :], gT[:, buf, :], B[3][:, 256:512], ALU.mult).then_inc(ev("gT_ready"), 1)

            def gate_step(count):
                dve.wait_ge(chunks_used, used(3, count))
                V.tensor_scalar(actb, B[0], LIMIT, None, ALU.min).then_inc(ev("gate_min"), 1)

            def up_step(count):
                dve.wait_ge(chunks_used, used(7, count))
                V.tensor_scalar(upb, B[1], -LIMIT, LIMIT, ALU.max, ALU.min).then_inc(ev("up_clip"), 1)
                dve.wait_ge(ev("up_clip"), count + 1)
                ch.step(V.scalar_tensor_tensor(upb, upb, 1.0, actb, ALU.add, ALU.mult))
                dve.wait_ge(ev("gate_sig"), count + 1)
                V.tensor_tensor(ab, upb, sigb, ALU.mult).then_inc(ev("a_ready"), 1)

            dve.wait_ge(ev("idE_ready"), 1)
            dve.wait_ge(ev("rank_ready"), 1)
            route(0, 0)
            dve.wait_ge(ev("pos_ps"), 1)
            dve.wait_ge(ev("flag_ready"), 1)
            ch.step(V.tensor_copy(posn, B[0][:, 64:65]))
            V.tensor_scalar(onehot, cst[:, C_IOTA:C_IOTA + 16], posn, flag, ALU.is_equal, ALU.mult).then_inc(ev("onehot_ready"), 1)
            slot_gates(0, 0)
            dve.wait_ge(ev("list_ps"), 1)
            V.tensor_copy(offb, B[0][:, 128:144]).then_inc(ev("offb_ready"), 1)
            ch.step(V.tensor_copy(small_i[0:1, 0:16], B[0][0:1, 144:160]))
            V.tensor_copy(small_i[0:1, 16:17], B[0][0:1, 160:161]).then_inc(ev("over_list"), 1)
            with dve.Fori(0, NE // 2) as i:
                ch.enter(i, 4)
                for u in range(2):
                    e = i * 2 + u
                    gate_step(e)
                    dve.wait_ge(ev("xe_ps"), e + 1)
                    route(e + 1, 1 - u)
                    slot_gates(e + 1, 1 - u)
                    up_step(e)
            ch.leave(NE // 2)
            dve.wait_ge(ev("over_list"), 1)
            n_over = dve.value_load(small_i[0:1, 16:17], min_val=0, max_val=MAX_OVER)
            with dve.If(n_over > 0):
                with dve.Fori(0, MAX_OVER) as j:
                    with dve.If(n_over > j):
                        ch.enter(j, 2)
                        e = dve.value_load(small_i[0:1, bass.ds(j, 1)], min_val=0, max_val=NE - 1)
                        off = offb[:, bass.ds(j, 1)]
                        dve.wait_ge(ev("combined"), j + (NE + 1))
                        route(e, 0, off)
                        slot_gates(j + (NE + 1), 0, off)
                        gate_step(j + NE)
                        up_step(j + NE)

            fin = Chain(dve, "dve_last_steps")
            dve.wait_ge(ev("moe_done"), 1)
            dve.wait_ge(ev("mod_out"), 12)
            for t in range(2):
                for half in range(2):
                    cols = slice(512 * half, 512 * (half + 1))
                    buf = k_pool[:, 512 * (2 * t + half):512 * (2 * t + half + 1)]
                    fin.step(V.tensor_tensor(buf, B[4 + 2 * t + half], g2[:, cols], ALU.mult))
                    V.tensor_tensor(xres[:, t, cols], xres[:, t, cols], buf, ALU.add).then_inc(ev("x2_ready"), 1)
            dve.wait_ge(ev("gain3_loaded"), 16)
            for t in range(2):
                dve.wait_ge(ev("rmsf"), t + 1)
                fin.step(V.reciprocal(rsf[:, t:t + 1], rsf[:, t:t + 1]))
                V.scalar_tensor_tensor(xres[:, t, :], xres[:, t, :], rsf[:, t:t + 1], gain, ALU.mult, ALU.mult).then_inc(ev("y_ready"), 1)

        @block.tensor
        def _(pe):
            mm, tr = nc.tensor.matmul, nc.tensor.transpose
            pe.wait_ge(ev("consts_loaded"), 64)
            pe.wait_ge(ev("cond_silu"), 1)
            tr(B[4][:, 0:16], cond, ident[0:16, 0:16]).then_inc(ev("condT_ps"), 1)
            pe.wait_ge(ev("condT_ready"), 1)

            def slot_wait(n):
                pe.wait_ge(slot_loaded[n % RING], 16 * (n // RING + 1))

            def mod_sums(n):
                if n >= 2:
                    pe.wait_ge(ev("mod_part"), n - 1 if n < 4 else n)
                at = mod_at(n)
                for r in range(2):
                    slot_wait(at + r)
                    w = ring[:, (at + r) % RING, :].rearrange("p (k n) -> p k n", k=4)
                    for j in range(4):
                        ins = mm(B[mod_bank(n)][32 * j:32 * (j + 1), :], condT[:, 4 * r + j, :], w[:, j, :],
                                 start=r == 0, stop=r == 1, tile_position=(0, 32 * j))
                    ins.then_inc(chunks_used, 1)

            def mod_spread(n):
                if n >= 2:
                    pe.wait_ge(ev("mod_out"), n - 1 if n < 5 else n)
                pe.wait_ge(ev("mod_part"), n + 1)
                mm(B[bc_bank(n)], cst[:, C_MODSEL:C_MODSEL + P], part[n % 2], start=True, stop=True).then_inc(ev("mod_bc"), 1)

            mod_sums(0)
            mod_sums(1)
            mod_spread(0)
            mod_sums(2)
            mod_spread(1)
            mod_sums(3)
            mod_spread(2)
            mod_spread(3)
            for t in range(2):
                pe.wait_ge(ev("h_ready"), t + 1)
                for q in range(2):
                    for k in range(4):
                        ins = tr(B[4 + 2 * t + q][:, P * k:P * (k + 1)], rows[:, t, P * (4 * q + k):P * (4 * q + k + 1)], ident)
                    ins.then_inc(ev("hT_ps"), 1)

            def project(i):
                if i == H_G:
                    pe.wait_ge(ev("ssg"), 2)
                elif i >= 2:
                    pe.wait_ge(ev("win_out"), i - 1)
                n = AT_WIN + i
                slot_wait(n)
                w = ring[:, n % RING, :].rearrange("p (k n) -> p k n", k=KT)
                bank = B[i % 2]
                for r in range(2):
                    for k in range(KT):
                        if i in (Z_F, Z_B, H_Q, K_0, K_1, Q_0, Q_1):
                            ins = mm(bank[:, 256 * r:256 * (r + 1)], w[:, k, P * r:P * (r + 1)],
                                     hT[:, k, :, :], start=k == 0, stop=k == KT - 1)
                        else:
                            ins = mm(bank[:, 256 * r:256 * (r + 1)], hT[:, k, r, :], w[:, k, :],
                                     start=k == 0, stop=k == KT - 1)
                ins.then_inc(chunks_used, 1)

            def level_mm(n):
                if n < 0:
                    pe.wait_ge(ev("ksum_ready"), 1)
                    pe.wait_ge(ev("win_out"), H_Q + 1)
                else:
                    pe.wait_ge(ev("lvl_qk"), 4 * (n + 1))
                    pe.wait_ge(ev("lvl_store"), 4 * n + 2)
                for d in range(1 if n < 0 else 2):
                    for m in range(4):
                        for q in range(2):
                            hd = slice(HD * q, HD * (q + 1))
                            keys = Kl[hd, d, P * m:P * (m + 1)]
                            if n < 0:
                                ins = mm(B[2 + q][:, P * m:P * (m + 1)], keys, hqT[hd, P * m:P * (m + 1)], start=True, stop=True)
                            else:
                                ins = mm(B[2 + q][:, 256 * d + 64 * m:256 * d + 64 * (m + 1)], keys,
                                         Qc[hd, d, 64 * m:64 * (m + 1)], start=True, stop=True)
                ins.then_inc(ev("lvl_mm"), 1)

            def scores(bank, g, keys):
                for h in range(HP):
                    for q in range(2):
                        hd = slice(HD * q, HD * (q + 1))
                        ins = mm(B[bank + q][:, P * h:P * (h + 1)], qT[hd, h, g, :], keys(hd, h), start=True, stop=True)
                return ins

            pe.wait_ge(ev("hT_ready"), 4)
            for i in (Z_F, Z_B, H_Q, H_I):
                project(i)
            pe.wait_ge(ev("early_loaded"), 48)
            for h in range(HP):
                ins = tr(B[6][:, P * h:P * (h + 1)], ck[:, P * h:P * (h + 1)], ident)
            ins.then_inc(ev("early_ps"), 1)
            for g in range(GM):
                ins = tr(B[7][:, P * g:P * (g + 1)], ws[:, g, :], ident)
            ins.then_inc(ev("early_ps"), 1)
            tr(B[2][:, 0:GM], gb_rows, ident[0:GM, 0:GM]).then_inc(ev("early_ps"), 1)
            pe.wait_ge(ev("bias_raw_loaded"), 64)
            pe.wait_ge(ev("flip_ready"), 1)
            for q in range(2):
                ins = mm(B[4 + q], flip, bias_raw[:, HP * q:HP * (q + 1), :], start=True, stop=True)
            ins.then_inc(ev("flip_ps"), 1)
            project(K_0)
            project(Q_0)
            pe.wait_ge(ev("early_out"), 3)
            level_mm(-1)
            project(K_1)
            level_mm(0)
            project(Q_1)
            level_mm(1)
            pe.wait_ge(ev("win_out"), K_1 + 1)
            for h in range(HP):
                ins = tr(B[6][:, P * h:P * (h + 1)], kT[:, h, 0, :], ident)
            ins.then_inc(ev("kout_ps"), 1)
            project(V_0)
            level_mm(2)
            pe.wait_ge(ev("biasN_ready"), 2)
            pe.wait_ge(ev("win_out"), Q_1 + 1)
            scores(4, 0, lambda hd, h: kT[hd, h, 0, :]).then_inc(ev("score_p"), 1)
            project(V_1)
            level_mm(3)
            project(G_V)
            level_mm(4)
            pe.wait_ge(ev("exp_p"), NH)
            pe.wait_ge(ev("kout_ready"), 1)
            for q in range(2):
                for h in range(HP):
                    ins = tr(B[6 + q][:, P * h:P * (h + 1)], probs_p[:, q, h, :], ident)
                ins.then_inc(ev("pT_ps"), 1)
            project(G_U)
            level_mm(5)
            pe.wait_ge(ev("pT_ready"), 2)
            for h in range(HP):
                for q in range(2):
                    head = 2 * h + q
                    ins = mm(B[4][:, HD * head:HD * (head + 1)], pT_p[:, q, P * h:P * (h + 1)],
                             v[:, 0, HD * head:HD * (head + 1)], start=True, stop=True)
            ins.then_inc(ev("att_p_ps"), 1)
            pe.wait_ge(ev("vg_ready"), 2)
            for g in range(GM):
                ins = mm(B[5][:, P * g:P * (g + 1)], wsT[:, g, :],
                         rows[:, :, 768 + HD * g:768 + HD * (g + 1)], start=True, stop=True)
            ins.then_inc(ev("z_ps"), 1)
            project(H_G)
            level_mm(6)

            pe.wait_ge(ev("gmlp_ready"), 1)
            scores(4, 1, lambda hd, h: kT[hd, h, 1, :])
            scores(6, 1, lambda hd, h: ckT[hd, h, :]).then_inc(ev("score_s"), 1)
            pe.wait_ge(ev("end_ready"), 4)
            for d in range(2):
                for h in range(RP):
                    ins = tr(B[1][:, P * (2 * d + h):P * (2 * d + h + 1)], Kend[:, d, h, :], ident)
            ins.then_inc(ev("kst_ps"), 1)
            pe.wait_ge(ev("lvl_store"), 30)
            pe.wait_ge(ev("mixer_loaded"), 144)
            for q in range(2):
                for g in range(G):
                    for h in range(RP):
                        out = B[2 + q][:, 256 * g + HD * h:256 * g + HD * (h + 1)]
                        m = 2 * h + g
                        ins = mm(out, AT[:, q, P * m:P * (m + 1)], hi[:, g, HD * (2 * h + q):HD * (2 * h + q + 1)],
                                 start=True, stop=g == 0)
                        for d in range(2 if g else 0):
                            ins = mm(out, Qend[HD * q:HD * (q + 1), d, h, :], s0[HD * q:HD * (q + 1), d, h, :],
                                     start=False, stop=d == 1)
            ins.then_inc(ev("o_ps"), 1)
            pe.wait_ge(ev("kst_ready"), 1)
            pe.wait_ge(ev("silu_g"), 1)
            for d in range(2):
                for h in range(RH):
                    ins = mm(B[0][0:HD, 256 * d + HD * h:256 * d + HD * (h + 1)],
                             kstT[:, d, h // 2, HD * (h % 2):HD * (h % 2 + 1)], hi[:, 0, HD * h:HD * (h + 1)], start=True, stop=True)
            ins.then_inc(ev("state_ps"), 1)

            def cat_transpose(g, kh, bank):
                for k in range(4):
                    ins = tr(B[bank][:, P * k:P * (k + 1)], rows[:, g, P * (4 * kh + k):P * (4 * kh + k + 1)], ident)
                ins.then_inc(ev("cat_ps"), 1)

            def probs_transpose(q):
                pe.wait_ge(ev("exp_s"), 2 * q + 2)
                for n in range(4 * q, 4 * q + 4):
                    ins = tr(B[4 + q % 2][:, P * (n % 4):P * (n % 4 + 1)], probs[:, n // 2, P * (n % 2):P * (n % 2 + 1)], ident)
                ins.then_inc(ev("sT_ps"), 1)

            def project_out(i):
                slot_wait(AT_WOUT + i)
                w = ring[:, (AT_WOUT + i) % RING, :].rearrange("p (k n) -> p k n", k=2)
                for t in range(2):
                    for kk in range(2):
                        for half in range(2):
                            ins = mm(B[2 * t + half], catT[:, 2 * WOUT[i] + kk, t, :], w[:, kk, 512 * half:512 * (half + 1)],
                                     start=i == 0 and kk == 0, stop=i == 3 and kk == 1)
                    if t == 0 and i == 3:
                        ins.then_inc(ev("wout_ps"), 1)
                ins.then_inc(chunks_used, 1)

            pe.wait_ge(ev("state_ready"), 1)
            mod_sums(4)
            mod_spread(4)
            mod_sums(5)
            mod_spread(5)
            mod_sums(6)
            pe.wait_ge(ev("hgrn_ready"), 1)
            pe.wait_ge(ev("ctx_sc"), 2)
            cat_transpose(0, 1, 6)
            cat_transpose(1, 1, 7)
            mod_spread(6)
            mod_sums(7)
            mod_spread(7)
            pe.wait_ge(ev("local_sc"), 2)
            probs_transpose(0)
            probs_transpose(1)
            mod_sums(8)
            mod_spread(8)
            pe.wait_ge(ev("sT_ready"), 1)
            probs_transpose(2)
            pe.wait_ge(ev("sT_ready"), 2)
            probs_transpose(3)
            mod_sums(9)
            mod_spread(9)
            pe.wait_ge(ev("catT_ready"), 2)
            pe.wait_ge(ev("mod_out"), 10)
            pe.wait_ge(ev("o_out"), 2)
            project_out(0)
            for n in range(16):
                if n % 4 == 0:
                    pe.wait_ge(ev("sT_ready"), n // 4 + 1)
                head = n // 2
                src = (sT_lo if n < 8 else sT_hi)[:, P * (n % 8):P * (n % 8 + 1)]
                val = (cv if n % 2 else v[:, 1, :])[:, HD * head:HD * (head + 1)]
                ins = mm(B[6][:, HD * head:HD * (head + 1)], src, val, start=n % 2 == 0, stop=n % 2 == 1)
            ins.then_inc(ev("att_s_ps"), 1)
            cat_transpose(0, 0, 7)
            project_out(1)
            pe.wait_ge(ev("att_s"), 1)
            cat_transpose(1, 0, 5)
            pe.wait_ge(ev("catT_ready"), 4)
            project_out(2)
            project_out(3)
            mod_sums(10)
            mod_spread(10)
            mod_sums(11)
            mod_spread(11)
            for n in range(4):
                if n == 2:
                    pe.wait_ge(ev("mod_out"), 12)
                mm(B[4 + n], zeros, cst[:, 0:512], start=True, stop=False)

            pe.wait_ge(ev("x1_ready"), 4)
            for t in range(2):
                pe.wait_ge(ev("h2_ready"), t + 1)
                for q in range(2):
                    if t:
                        pe.wait_ge(ev("h2T_ready"), q + 1)
                    for k in range(4):
                        ins = tr(B[2 + q][:, P * k:P * (k + 1)], rows[:, t, P * (4 * q + k):P * (4 * q + k + 1)], ident)
                    ins.then_inc(ev("h2T_ps"), 1)
            for t in range(2):
                pe.wait_ge(ev("h2T_ready"), 2 * t + 2)
                out = B[0][:, NE * t:NE * (t + 1)]
                mm(out, ones_rows, rbias, start=True, stop=False)
                for k in range(KT):
                    ins = mm(out, h2T[:, k, t, :], rw[:, k, :], start=False, stop=k == KT - 1)
            ins.then_inc(ev("logits_ps"), 1)
            pe.wait_ge(ev("mask_ready"), 1)
            tri = cst[:, C_TRI:C_TRI + P]
            mm(B[1][:, 0:NE], tri, msk[:, 0, :], start=True, stop=True)
            mm(B[1][:, NE:2 * NE], tri, msk[:, 1, :], start=True, stop=False)
            mm(B[1][:, NE:2 * NE], ones[:, 0:1].to_broadcast([P, P]), msk[:, 0, :], start=False, stop=True)
            for t in range(2):
                ins = mm(B[1][:, 64:65], mask4[:, t].rearrange("p r e -> p (r e)"), ones[:, 0:1], start=t == 0, stop=t == 1)
            ins.then_inc(ev("rank_ps"), 1)
            pe.wait_ge(ev("rank_ready"), 1)
            pe.wait_ge(ev("gate_ready"), 1)
            pe.wait_ge(ev("flag_ready"), 1)
            for t in range(2):
                tr(B[1][0:NE, P * t:P * (t + 1)], rank[:, t, 0:NE], ident)
                ins = tr(B[1][0:NE, 256 + P * t:256 + P * (t + 1)], gate[:, t, :], ident)
            ins.then_inc(ev("rgT_ps"), 1)
            mm(B[0][:, 64:65], cst[:, C_STRI:C_STRI + P], flag, start=True, stop=True).then_inc(ev("pos_ps"), 1)

            def spread(buf, count):
                pe.wait_ge(ev("route_ready"), count + 1)
                mm(B[3], pick[:, buf, :], rgT, start=True, stop=True).then_inc(ev("bc_ps"), 1)

            def gather(count):
                pe.wait_ge(ev("gT_ready"), count + 1)
                for k in range(KT):
                    for t in range(2):
                        ins = mm(B[3][:, CAP * k:CAP * (k + 1)], rows[:, t, P * k:P * (k + 1)], Ptok[:, t, :],
                                 start=t == 0, stop=t == 1)
                ins.then_inc(ev("xe_ps"), 1)

            def product(bank, m, buf, lhsT, count):
                for half in range(2):
                    cols = slice(512 * half, 512 * (half + 1))
                    mm(bank[CAP * half:CAP * (half + 1), :], pick[:, buf, 0:CAP], mbias[:, m, cols], start=True, stop=False)
                for r in range(4):
                    cidx = 4 * m + r
                    pe.wait_ge(slot_loaded[expert_slot(cidx)], chunk_loads(cidx, count))
                    w = ring[:, expert_slot(cidx), :].rearrange("p (k n) -> p k n", k=2)
                    for kk in range(2):
                        for half in range(2):
                            ins = mm(bank[CAP * half:CAP * (half + 1), :], lhsT(2 * r + kk), w[:, kk, 512 * half:512 * (half + 1)],
                                     start=False, stop=r == 3 and kk == 1)
                    ins.then_inc(chunks_used, 1)

            def combine(buf, stored):
                pe.wait_ge(ev("y_sb"), stored)
                for t in range(2):
                    for half in range(2):
                        r = slice(CAP * half, CAP * (half + 1))
                        ins = mm(B[4 + 2 * t + half], gT[r, buf, P * t:P * (t + 1)], ysb[r, :], start=False, stop=False)
                ins.then_inc(ev("combined"), 1)

            def xe_tile(k):
                return xe[:, k, :]

            def a_tile(k):
                return aT[:, k % 4, CAP * (k // 4):CAP * (k // 4 + 1)]

            def down(buf, count):
                pe.wait_ge(ev("a_ready"), count + 1)
                for q in range(4):
                    ins = tr(B[2][:, P * q:P * (q + 1)], ab[:, P * q:P * (q + 1)], ident)
                ins.then_inc(ev("aT_ps"), 1)
                pe.wait_ge(ev("aT_ready"), count + 1)
                product(B[2], 2, buf, a_tile, count)

            pe.wait_ge(ev("rgT_ready"), 1)
            spread(0, 0)
            pe.wait_ge(ev("onehot_ready"), 1)
            mm(B[0][:, 128:144], cst[:, C_OFF:C_OFF + 1].to_broadcast([P, P]), onehot, start=True, stop=True)
            mm(B[0][:, 144:160], cst[:, C_E:C_E + 1].to_broadcast([P, P]), onehot, start=True, stop=True)
            mm(B[0][:, 160:161], ones[:, 0:1].to_broadcast([P, P]), flag, start=True, stop=True).then_inc(ev("list_ps"), 1)
            gather(0)
            pe.wait_ge(ev("mbias_loaded"), 48)
            pe.wait_ge(ev("over_list"), 1)
            with pe.Fori(0, NE // 2) as i:
                for u in range(2):
                    e = i * 2 + u
                    pe.wait_ge(ev("xe_ready"), e + 1)
                    product(B[0], 0, u, xe_tile, e)
                    combine(1 - u, e + 1)
                    spread(1 - u, e + 1)
                    product(B[1], 1, u, xe_tile, e)
                    gather(e + 1)
                    down(u, e)
            combine(1, NE + 1)
            n_over = pe.value_load(small_i[0:1, 16:17], min_val=0, max_val=MAX_OVER)
            with pe.If(n_over > 0):
                with pe.Fori(0, MAX_OVER) as j:
                    with pe.If(n_over > j):
                        spread(0, j + (NE + 1))
                        gather(j + (NE + 1))
                        pe.wait_ge(ev("xe_ready"), j + (NE + 2))
                        product(B[0], 0, 0, xe_tile, j + NE)
                        product(B[1], 1, 0, xe_tile, j + NE)
                        down(0, j + NE)
                        combine(0, j + (NE + 2))
            for n in range(4):
                ins = mm(B[4 + n][:, 0:16], zeros, cst[:, 0:16], start=False, stop=True)
            ins.then_inc(ev("moe_done"), 1)


_INS = ['x_prompt', 'x_sample', 'cache_k', 'cache_v', 'state_hgrn_fwd', 'state_hgrn_bwd', 'c', 'c_ctx',
        'w_mod', 'b_mod', 'norm1_g', 'norm2_g', 'w_in', 'na_rel_bias', 'hgrn_lb', 'hgrn_onorm_g',
        'gmlp_vnorm_g', 'gmlp_ws', 'gmlp_b', 'w_out', 'router_w', 'router_b', 'w_gate', 'b_gate',
        'w_up', 'b_up', 'w_down', 'b_down', 'final_g']
_OUTS = [(1, P, D), (1, P, D), (1, 1, P, NH, HD), (1, 1, P, NH, HD), (1, 1, RH, HD, HD), (1, 1, RH, HD, HD)]


def kernel(**inputs):
    import concourse.bacc as bacc
    from concourse.bass_utils import run_bass_kernel_spmd

    nc = bacc.Bacc("TRN2", target_bir_lowering=False, num_devices=1)
    arrays, args = {}, []
    const_f32, const_masks = shape_constants()
    given = [(name, inputs[name]) for name in _INS] + [("const_f32", const_f32), ("const_masks", const_masks)]
    for name, array in given:
        array = np.ascontiguousarray(array)
        arrays[f"in_{name}"] = array
        args.append(nc.dram_tensor(f"in_{name}", array.shape, mybir.dt.from_np(array.dtype), kind="ExternalInput").ap())
    for i, shape in enumerate(_OUTS):
        args.append(nc.dram_tensor(f"out_{i}", shape, F32, kind="ExternalOutput").ap())
    hybrid_layer(nc, *args)
    r = run_bass_kernel_spmd(nc, [arrays], core_ids=[0])
    return tuple(r.results[0][f"out_{i}"] for i in range(len(_OUTS)))
```

```python
from contextlib import ExitStack

import numpy as np

import concourse.bass as bass
from concourse import mybir

F32 = mybir.dt.float32
I32 = mybir.dt.int32
U8 = mybir.dt.uint8
ALU = mybir.AluOpType
ACT = mybir.ActivationFunctionType
AX = mybir.AxisListType

P = 128
D = 1024
KT = D // P
G = 2
HALF = 64
HD = 64
NH = 8
HP = NH // 2
RH = 4
RP = RH // 2
GM = 4
GRID_W = 64
NA_KH, NA_KW = 8, 16
NE = 32
TOP_K = 4
CAP = 64
CHUNKS = G * P // CAP
MAX_OVER = (G * P * TOP_K - NE) // CAP
LIMIT, ALPHA = 7.0, 1.702
EPS = 1e-6
F_FLOOR = 1e-30
LN_SPLIT = 60
NEG = -1e30
SCALE = HD ** -0.5

RING = 12
SLOT = 2048
MODS = [1, 0, 2, 4, 3, 5]
WIN = [7, 8, 6, 9, 2, 0, 3, 1, 4, 5, 12, 11, 10]
Z_F, Z_B, H_Q, H_I, K_0, Q_0, K_1, Q_1, V_0, V_1, G_V, G_U, H_G = range(13)
AT_WIN = 8
AT_MODS2 = AT_WIN + len(WIN)
AT_WOUT = AT_MODS2 + 12
AT_MODG2 = AT_WOUT + 4
AT_MOE = AT_MODG2 + 4
WOUT = [2, 3, 0, 1]
LEVELS = [64, 32, 16, 8, 4, 2, 1]

C_IDENT, C_TRI, C_STRI, C_MODSEL, C_SLOTROW = 0, P, 2 * P, 3 * P, 4 * P
C_SLOTCOL = C_SLOTROW + CAP
C_THR, C_E, C_OFF = C_SLOTCOL + 1, C_SLOTCOL + 2, C_SLOTCOL + 3
C_IOTA = C_SLOTCOL + 4
C_END = C_IOTA + 16
M_WINDOW = 14


def shape_constants():
    f = np.zeros((P, C_END), np.float32)
    i = np.arange(P)
    f[:, C_IDENT:C_IDENT + P] = np.eye(P)
    f[:, C_TRI:C_TRI + P] = i[:, None] <= i[None, :]
    f[:, C_STRI:C_STRI + P] = i[:, None] < i[None, :]
    for j in range(4):
        for r in range(G):
            f[32 * j + r, C_MODSEL + HALF * r:C_MODSEL + HALF * (r + 1)] = 1
    f[:, C_SLOTROW:C_SLOTROW + CAP] = np.arange(1, CAP + 1)
    f[:, C_SLOTCOL] = i % CAP + 1
    f[:, C_THR] = np.where(i < NE, 1e9, CAP * (i // NE))
    f[:, C_E] = i % NE
    f[:, C_OFF] = CAP * (i // NE)
    f[:, C_IOTA:C_IOTA + 16] = np.arange(16)
    m = np.zeros((P, 16, P), np.float32)
    s, t = i[:, None], i[None, :]
    for n, w in enumerate(LEVELS):
        same = s // (2 * w) == t // (2 * w)
        first, second = s % (2 * w) < w, t % (2 * w) >= w
        m[:, n] = same & first & second
        m[:, 7 + n] = m[:, n].T
    qc, kc = s % GRID_W, t % GRID_W
    start = np.clip(qc - NA_KW // 2, 0, GRID_W - NA_KW)
    m[:, M_WINDOW] = (kc >= start) & (kc < start + NA_KW)
    return f, m.reshape(P, 16 * P)


def hybrid_layer(nc, x_prompt, x_sample, cache_k, cache_v, state_hgrn_fwd, state_hgrn_bwd, c, c_ctx,
                 w_mod, b_mod, norm1_g, norm2_g, w_in, na_rel_bias, hgrn_lb, hgrn_onorm_g,
                 gmlp_vnorm_g, gmlp_ws, gmlp_b, w_out, router_w, router_b, w_gate, b_gate,
                 w_up, b_up, w_down, b_down, final_g, const_f32, const_masks,
                 y_prompt, y_sample, new_k, new_v, new_sf, new_sb):
    assert CHUNKS * NE == P and MAX_OVER <= 16
    ctx = ExitStack()
    with ctx:
        def sb(name, cols, dt=F32, parts=P):
            return ctx.enter_context(nc.sbuf_tensor(name, [parts, cols], dt))[:, :]

        events = {}

        def ev(name):
            if name not in events:
                events[name] = ctx.enter_context(nc.semaphore(name))
            return events[name]

        ring = sb("ring", RING * SLOT).rearrange("p (s w) -> p s w", s=RING)
        cst = sb("cst", C_END)
        masks = sb("masks", 16 * P, U8).rearrange("p (m t) -> p m t", m=16)
        xres = sb("xres", 2 * D).rearrange("p (t d) -> p t d", t=2)
        gain = sb("gain", D)
        gsc = sb("gsc", D)
        shf = sb("shf", D)
        rows = sb("rows", 2 * D).rearrange("p (t d) -> p t d", t=2)
        colsT = sb("colsT", 2 * D)
        kv_pool = sb("kv_pool", 3 * 1024)
        hq_hi = sb("hq_hi", 2 * 512)
        keyT = sb("keyT", 1024).rearrange("p (d n) -> p d n", d=2)
        cumT = sb("cumT", 1024).rearrange("p (d n) -> p d n", d=2)
        tmp = sb("tmp", 1024)
        g12 = sb("g12", 2 * D)
        q_start = sb("q_start", 512)
        k_pool = sb("k_pool", 2048)
        d_pool = sb("d_pool", 1024)
        at_pool = sb("at_pool", 1024)
        biasN = sb("biasN", 1024).rearrange("p (h k) -> p h k", h=NH)
        cv = sb("cv", 512)
        ckT = sb("ckT", 512).rearrange("p (h l) -> p h l", h=HP)
        wsT = sb("wsT", 512).rearrange("p (g t) -> p g t", g=GM)
        condT = sb("condT", KT * 32).rearrange("p (k m) -> p k m", k=KT)
        rbias = sb("rbias", NE, parts=1)
        s0 = sb("s0", 2 * RP * HD).rearrange("p (d h v) -> p d h v", d=2, h=RP)
        rw = sb("rw", KT * NE).rearrange("p (k e) -> p k e", k=KT)
        vng = sb("vng", GM * HD)
        ong = sb("ong", HD)
        cond = sb("cond", P, parts=16)
        gb_rows = sb("gb_rows", P, parts=GM)
        small = sb("small", 120)
        ones = sb("ones", 8)
        small_i = sb("small_i", 18, I32, parts=1)
        ones_rows = ones[0:1, 0:1].to_broadcast([1, P])

        ident = cst[:, C_IDENT:C_IDENT + P]
        ck = d_pool[:, 0:512]
        ws = d_pool[:, 512:1024].rearrange("p (g s) -> p g s", g=GM)
        hT = colsT.rearrange("p (k g t) -> p k g t", k=KT, g=G)
        catT = colsT.rearrange("p (k t gt) -> p k t gt", k=KT, t=2)
        h2T = catT
        qT, kT = (kv_pool[:, 1024 * n:1024 * (n + 1)].rearrange("p (h g t) -> p h g t", h=HP, g=G)
                  for n in range(2))
        v = kv_pool[:, 2048:3072].rearrange("p (g n) -> p g n", g=G)
        hqT = hq_hi[:, 0:512]
        hi = hq_hi[:, 512:1024].rearrange("p (g n) -> p g n", g=G)
        sig = tmp.rearrange("p (d n) -> p d n", d=2)
        kout = rows[:, :, 512:768]
        state_out = tmp[:, 0:512]
        norm1_row, scale1_row, shift1_row = cumT[0:1, :, :], keyT[0:1, :, :], hq_hi[0:1, :]
        xtmp = [tmp[:, 0:512], tmp[:, 512:1024]]
        gtmp = tmp[:, 512:1024]
        part = [at_pool[:, 0:512], at_pool[:, 512:1024]]
        AT = at_pool.rearrange("p (q n) -> p q n", q=2)
        Kl = k_pool[:, 0:1024].rearrange("p (d n) -> p d n", d=2)
        Qpair = gain.rearrange("p (d a q n) -> p d a q n", d=2, a=4, q=2)
        Qend = q_start.rearrange("p (d h t) -> p d h t", d=2, h=RP)
        Kend = k_pool[:, 0:512].rearrange("p (d h t) -> p d h t", d=2, h=RP)
        g1, g2 = g12[:, 0:D], g12[:, D:2 * D]
        Dl = d_pool.rearrange("p (d n) -> p d n", d=2)
        Dk = Dl[:, :, 0:256].rearrange("p d (h t) -> p d h t", h=RP)
        Dq = Dl[:, :, 256:512].rearrange("p d (h t) -> p d h t", h=RP)
        cum4 = cumT.rearrange("p d (h g t) -> p d h g t", h=RP, g=G)
        key4 = keyT.rearrange("p d (h g t) -> p d h g t", h=RP, g=G)
        hq4 = hqT.rearrange("p (h g t) -> p h g t", h=RP, g=G)
        kstT = d_pool[:, 0:512].rearrange("p (d h k) -> p d h k", d=2, h=RP)
        probs = k_pool[:, :].rearrange("p (h k) -> p h k", h=NH)
        probs_p = rows[:, :, 0:512].rearrange("p q (h k) -> p q h k", h=HP)
        pT_p = k_pool[:, 1024:2048].rearrange("p (q n) -> p q n", q=2)
        bias_raw = kv_pool[:, 2048:3072].rearrange("p (h k) -> p h k", h=NH)
        flip = kv_pool[:, 0:P]
        biasN_flat = biasN.rearrange("p h k -> p (h k)")
        sT_lo = biasN_flat
        sT_hi = d_pool
        ss = small[:, 0:2]
        rstd = small[:, 2:4]
        lbT = small[:, 4:8]
        omlT = small[:, 8:12]
        lb_t = small[:, 12:20]
        gbT = small[:, 20:24]
        ssg = small[:, 24:26]
        rsg = small[:, 26:28]
        sso = small[:, 28:36]
        rso = small[:, 36:44]
        mx = small[:, 44:52]
        nmx = small[:, 52:60]
        rsum = small[:, 60:68]
        rinv = small[:, 68:76]
        mx_s = small[:, 76:84]
        nmx_s = small[:, 84:92]
        rsum_s = small[:, 92:100]
        rinv_s = small[:, 100:108]
        eps = small[:, 108:109]
        ssf = small[:, 110:112]
        rsf = small[:, 112:114]
        ss2 = small[:, 114:116]
        rs2 = small[:, 116:118]
        zcol = small[:, 118:119]

        moe_pool = kv_pool
        mbias = moe_pool[0:NE, :].rearrange("p (m n) -> p m n", m=3)
        actb = k_pool[:, 0:512]
        upb = k_pool[:, 512:1024]
        sigb = k_pool[:, 1024:1536]
        aT = k_pool[:, 1536:2048].rearrange("p (c s) -> p c s", c=4)
        ab = d_pool[:, 0:512]
        ysb = d_pool[:, 512:1024]
        xe = at_pool[:, 0:512].rearrange("p (k s) -> p k s", k=KT)
        gT = at_pool[:, 512:1024].rearrange("p (b t) -> p b t", b=2)
        pick = cumT[0:NE, 0, 0:256].rearrange("p (b m) -> p b m", b=2)
        Ptok = keyT[:, 0, 0:2 * CAP].rearrange("p (t s) -> p t s", t=2)
        rank = keyT[:, 0, 128:128 + 2 * (NE + 1)].rearrange("p (t e) -> p t e", t=2)
        gate = keyT[:, 0, 200:264].rearrange("p (t e) -> p t e", t=2)
        lg = keyT[:, 0, 264:328].rearrange("p (t e) -> p t e", t=2)
        msk = keyT[:, 0, 328:392].rearrange("p (t e) -> p t e", t=2)
        eqm = keyT[:, 0, 392:456].rearrange("p (t e) -> p t e", t=2)
        csm = keyT[:, 1, 0:64].rearrange("p (t e) -> p t e", t=2)
        ex = keyT[:, 1, 64:128].rearrange("p (t e) -> p t e", t=2)
        rsm = keyT[:, 1, 128:160]
        flag = keyT[:, 1, 160:161]
        posn = keyT[:, 1, 161:162]
        onehot = keyT[:, 1, 162:178]
        offb = keyT[:, 1, 178:194]
        mask4 = keyT[:, 1, 194:450].rearrange("p (t r e) -> p t r e", t=2, r=CHUNKS)
        rgT = cumT[0:NE, 1, :]
        zeros = zcol.to_broadcast([P, P])
        identE = wsT[0:NE, 0, 0:NE + 1]

        B = [ctx.enter_context(nc.psum_tensor(f"bank{n}", [P, 512], F32))[:, :] for n in range(8)]

        def mod_at(n):
            return 2 * n if n < 4 else AT_MODS2 + 2 * (n - 4) if n < 10 else AT_MODG2 + 2 * (n - 10)

        def mod_bank(n):
            return n % 2 if n < 4 or 6 <= n < 10 else {4: 6, 5: 7, 10: 6, 11: 7}[n]

        def bc_bank(n):
            return 2 + n if n < 4 else mod_bank(n) if n < 10 else n - 6

        def mod_part_buf(n):
            return biasN_flat[:, 512 * (n % 2):512 * (n % 2 + 1)] if n in (4, 5) else part[n % 2]

        def bcast_row(ap):
            return ap.partition_broadcast(P).rearrange("p a d -> p (a d)")

        def level_view(ap, w):
            return ap.rearrange("p (n h m) -> p n h m", h=2, m=w)

        slot_loaded = [ctx.enter_context(nc.semaphore(f"slot{n}_loaded")) for n in range(RING)]
        chunks_used = ctx.enter_context(nc.semaphore("chunks_used"))

        def halves(ap):
            return ap.rearrange("(o p) d -> o p d", p=HALF)

        def expert_slot(cidx):
            return (AT_MOE + cidx) % RING

        def chunk_loads(cidx, e):
            return ((AT_MOE + cidx) // RING + 1 + e) * 16

        def used(cidx, e):
            return e * RING + (AT_MOE + cidx + 1)

        class Chain:

            def __init__(self, eng, name):
                self.eng, self.sem, self.n, self.at = eng, ev(name), 0, None

            def step(self, ins):
                ins.then_inc(self.sem, 1)
                self.n += 1
                self.eng.wait_ge(self.sem, self.n if self.at is None else self.at + self.n)

            def enter(self, reg, per):
                self.at, self.per, self.start = reg * per, per, self.n

            def leave(self, times):
                assert self.n - self.start == self.per, (self.n - self.start, self.per)
                self.at, self.n = None, self.start + self.per * times

        block = ctx.enter_context(nc.Block())

        @block.sync
        def _(sp):
            def slot_free(n):
                if n >= RING:
                    sp.wait_ge(chunks_used, n - RING + 1)

            def load(n, view, src):
                slot_free(n)
                sp.dma_start(view, src).then_inc(slot_loaded[n % RING], 16)

            n = 0
            sp.dma_start(cond[0:8, :], c_ctx.rearrange("(k p) -> k p", p=P)).then_inc(ev("cond_loaded"), 16)
            sp.dma_start(cond[8:16, :], c.rearrange("b (k p) -> (b k) p", p=P)).then_inc(ev("cond_loaded"), 16)

            def load_mod(m):
                nonlocal n
                for half in range(2):
                    for r in range(2):
                        src = w_mod[0, 512 * r:512 * (r + 1), m * D + 512 * half:m * D + 512 * (half + 1)]
                        load(n, ring[:, n % RING, :].rearrange("p (k n) -> p k n", k=4),
                             src.rearrange("(k p) n -> p k n", p=P))
                        n += 1

            for m in MODS[:2]:
                load_mod(m)
            for b in WIN:
                load(n, ring[:, n % RING, :].rearrange("p (k n) -> p k n", k=KT),
                     w_in[0, :, 256 * b:256 * (b + 1)].rearrange("(k p) n -> p k n", p=P))
                n += 1
            for m in MODS[2:5]:
                load_mod(m)
            for r in WOUT:
                load(n, ring[:, n % RING, :].rearrange("p (k n) -> p k n", k=2),
                     w_out[0, 256 * r:256 * (r + 1), :].rearrange("(k p) n -> p k n", p=P))
                n += 1
            load_mod(MODS[5])
            assert n == AT_MOE

            def load_expert(e, count):
                for cidx in range(RING):
                    w = (w_gate, w_up, w_down)[cidx // 4]
                    sp.wait_ge(chunks_used, used(cidx - RING, count))
                    sp.dma_start(ring[:, expert_slot(cidx), :].rearrange("p (k n) -> p k n", k=2),
                                 w[0, bass.ds(e, 1), 256 * (cidx % 4):256 * (cidx % 4 + 1), :]
                                 .rearrange("a (k p) n -> p (a k) n", p=P)).then_inc(slot_loaded[expert_slot(cidx)], 16)

            with sp.Fori(0, NE) as e:
                load_expert(e, e)
            sp.wait_ge(ev("over_list"), 1)
            n_over = sp.value_load(small_i[0:1, 16:17], min_val=0, max_val=MAX_OVER)
            with sp.If(n_over > 0):
                with sp.Fori(0, MAX_OVER) as j:
                    with sp.If(n_over > j):
                        e = sp.value_load(small_i[0:1, bass.ds(j, 1)], min_val=0, max_val=NE - 1)
                        load_expert(e, j + NE)

            for t in range(2):
                sp.wait_ge(ev("y_ready"), t + 1)
                sp.dma_start(halves(y_prompt[0])[t], xres[0:HALF, t, :]).then_inc(ev("y_stored"), 16)
                sp.dma_start(halves(y_sample[0])[t], xres[HALF:P, t, :]).then_inc(ev("y_stored"), 16)
            sp.wait_ge(ev("y_stored"), 64)

        @block.gpsimd
        def _(pool):
            nc.gpsimd.memset(condT, 0.0).then_inc(ev("cols_set"), 1)
            nc.gpsimd.memset(ones, 1.0).then_inc(ev("cols_set"), 1)
            nc.gpsimd.memset(eps, EPS).then_inc(ev("cols_set"), 1)
            nc.gpsimd.memset(zcol, 0.0).then_inc(ev("cols_set"), 1)

            def small_load(name, dst, src):
                pool.dma_start(dst, src).then_inc(ev(name), 16)

            pool.wait_ge(chunks_used, 1)
            small_load("masks_loaded", k_pool, const_masks)
            small_load("early_loaded", ck, cache_k.rearrange("b l s h d -> (b l s) (h d)"))
            small_load("early_loaded", ws, gmlp_ws[0].rearrange("g t s -> t g s"))
            small_load("early_loaded", gb_rows, gmlp_b[0])
            for qr in range(2):
                for kr in range(2):
                    off = (NA_KH - 1 + kr - qr) * (2 * NA_KW - 1) + NA_KW - GRID_W
                    src = bass.AP(tensor=na_rel_bias.tensor, offset=na_rel_bias.offset + off,
                                  ap=[[1, GRID_W], [(2 * NA_KH - 1) * (2 * NA_KW - 1), NH], [1, GRID_W]])
                    small_load("bias_raw_loaded", bias_raw[64 * (1 - qr):64 * (2 - qr), :, 64 * kr:64 * (kr + 1)], src)
            small_load("mixer_loaded", cv, cache_v.rearrange("b l s h d -> (b l s) (h d)"))
            for d, src in enumerate((state_hgrn_fwd, state_hgrn_bwd)):
                small_load("mixer_loaded", s0[:, d], src[0, 0].rearrange("(h q) k v -> (q k) h v", q=2))
            small_load("mixer_loaded", vng, bcast_row(gmlp_vnorm_g[0:1, :]))
            small_load("mixer_loaded", ong, bcast_row(hgrn_onorm_g[0:1, :]))
            small_load("mixer_loaded", rw, router_w[0].rearrange("(k p) e -> p k e", p=P))
            small_load("mixer_loaded", rbias, router_b)
            small_load("mixer_loaded", g1, bcast_row(b_mod[0:1, 2 * D:3 * D]))
            small_load("mixer_loaded", g2, bcast_row(b_mod[0:1, 5 * D:6 * D]))
            pool.wait_ge(ev("masks_ready"), 1)
            nc.gpsimd.memset(Kl, 0.0).then_inc(ev("k_zero"), 1)
            pool.wait_ge(ev("h_ready"), 4)
            nc.gpsimd.memset(gain, 0.0).then_inc(ev("k_zero"), 1)
            small_load("norm2_loaded", gsc, bcast_row(b_mod[0:1, 4 * D:5 * D]))
            small_load("norm2_loaded", shf, bcast_row(b_mod[0:1, 3 * D:4 * D]))

            pool.wait_ge(ev("kout_ready"), 1)
            pool.dma_start(new_k.rearrange("b l s (g h) d -> (b l s) g (h d)", g=2), kout).then_inc(ev("kout_stored"), 16)
            pool.wait_ge(ev("win_out"), V_1 + 1)
            pool.dma_start(new_v.rearrange("b l s h d -> (b l s) (h d)"), v[:, 0, :]).then_inc(ev("caches_stored"), 16)
            pool.wait_ge(ev("lvl_mm"), 15)
            small_load("norm2_loaded", gain, bcast_row(norm2_g[0:1, :]))
            pool.wait_ge(ev("state_ready"), 1)
            for d, out in enumerate((new_sf, new_sb)):
                pool.dma_start(out.rearrange("b l h k v -> k (b l h) v"),
                               state_out[0:HD, 256 * d:256 * (d + 1)].rearrange("k (h v) -> k h v", h=RH)).then_inc(ev("caches_stored"), 16)
            nc.gpsimd.memset(identE, 0.0).then_inc(ev("idE_zero"), 1)
            pool.wait_ge(ev("idE_zero"), 1)
            nc.gpsimd.affine_select(out=identE, in_=identE, compare_op=ALU.not_equal, fill=1.0, base=0,
                                    pattern=[[-1, NE + 1]], channel_multiplier=1).then_inc(ev("idE_ready"), 1)
            pool.wait_ge(ev("mod_out"), 6)
            small_load("gain3_loaded", gain, bcast_row(final_g.rearrange("(a d) -> a d", a=1)))
            pool.wait_ge(ev("kout_stored"), 16)
            pool.wait_ge(ev("caches_stored"), 48)
            pool.wait_ge(ev("cat_ps"), 4)
            for m, src in enumerate((b_gate, b_up, b_down)):
                small_load("mbias_loaded", mbias[:, m, :], src[0])
            pool.wait_ge(ev("mbias_loaded"), 48)
            pool.wait_ge(ev("gain3_loaded"), 16)

        @block.scalar
        def _(act):
            def small_load(name, dst, src, **kw):
                act.dma_start(dst, src, **kw).then_inc(ev(name), 16)

            small_load("consts_loaded", cst, const_f32)
            small_load("consts_loaded", norm1_row.rearrange("p a b -> p (a b)"), norm1_g)
            small_load("consts_loaded", scale1_row.rearrange("p a b -> p (a b)"), b_mod[0:1, D:2 * D])
            small_load("consts_loaded", shift1_row, b_mod[0:1, 0:D])
            for t in range(2):
                small_load("x_loaded", xres[0:HALF, t, :], halves(x_prompt[0])[t])
                small_load("x_loaded", xres[HALF:P, t, :], halves(x_sample[0])[t])
            small_load("lb_loaded", lb_t[:, 0:4], hgrn_lb.rearrange("d l (h p) -> p (d l h)", p=P),
                       allow_slow_non_contiguous=True)
            act.wait_ge(ev("cond_loaded"), 32)
            nc.scalar.activation(gtmp[0:16, 0:P], cond, ACT.Sigmoid).then_inc(ev("cond_sig"), 1)

            act.wait_ge(ev("x_loaded"), 64)
            for t in range(2):
                nc.scalar.activation(rows[:, t, :], xres[:, t, :], ACT.Square, accum_out=ss[:, t:t + 1]).then_inc(ev("ss1"), 1)
            act.wait_ge(ev("ss1"), 2)
            act.wait_ge(ev("cols_set"), 4)
            nc.scalar.activation(rstd, ss, ACT.Sqrt, bias=eps, scale=1.0 / D).then_inc(ev("rms1"), 1)
            for t, q in ((0, 0), (1, 0), (0, 1)):
                act.wait_ge(ev("hT_ps"), 2 * q + t + 1)
                nc.scalar.copy(hT[:, 4 * q:4 * q + 4, :, HALF * t:HALF * (t + 1)],
                               B[2 + 4 * q + t].rearrange("p (k g u) -> p k g u", k=4, g=G)).then_inc(ev("hT_ready"), 1)
            act.wait_ge(ev("lb_shift"), 1)
            nc.scalar.activation(lb_t[:, 0:4], lb_t[:, 4:8], ACT.Exp).then_inc(ev("lb_exp"), 1)

            def win_wait(i):
                act.wait_ge(chunks_used, AT_WIN + i + 1)

            for d, i in enumerate((Z_F, Z_B)):
                win_wait(i)
                if d == 0:
                    act.wait_ge(ev("cond_silu"), 1)
                nc.scalar.activation(sig[:, d, :], B[i % 2], ACT.Sigmoid).then_inc(ev("sig_z"), 1)
                nc.scalar.activation(keyT[:, d, :], B[i % 2], ACT.Sigmoid, scale=-1.0).then_inc(ev("win_out"), 1)
            win_wait(H_Q)
            nc.scalar.copy(hqT, B[H_Q % 2]).then_inc(ev("win_out"), 1)
            act.wait_ge(ev("f_parts"), 1)
            nc.scalar.activation(cumT, cumT, ACT.Ln).then_inc(ev("ln_parts"), 1)
            nc.scalar.activation(sig, sig, ACT.Ln, scale=2.0 ** LN_SPLIT).then_inc(ev("ln_parts"), 1)
            win_wait(H_I)
            nc.scalar.copy(hi.rearrange("p g n -> p (g n)"), B[H_I % 2]).then_inc(ev("win_out"), 1)

            def copy_win(i):
                win_wait(i)
                if i in (K_0, Q_0, K_1, Q_1):
                    dst = (kT if i in (K_0, K_1) else qT)[:, 2 * (i >= K_1):2 * (i >= K_1) + 2]
                    nc.scalar.copy(dst, B[i % 2].rearrange("p (h g t) -> p h g t", h=2, g=G)).then_inc(ev("win_out"), 1)
                else:
                    dst = v[:, :, 256 * (i - V_0):256 * (i - V_0 + 1)]
                    nc.scalar.copy(dst, B[i % 2].rearrange("p (g n) -> p g n", g=G)).then_inc(ev("win_out"), 1)

            def level_exp(n):
                act.wait_ge(ev("lvl_diff"), n + 1)
                for d in range(2):
                    x = level_view(Dl[:, d, :], LEVELS[n])
                    for h in range(2):
                        query = h == 1 - d
                        nc.scalar.activation(x[:, :, h, :], x[:, :, h, :], ACT.Exp,
                                             scale=1.0 if query else -1.0).then_inc(ev("lvl_exp"), 1)

            copy_win(K_0)
            copy_win(Q_0)
            level_exp(0)
            copy_win(K_1)
            level_exp(1)
            copy_win(Q_1)
            act.wait_ge(ev("kout_ps"), 1)
            nc.scalar.copy(kout, B[6].rearrange("p (g n) -> p g n", g=2)).then_inc(ev("kout_ready"), 1)
            level_exp(2)
            copy_win(V_0)
            act.wait_ge(ev("nmx_p"), 1)
            for q in range(2):
                for h in range(HP):
                    n = HP * q + h
                    nc.scalar.activation(probs_p[:, q, h, :], B[4 + q][:, P * h:P * (h + 1)], ACT.Exp, scale=SCALE,
                                         bias=nmx[:, n:n + 1], accum_out=rsum[:, n:n + 1]).then_inc(ev("exp_p"), 1)
            level_exp(3)
            copy_win(V_1)
            level_exp(4)
            win_wait(G_V)
            gv = B[G_V % 2].rearrange("p (g n) -> p g n", g=G)
            nc.scalar.copy(rows[:, :, 768:1024], gv).then_inc(ev("gv_out"), 1)
            act.wait_ge(ev("gv_out"), 1)
            for g in range(G):
                nc.scalar.activation(gv[:, g, :], gv[:, g, :], ACT.Square, accum_out=ssg[:, g:g + 1]).then_inc(ev("ssg"), 1)
            act.wait_ge(ev("ssg"), 2)
            nc.scalar.activation(rsg, ssg, ACT.Sqrt, bias=eps, scale=1.0 / (GM * HD)).then_inc(ev("rmsg"), 1)
            for q in range(2):
                act.wait_ge(ev("pT_ps"), q + 1)
                nc.scalar.copy(pT_p[:, q, :], B[6 + q]).then_inc(ev("pT_ready"), 1)
            level_exp(5)
            level_exp(6)
            act.wait_ge(ev("end_diff"), 2)
            nc.scalar.activation(Dk, Dk, ACT.Exp, scale=-1.0).then_inc(ev("end_exp"), 1)
            for d in range(2):
                nc.scalar.activation(Dq[:, d], cum4[:, d, :, 1, :], ACT.Exp).then_inc(ev("end_exp"), 1)
            win_wait(H_G)
            nc.scalar.activation(gtmp, B[H_G % 2], ACT.Sigmoid).then_inc(ev("sig_g"), 1)

            act.wait_ge(ev("kst_ps"), 1)
            nc.scalar.copy(kstT.rearrange("p d h k -> p (d h k)"), B[1]).then_inc(ev("kst_ready"), 1)
            act.wait_ge(ev("score_s"), 1)
            for q in range(2):
                nc.scalar.mul(probs[:, q:NH:2, P:2 * P], B[6 + q].rearrange("p (h k) -> p h k", h=HP), SCALE).then_inc(ev("ctx_sc"), 1)
            act.wait_ge(ev("state_ps"), 1)
            nc.scalar.copy(state_out[0:HD, :], B[0][0:HD, :]).then_inc(ev("state_ready"), 1)
            act.wait_ge(ev("ms_o"), 1)
            nc.scalar.activation(rso, sso, ACT.Sqrt).then_inc(ev("rms_o"), 1)
            act.wait_ge(ev("nmx_s"), 1)
            for h in range(NH):
                nc.scalar.activation(probs[:, h, :], probs[:, h, :], ACT.Exp, bias=nmx_s[:, h:h + 1],
                                     accum_out=rsum_s[:, h:h + 1]).then_inc(ev("exp_s"), 1)

            def cat_out(n, bank):
                g, kh = n % 2, 1 - n // 2
                act.wait_ge(ev("cat_ps"), n + 1)
                nc.scalar.copy(catT[:, 4 * kh:4 * kh + 4, :, HALF * g:HALF * (g + 1)],
                               B[bank].rearrange("p (k t u) -> p k t u", k=4, t=2)).then_inc(ev("catT_ready"), 1)

            def probs_out(q):
                act.wait_ge(ev("sT_ps"), q + 1)
                dst = (sT_lo if q < 2 else sT_hi)[:, 512 * (q % 2):512 * (q % 2 + 1)]
                nc.scalar.copy(dst, B[4 + q % 2]).then_inc(ev("sT_ready"), 1)

            cat_out(0, 6)
            cat_out(1, 7)
            for q in range(4):
                probs_out(q)
            cat_out(2, 7)
            cat_out(3, 5)

            for t in range(2):
                act.wait_ge(ev("x1_ready"), 2 * t + 2)
                nc.scalar.activation(k_pool[:, D * t:D * (t + 1)], xres[:, t, :], ACT.Square, accum_out=ss2[:, t:t + 1]).then_inc(ev("ss2"), 1)
                act.wait_ge(ev("ss2"), t + 1)
                nc.scalar.activation(rs2[:, t:t + 1], ss2[:, t:t + 1], ACT.Sqrt, bias=eps, scale=1.0 / D).then_inc(ev("rms2"), 1)
            for t in range(2):
                for q in range(2):
                    act.wait_ge(ev("h2T_ps"), 2 * t + q + 1)
                    nc.scalar.copy(h2T[:, 4 * q:4 * q + 4, t, :],
                                   B[2 + q].rearrange("p (k u) -> p k u", k=4)).then_inc(ev("h2T_ready"), 1)
            act.wait_ge(ev("nv1"), 1)
            for t in range(2):
                nc.scalar.activation(ex[:, t, :], lg[:, t, :], ACT.Exp, bias=rsm[:, 16 + t:17 + t]).then_inc(ev("r_exp"), 1)
            act.wait_ge(ev("rgT_ps"), 1)
            nc.scalar.copy(rgT, B[1][0:NE, :]).then_inc(ev("rgT_ready"), 1)

            def tokens_out(count):
                act.wait_ge(ev("xe_ps"), count + 1)
                nc.scalar.copy(xe.rearrange("p k s -> p (k s)"), B[3]).then_inc(ev("xe_ready"), 1)

            def sigmoid_step(count):
                act.wait_ge(ev("gate_min"), count + 1)
                nc.scalar.activation(sigb, actb, ACT.Sigmoid, scale=ALPHA).then_inc(ev("gate_sig"), 1)

            def down_steps(count):
                act.wait_ge(ev("aT_ps"), count + 1)
                nc.scalar.copy(aT.rearrange("p c s -> p (c s)"), B[2]).then_inc(ev("aT_ready"), 1)
                act.wait_ge(chunks_used, used(11, count))
                nc.scalar.copy(ysb, B[2]).then_inc(ev("y_sb"), 1)

            act.wait_ge(ev("mixer_freed"), 1)
            tokens_out(0)
            with act.Fori(0, NE) as e:
                sigmoid_step(e)
                tokens_out(e + 1)
                down_steps(e)
            act.wait_ge(ev("over_list"), 1)
            n_over = act.value_load(small_i[0:1, 16:17], min_val=0, max_val=MAX_OVER)
            with act.If(n_over > 0):
                with act.Fori(0, MAX_OVER) as j:
                    with act.If(n_over > j):
                        tokens_out(j + (NE + 1))
                        sigmoid_step(j + NE)
                        down_steps(j + NE)

            nc.scalar.activation(rsf[:, 0:1], eps, ACT.Sqrt).then_inc(ev("root_table"), 1)
            act.wait_ge(ev("root_table"), 1)
            for t in range(2):
                act.wait_ge(ev("x2_ready"), 2 * t + 2)
                nc.scalar.activation(rows[:, t, :], xres[:, t, :], ACT.Square, accum_out=ssf[:, t:t + 1]).then_inc(ev("ssf"), 1)
                act.wait_ge(ev("ssf"), t + 1)
                nc.scalar.activation(rsf[:, t:t + 1], ssf[:, t:t + 1], ACT.Sqrt, bias=eps, scale=1.0 / D).then_inc(ev("rmsf"), 1)

        @block.vector
        def _(dve):
            ch = Chain(dve, "dve_steps")
            V = nc.vector

            dve.wait_ge(ev("cond_sig"), 1)
            V.tensor_tensor(cond, cond, gtmp[0:16, 0:P], ALU.mult).then_inc(ev("cond_silu"), 1)
            dve.wait_ge(ev("consts_loaded"), 64)
            V.tensor_copy(flip, ident[:, ::-1]).then_inc(ev("flip_ready"), 1)
            dve.wait_ge(ev("condT_ps"), 1)
            dve.wait_ge(ev("cols_set"), 4)
            V.tensor_copy(condT[:, :, 0:G], B[0][:, 0:16].rearrange("p (r k) -> p k r", r=G)).then_inc(ev("condT_ready"), 1)

            def mod_part(n):
                dve.wait_ge(chunks_used, mod_at(n) + 2)
                if n >= 2:
                    dve.wait_ge(ev("mod_bc"), n - 1)
                V.tensor_copy(mod_part_buf(n), B[mod_bank(n)]).then_inc(ev("mod_part"), 1)

            def mod_out(n):
                dve.wait_ge(ev("mod_bc"), n + 1)
                m, cols = MODS[n // 2], slice(512 * (n % 2), 512 * (n % 2 + 1))
                src = B[bc_bank(n)]
                if m == 1:
                    V.scalar_tensor_tensor(gsc[:, cols], src, 1.0, norm1_sb[n], ALU.add, ALU.mult).then_inc(ev("mod_out"), 1)
                elif m == 4:
                    ch.step(V.scalar_tensor_tensor(gsc[:, cols], src, 1.0, gsc[:, cols], ALU.add, ALU.add))
                    V.tensor_tensor(gsc[:, cols], gsc[:, cols], gain[:, cols], ALU.mult).then_inc(ev("mod_out"), 1)
                else:
                    dst = {3: shf, 2: g1, 5: g2}[m]
                    V.tensor_tensor(dst[:, cols], src, dst[:, cols], ALU.add).then_inc(ev("mod_out"), 1)

            def add_shift(n):
                dve.wait_ge(ev("mod_bc"), n + 1)
                cols = slice(512 * (n % 2), 512 * (n % 2 + 1))
                for t in range(2):
                    V.tensor_tensor(rows[:, t, cols], rows[:, t, cols], B[bc_bank(n)], ALU.add).then_inc(ev("h_ready"), 1)

            norm1_sb = [gain[:, 512 * half:512 * (half + 1)] for half in range(2)]
            dve.wait_ge(ev("gain_ps"), 2)
            for half in range(2):
                ch.step(V.tensor_copy(norm1_sb[half], B[6 + half]))
            mod_part(0)
            mod_part(1)
            mod_out(0)
            mod_out(1)
            dve.wait_ge(ev("rms1"), 1)
            ch.step(V.reciprocal(rstd, rstd))
            dve.wait_ge(ev("mod_out"), 2)
            mod_part(2)
            for t in range(2):
                V.scalar_tensor_tensor(rows[:, t, :], xres[:, t, :], rstd[:, t:t + 1], gsc, ALU.mult, ALU.mult).then_inc(ev("rows_scaled"), 1)
            dve.wait_ge(ev("rows_scaled"), 2)
            mod_part(3)
            add_shift(2)
            add_shift(3)

            dve.wait_ge(ev("lb_loaded"), 16)
            ch.step(V.tensor_tensor(lb_t[:, 4:8], lb_t[:, 0:4], lb_t[:, 0:4], ALU.max))
            V.tensor_tensor(lb_t[:, 4:8], lb_t[:, 0:4], lb_t[:, 4:8], ALU.subtract).then_inc(ev("lb_shift"), 1)
            dve.wait_ge(ev("hT_ps"), 4)
            V.tensor_copy(hT[:, 4:8, :, HALF:P], B[7].rearrange("p (k g u) -> p k g u", k=4, g=G)).then_inc(ev("hT_ready"), 1)
            dve.wait_ge(ev("lb_exp"), 1)
            ch.step(V.reciprocal(lb_t[:, 4:8], lb_t[:, 0:4]))
            ch.step(V.tensor_tensor(lb_t[:, 4:8], lb_t[:, 0:4], lb_t[:, 4:8], ALU.mult))
            ch.step(V.tensor_tensor(lbT, lb_t[:, 4:8], lb_t[:, 4:8], ALU.subtract))
            ch.step(V.tensor_scalar(omlT, lbT, -1.0, 1.0, ALU.mult, ALU.add))
            dve.wait_ge(ev("masks_loaded"), 16)
            V.tensor_copy(masks.rearrange("p m t -> p (m t)"), k_pool).then_inc(ev("masks_ready"), 1)
            V.memset(biasN, NEG).then_inc(ev("biasN_neg"), 1)

            for d in range(2):
                dve.wait_ge(ev("win_out"), d + 1)
                dve.wait_ge(ev("sig_z"), d + 1)
                for h in range(RP):
                    n, cols = 2 * d + h, slice(256 * h, 256 * (h + 1))
                    V.tensor_scalar(sig[:, d, cols], sig[:, d, cols], omlT[:, n:n + 1], lbT[:, n:n + 1],
                                    ALU.mult, ALU.add).then_inc(ev("f_ready"), 1)
                    V.tensor_scalar(keyT[:, d, cols], keyT[:, d, cols], omlT[:, n:n + 1], None, ALU.mult).then_inc(ev("key_ready"), 1)
            dve.wait_ge(ev("f_ready"), 4)
            ch.step(V.tensor_scalar(cumT, sig, 2.0 ** -LN_SPLIT, None, ALU.max))
            V.tensor_scalar(sig, sig, F_FLOOR, 2.0 ** -LN_SPLIT, ALU.max, ALU.min).then_inc(ev("f_parts"), 1)
            dve.wait_ge(ev("early_ps"), 3)
            V.tensor_copy(ckT.rearrange("p h l -> p (h l)"), B[6]).then_inc(ev("early_out"), 1)
            V.tensor_copy(wsT.rearrange("p g t -> p (g t)"), B[7]).then_inc(ev("early_out"), 1)
            V.tensor_copy(gbT, B[2][:, 0:GM]).then_inc(ev("early_out"), 1)
            dve.wait_ge(ev("flip_ps"), 1)
            dve.wait_ge(ev("masks_ready"), 1)
            dve.wait_ge(ev("biasN_neg"), 1)
            for q in range(2):
                V.copy_predicated(biasN[:, HP * q:HP * (q + 1), :], masks[:, M_WINDOW, :].unsqueeze(1).to_broadcast([P, HP, P]),
                                  B[4 + q].rearrange("p (h k) -> p h k", h=HP)).then_inc(ev("biasN_ready"), 1)
            ch.step(V.memset(Dl[:, 0, :], 1.0))
            ch.step(V.memset(Dl[:, 0, 0:512:P], 0.0))
            dve.wait_ge(ev("ln_parts"), 2)
            ch.step(V.tensor_tensor(sig, sig, cumT, ALU.add))
            V.tensor_tensor_scan(cumT[:, 0, :], Dl[:, 0, :], sig[:, 0, :], 0.0, ALU.mult, ALU.add).then_inc(ev("scan_done"), 1)
            V.tensor_tensor_scan(cumT[:, 1, ::-1], Dl[:, 0, :], sig[:, 1, ::-1], 0.0, ALU.mult, ALU.add).then_inc(ev("scan_done"), 1)
            dve.wait_ge(ev("key_ready"), 4)
            dve.wait_ge(ev("k_zero"), 1)
            V.tensor_tensor(Kl[:, 0, :], keyT[:, 0, :], keyT[:, 1, :], ALU.add).then_inc(ev("ksum_ready"), 1)
            dve.wait_ge(ev("scan_done"), 2)

            def level_diff(n):
                w = LEVELS[n]
                for d in range(2):
                    b = cumT[:, d, :].rearrange("p (n m) -> p n m", m=2 * w)
                    edge = b[:, :, w - 1:w] if d == 0 else b[:, :, w:w + 1]
                    ins = V.tensor_tensor(Dl[:, d, :].rearrange("p (n m) -> p n m", m=2 * w), b,
                                          edge.to_broadcast([P, 256 // w, 2 * w]), ALU.subtract)
                ins.then_inc(ev("lvl_diff"), 1)

            def level_qk(n, d):
                w = LEVELS[n]
                dve.wait_ge(ev("lvl_exp"), 4 * n + 2 * d + 2)
                dve.wait_ge(ev("lvl_mm"), max(1, 2 * n + d))
                if n == 0:
                    dve.wait_ge(ev("k_zero"), 2)
                ex_ = level_view(Dl[:, d, :], w)
                for q in range(2):
                    hd = slice(HD * q, HD * (q + 1))
                    V.tensor_tensor(Qpair[hd, d, :, q, :].rearrange("p a (n m) -> p a n m", m=w),
                                    Dl[hd, d, :].rearrange("p (a n h m) -> p a n h m", a=4, h=2, m=w)[:, :, :, 1 - d, :],
                                    hqT[hd, :].rearrange("p (a n h m) -> p a n h m", a=4, h=2, m=w)[:, :, :, 1 - d, :],
                                    ALU.mult).then_inc(ev("lvl_qk"), 1)
                V.tensor_tensor(level_view(Kl[:, d, :], w)[:, :, d, :], ex_[:, :, d, :],
                                level_view(keyT[:, d, :], w)[:, :, d, :], ALU.mult).then_inc(ev("lvl_qk"), 1)

            def diagonal_store():
                dve.wait_ge(ev("lvl_mm"), 1)
                for q in range(2):
                    V.tensor_copy(AT[:, q, :], B[2 + q]).then_inc(ev("lvl_store"), 1)

            def level_store(n, d):
                w = LEVELS[n]
                dve.wait_ge(ev("lvl_mm"), 2 * n + d + 2)
                dve.wait_ge(ev("lvl_store"), 4 * n + 2 * d + 2)
                for q in range(2):
                    V.copy_predicated(AT[:, q, :].rearrange("p (a n h m) -> p a n h m", a=4, h=2, m=w)[:, :, :, 1 - d, :],
                                      level_view(masks[:, 7 * d + n, :], w)[:, :, 1 - d, :].unsqueeze(1).to_broadcast([P, 4, 64 // w, w]),
                                      B[2 + d].rearrange("p (a q n m) -> p a q n m", a=4, q=2, m=w)[:, :, q]).then_inc(ev("lvl_store"), 1)

            def hgrn_level(n, d):
                level_qk(n, d)
                if d:
                    dve.wait_ge(ev("lvl_qk"), 6 * (n + 1))
                    if n + 1 < len(LEVELS):
                        level_diff(n + 1)
                    else:
                        for dd in range(2):
                            edge = cum4[:, dd, :, 0, P - 1:P] if dd == 0 else cum4[:, dd, :, 0, 0:1]
                            V.tensor_tensor(Dk[:, dd], cum4[:, dd, :, 0, :], edge.to_broadcast([P, RP, P]), ALU.subtract).then_inc(ev("end_diff"), 1)

            level_diff(0)
            hgrn_level(0, 0)
            hgrn_level(0, 1)
            diagonal_store()
            for n in range(1, len(LEVELS)):
                for d in range(2):
                    level_store(n - 1, d)
                    hgrn_level(n, d)
                if n == 2:
                    dve.wait_ge(ev("score_p"), 1)
                    for q in range(2):
                        V.tensor_reduce(mx[:, HP * q:HP * (q + 1)], B[4 + q].rearrange("p (h k) -> p h k", h=HP), AX.X, ALU.max).then_inc(ev("mx_p"), 1)
                    dve.wait_ge(ev("mx_p"), 2)
                    V.tensor_scalar(nmx, mx, -SCALE, None, ALU.mult).then_inc(ev("nmx_p"), 1)
                if n == 4:
                    dve.wait_ge(ev("exp_p"), NH)
                    ch.step(V.reciprocal(rinv, rsum))
                if n == 5:
                    dve.wait_ge(ev("rmsg"), 1)
                    ch.step(V.reciprocal(rsg, rsg))
                    dve.wait_ge(ev("mixer_loaded"), 144)
                    for g in range(G):
                        V.scalar_tensor_tensor(rows[:, g, 768:1024], rows[:, g, 768:1024], rsg[:, g:g + 1], vng,
                                               ALU.mult, ALU.mult).then_inc(ev("vg_ready"), 1)
                    dve.wait_ge(ev("att_p_ps"), 1)
                    V.tensor_tensor(rows[:, 0, 0:512].rearrange("p (h q d) -> p h q d", h=HP, q=2), B[4].rearrange("p (h q d) -> p h q d", h=HP, q=2),
                                    rinv.rearrange("p (q h) -> p h q", q=2).unsqueeze(3).to_broadcast([P, HP, 2, HD]), ALU.mult)
                    dve.wait_ge(ev("z_ps"), 1)
                    for g in range(GM):
                        V.tensor_scalar(rows[:, :, 768 + HD * g:768 + HD * (g + 1)], B[5][:, P * g:P * (g + 1)].rearrange("p (r n) -> p r n", r=G),
                                        gbT[:, g:g + 1], None, ALU.add).then_inc(ev("zb_ready"), 1)
                    dve.wait_ge(ev("zb_ready"), 4)
                    V.tensor_tensor(rows[:, :, 768:1024], rows[:, :, 768:1024], B[G_U % 2].rearrange("p (g n) -> p g n", g=G),
                                    ALU.mult).then_inc(ev("gmlp_ready"), 1)
            level_store(6, 0)
            dve.wait_ge(ev("end_exp"), 3)
            dve.wait_ge(ev("lvl_mm"), 15)
            for d in range(2):
                V.tensor_tensor(Kend[:, d], Dk[:, d], key4[:, d, :, 0, :], ALU.mult).then_inc(ev("end_ready"), 1)
            for d in range(2):
                V.tensor_tensor(Qend[:, d], Dq[:, d], hq4[:, :, 1, :], ALU.mult).then_inc(ev("end_ready"), 1)
            level_store(6, 1)
            dve.wait_ge(ev("score_s"), 1)
            dve.wait_ge(ev("kst_ps"), 1)
            dve.wait_ge(ev("biasN_ready"), 2)
            for q in range(2):
                V.scalar_tensor_tensor(probs[:, q:NH:2, 0:P], B[4 + q].rearrange("p (h k) -> p h k", h=HP), SCALE,
                                       biasN[:, q:NH:2, :], ALU.mult, ALU.add).then_inc(ev("local_sc"), 1)
            dve.wait_ge(ev("sig_g"), 1)
            dve.wait_ge(ev("kout_stored"), 16)
            V.tensor_tensor(rows[:, :, 512:768], gtmp.rearrange("p (g n) -> p g n", g=G),
                            B[H_G % 2].rearrange("p (g n) -> p g n", g=G), ALU.mult).then_inc(ev("silu_g"), 1)
            dve.wait_ge(ev("local_sc"), 2)
            dve.wait_ge(ev("ctx_sc"), 2)
            ch.step(V.tensor_reduce(mx_s, probs, AX.X, ALU.max))
            V.tensor_scalar(nmx_s, mx_s, -1.0, None, ALU.mult).then_inc(ev("nmx_s"), 1)
            mod_part(4)

            dve.wait_ge(ev("o_ps"), 1)
            o_sb = gtmp.rearrange("p (g h n) -> p g h n", g=G, h=RH)
            dve.wait_ge(ev("silu_g"), 1)
            for q in range(2):
                src = B[2 + q].rearrange("p (g h n) -> p g h n", g=G, h=4)[:, :, 0:RP, :]
                V.tensor_copy(o_sb[:, :, q:RH:2, :], src).then_inc(ev("o_out"), 1)
            dve.wait_ge(ev("o_out"), 2)
            o_rows = gtmp.rearrange("p (n v) -> p n v", v=HD)
            o_sq = keyT[:, 0, :].rearrange("p (n v) -> p n v", v=HD)
            ch.step(V.tensor_tensor(o_sq, o_rows, o_rows, ALU.mult))
            ch.step(V.tensor_reduce(sso, o_sq, AX.X, ALU.add))
            V.tensor_scalar(sso, sso, 1.0 / HD, EPS, ALU.mult, ALU.add).then_inc(ev("ms_o"), 1)
            mod_part(5)
            mod_out(4)
            mod_out(5)
            dve.wait_ge(ev("rms_o"), 1)
            ch.step(V.reciprocal(rso, rso))
            ch.step(V.tensor_tensor(o_rows, o_rows, rso.unsqueeze(2).to_broadcast([P, 8, HD]), ALU.mult))
            ch.step(V.tensor_tensor(o_rows, o_rows, ong.unsqueeze(1).to_broadcast([P, 8, HD]), ALU.mult))
            V.tensor_tensor(rows[:, :, 512:768], rows[:, :, 512:768], gtmp.rearrange("p (g n) -> p g n", g=G),
                            ALU.mult).then_inc(ev("hgrn_ready"), 1)
            dve.wait_ge(ev("norm2_loaded"), 48)
            mod_part(6)
            mod_part(7)
            mod_out(6)
            mod_out(7)
            dve.wait_ge(ev("exp_s"), NH)
            ch.step(V.reciprocal(rinv_s, rsum_s))
            mod_part(8)
            mod_part(9)
            mod_out(8)
            mod_out(9)
            dve.wait_ge(ev("att_s_ps"), 1)
            V.tensor_tensor(rows[:, 1, 0:512].rearrange("p (h d) -> p h d", h=NH), B[6].rearrange("p (h d) -> p h d", h=NH),
                            rinv_s.unsqueeze(2).to_broadcast([P, NH, HD]), ALU.mult).then_inc(ev("att_s"), 1)

            dve.wait_ge(ev("caches_stored"), 48)
            for t in range(2):
                if t == 0:
                    dve.wait_ge(ev("wout_ps"), 1)
                else:
                    dve.wait_ge(chunks_used, AT_MODG2)
                for half in range(2):
                    cols = slice(512 * half, 512 * (half + 1))
                    ch.step(V.tensor_tensor(xtmp[half], B[2 * t + half], g1[:, cols], ALU.mult))
                    V.tensor_tensor(xres[:, t, cols], xres[:, t, cols], xtmp[half], ALU.add).then_inc(ev("x1_ready"), 1)
                if t == 0:
                    dve.wait_ge(ev("mod_out"), 8)
                    dve.wait_ge(ev("cat_ps"), 4)
                dve.wait_ge(ev("x1_ready"), 2 * t + 2)
                V.tensor_tensor(rows[:, t, :], xres[:, t, :], gsc, ALU.mult).then_inc(ev("rows_scaled"), 1)
            for t in range(2):
                dve.wait_ge(ev("rms2"), t + 1)
                ch.step(V.reciprocal(rs2[:, t:t + 1], rs2[:, t:t + 1]))
                dve.wait_ge(ev("rows_scaled"), t + 3)
                V.scalar_tensor_tensor(rows[:, t, :], rows[:, t, :], rs2[:, t:t + 1], shf, ALU.mult, ALU.add).then_inc(ev("h2_ready"), 1)
            mod_part(10)
            mod_part(11)
            V.memset(rank, 0.0).then_inc(ev("rank_zero"), 1)
            V.memset(csm, 1.0).then_inc(ev("csm_set"), 1)
            dve.wait_ge(ev("csm_set"), 1)
            ch.step(V.memset(csm[:, 1, 0:1], 0.0))
            V.memset(ysb, 0.0).then_inc(ev("y_sb"), 1)

            both = [P, 2, NE]
            dve.wait_ge(ev("logits_ps"), 1)
            logits = B[0][:, 0:2 * NE].rearrange("p (t e) -> p t e", t=2)
            V.tensor_copy(lg, logits).then_inc(ev("lg_ready"), 1)
            for t in range(2):
                V.max(rsm[:, 8 * t:8 * t + 8], logits[:, t, :]).then_inc(ev("lg_ready"), 1)
            dve.wait_ge(ev("lg_ready"), 3)
            V.tensor_scalar(rsm[:, 16:18], rsm[:, 0:16:8], -1.0, None, ALU.mult).then_inc(ev("nv1"), 1)
            v4 = rsm[:, 3:16:8].unsqueeze(2).to_broadcast(both)
            ch.step(V.tensor_tensor(eqm, lg, v4, ALU.is_equal))
            ch.step(V.tensor_tensor(msk, lg, v4, ALU.is_gt))
            V.tensor_tensor_scan(mask4[:, 0, 0:2, :].rearrange("p r e -> p (r e)"), csm.rearrange("p t e -> p (t e)"),
                                 eqm.rearrange("p t e -> p (t e)"), 0.0, ALU.mult, ALU.add).then_inc(ev("ties"), 1)
            ch.step(V.tensor_reduce(rsm[:, 18:20], msk, AX.X, ALU.add))
            dve.wait_ge(ev("ties"), 1)
            ch.step(V.tensor_tensor(csm, mask4[:, 0, 0:2, :], rsm[:, 18:20].unsqueeze(2).to_broadcast(both), ALU.add))
            ch.step(V.scalar_tensor_tensor(eqm, csm, float(TOP_K), eqm, ALU.is_le, ALU.mult))
            ch.step(V.tensor_tensor(msk, msk, eqm, ALU.add))
            V.tensor_copy(mask4, msk.unsqueeze(2).to_broadcast([P, 2, CHUNKS, NE])).then_inc(ev("mask_ready"), 1)
            dve.wait_ge(ev("r_exp"), 2)
            ch.step(V.tensor_tensor(ex, ex, msk, ALU.mult))
            ch.step(V.tensor_reduce(rsm[:, 22:24], ex, AX.X, ALU.add))
            ch.step(V.reciprocal(rsm[:, 24:26], rsm[:, 22:24]))
            V.tensor_tensor(gate, ex, rsm[:, 24:26].unsqueeze(2).to_broadcast(both), ALU.mult).then_inc(ev("gate_ready"), 1)
            mod_out(10)
            dve.wait_ge(ev("rank_zero"), 1)
            dve.wait_ge(ev("rank_ps"), 1)
            V.tensor_tensor(rank[:, :, 0:NE], B[1][:, 0:2 * NE].rearrange("p (t e) -> p t e", t=2), msk, ALU.mult).then_inc(ev("rank_ready"), 1)
            V.tensor_tensor(flag, B[1][:, 64:65], cst[:, C_THR:C_THR + 1], ALU.is_gt).then_inc(ev("flag_ready"), 1)

            def route(e, buf, off=None):
                V.tensor_copy(pick[:, buf, :], identE[:, bass.ds(e, 1)].to_broadcast([NE, P]))
                for t in range(2):
                    r = rank[:, t, bass.ds(e, 1)]
                    if off is None:
                        ins = V.tensor_scalar(Ptok[:, t, :], cst[:, C_SLOTROW:C_SLOTROW + CAP], r, None, ALU.is_equal)
                    else:
                        ins = V.tensor_scalar(Ptok[:, t, :], cst[:, C_SLOTROW:C_SLOTROW + CAP], off, r, ALU.add, ALU.is_equal)
                ins.then_inc(ev("route_ready"), 1)

            def slot_gates(count, buf, off=None):
                dve.wait_ge(ev("bc_ps"), count + 1)
                scol = cst[:, C_SLOTCOL:C_SLOTCOL + 1]
                if off is None:
                    ch.step(V.tensor_scalar(gT[:, buf, :], B[3][:, 0:256], scol, None, ALU.is_equal))
                else:
                    ch.step(V.tensor_scalar(gT[:, buf, :], B[3][:, 0:256], off, scol, ALU.subtract, ALU.is_equal))
                V.tensor_tensor(gT[:, buf, :], gT[:, buf, :], B[3][:, 256:512], ALU.mult).then_inc(ev("gT_ready"), 1)

            def gate_step(count):
                dve.wait_ge(chunks_used, used(3, count))
                V.tensor_scalar(actb, B[0], LIMIT, None, ALU.min).then_inc(ev("gate_min"), 1)

            def up_step(count):
                dve.wait_ge(chunks_used, used(7, count))
                V.tensor_scalar(upb, B[1], -LIMIT, LIMIT, ALU.max, ALU.min).then_inc(ev("up_clip"), 1)
                dve.wait_ge(ev("up_clip"), count + 1)
                ch.step(V.scalar_tensor_tensor(upb, upb, 1.0, actb, ALU.add, ALU.mult))
                dve.wait_ge(ev("gate_sig"), count + 1)
                V.tensor_tensor(ab, upb, sigb, ALU.mult).then_inc(ev("a_ready"), 1)

            dve.wait_ge(ev("idE_ready"), 1)
            dve.wait_ge(ev("rank_ready"), 1)
            route(0, 0)
            dve.wait_ge(ev("pos_ps"), 1)
            dve.wait_ge(ev("flag_ready"), 1)
            ch.step(V.tensor_copy(posn, B[0][:, 64:65]))
            V.tensor_scalar(onehot, cst[:, C_IOTA:C_IOTA + 16], posn, flag, ALU.is_equal, ALU.mult).then_inc(ev("onehot_ready"), 1)
            mod_out(11)
            V.memset(gT[:, 1, :], 0.0).then_inc(ev("mixer_freed"), 1)
            slot_gates(0, 0)
            dve.wait_ge(ev("list_ps"), 1)
            ch.step(V.tensor_copy(offb, B[0][:, 128:144]))
            ch.step(V.tensor_copy(small_i[0:1, 0:16], B[0][0:1, 144:160]))
            V.tensor_copy(small_i[0:1, 16:17], B[0][0:1, 160:161]).then_inc(ev("over_list"), 1)
            with dve.Fori(0, NE // 2) as i:
                ch.enter(i, 4)
                for u in range(2):
                    e = i * 2 + u
                    gate_step(e)
                    dve.wait_ge(ev("xe_ps"), e + 1)
                    route(e + 1, 1 - u)
                    slot_gates(e + 1, 1 - u)
                    up_step(e)
            ch.leave(NE // 2)
            dve.wait_ge(ev("over_list"), 1)
            n_over = dve.value_load(small_i[0:1, 16:17], min_val=0, max_val=MAX_OVER)
            with dve.If(n_over > 0):
                with dve.Fori(0, MAX_OVER) as j:
                    with dve.If(n_over > j):
                        ch.enter(j, 2)
                        e = dve.value_load(small_i[0:1, bass.ds(j, 1)], min_val=0, max_val=NE - 1)
                        off = offb[:, bass.ds(j, 1)]
                        dve.wait_ge(ev("combined"), j + (NE + 1))
                        route(e, 0, off)
                        slot_gates(j + (NE + 1), 0, off)
                        gate_step(j + NE)
                        up_step(j + NE)

            fin = Chain(dve, "dve_last_steps")
            dve.wait_ge(ev("moe_done"), 1)
            dve.wait_ge(ev("mod_out"), 10)
            for t in range(2):
                for half in range(2):
                    cols = slice(512 * half, 512 * (half + 1))
                    buf = k_pool[:, 512 * (2 * t + half):512 * (2 * t + half + 1)]
                    fin.step(V.tensor_tensor(buf, B[4 + 2 * t + half], g2[:, cols], ALU.mult))
                    V.tensor_tensor(xres[:, t, cols], xres[:, t, cols], buf, ALU.add).then_inc(ev("x2_ready"), 1)
            dve.wait_ge(ev("gain3_loaded"), 16)
            for t in range(2):
                dve.wait_ge(ev("rmsf"), t + 1)
                fin.step(V.reciprocal(rsf[:, t:t + 1], rsf[:, t:t + 1]))
                V.scalar_tensor_tensor(xres[:, t, :], xres[:, t, :], rsf[:, t:t + 1], gain, ALU.mult, ALU.mult).then_inc(ev("y_ready"), 1)

        @block.tensor
        def _(pe):
            mm, tr = nc.tensor.matmul, nc.tensor.transpose
            pe.wait_ge(ev("consts_loaded"), 64)
            pe.wait_ge(ev("cond_silu"), 1)
            tr(B[0][:, 0:16], cond, ident[0:16, 0:16]).then_inc(ev("condT_ps"), 1)
            pe.wait_ge(ev("cols_set"), 4)
            for half in range(2):
                mm(B[6 + half], ones_rows, norm1_row[:, half, :], start=True, stop=True).then_inc(ev("gain_ps"), 1)
            for half in range(2):
                mm(B[2 + half], ones_rows, scale1_row[:, half, :], start=True, stop=False)
            for half in range(2):
                mm(B[4 + half], ones_rows, shift1_row[:, 512 * half:512 * (half + 1)], start=True, stop=False)
            pe.wait_ge(ev("condT_ready"), 1)

            def slot_wait(n):
                pe.wait_ge(slot_loaded[n % RING], 16 * (n // RING + 1))

            def mod_sums(n):
                if n in (2, 3):
                    pe.wait_ge(ev("mod_part"), n - 1)
                elif n in (8, 9):
                    pe.wait_ge(ev("mod_out"), n - 3)
                at = mod_at(n)
                for r in range(2):
                    slot_wait(at + r)
                    w = ring[:, (at + r) % RING, :].rearrange("p (k n) -> p k n", k=4)
                    for j in range(4):
                        ins = mm(B[mod_bank(n)][32 * j:32 * (j + 1), :], condT[:, 4 * r + j, :], w[:, j, :],
                                 start=r == 0, stop=r == 1, tile_position=(0, 32 * j))
                    ins.then_inc(chunks_used, 1)

            def mod_spread(n):
                pe.wait_ge(ev("mod_part"), n + 1)
                mm(B[bc_bank(n)], cst[:, C_MODSEL:C_MODSEL + P], mod_part_buf(n), start=n >= 4, stop=True).then_inc(ev("mod_bc"), 1)

            def h_transpose(q):
                for t in range(2):
                    pe.wait_ge(ev("h_ready"), 2 * q + t + 1)
                    for k in range(4):
                        ins = tr(B[2 + 4 * q + t][:, P * k:P * (k + 1)], rows[:, t, P * (4 * q + k):P * (4 * q + k + 1)], ident)
                    ins.then_inc(ev("hT_ps"), 1)

            mod_sums(0)
            mod_sums(1)
            mod_spread(0)
            mod_spread(1)
            mod_sums(2)
            mod_spread(2)
            mod_sums(3)
            h_transpose(0)
            mod_spread(3)
            h_transpose(1)

            def keep_clock(n, bank):
                for _ in range(n):
                    mm(bank, ident, cst[:, 0:512], start=True, stop=True)

            def project(i, between=None):
                if i == H_G:
                    pe.wait_ge(ev("ssg"), 2)
                elif i >= 2:
                    pe.wait_ge(ev("win_out"), i - 1)
                n = AT_WIN + i
                slot_wait(n)
                w = ring[:, n % RING, :].rearrange("p (k n) -> p k n", k=KT)
                bank = B[i % 2]
                for r in range(2):
                    if r and between:
                        between()
                    for k in range(KT):
                        if i in (Z_F, Z_B, H_Q, K_0, K_1, Q_0, Q_1):
                            ins = mm(bank[:, 256 * r:256 * (r + 1)], w[:, k, P * r:P * (r + 1)],
                                     hT[:, k, :, :], start=k == 0, stop=k == KT - 1)
                        else:
                            ins = mm(bank[:, 256 * r:256 * (r + 1)], hT[:, k, r, :], w[:, k, :],
                                     start=k == 0, stop=k == KT - 1)
                ins.then_inc(chunks_used, 1)

            def diagonal():
                pe.wait_ge(ev("ksum_ready"), 1)
                pe.wait_ge(ev("win_out"), H_Q + 1)
                for m in range(4):
                    for q in range(2):
                        hd = slice(HD * q, HD * (q + 1))
                        ins = mm(B[2 + q][:, P * m:P * (m + 1)], Kl[hd, 0, P * m:P * (m + 1)], hqT[hd, P * m:P * (m + 1)],
                                 start=True, stop=True)
                ins.then_inc(ev("lvl_mm"), 1)

            def level(n, d):
                pe.wait_ge(ev("lvl_qk"), 6 * n + 3 * d + 3)
                pe.wait_ge(ev("lvl_store"), max(2, 4 * n + 2 * d))
                for m in range(4):
                    ins = mm(B[2 + d][:, P * m:P * (m + 1)], Kl[:, d, P * m:P * (m + 1)], Qpair[:, d, m],
                             start=True, stop=True)
                ins.then_inc(ev("lvl_mm"), 1)

            def project_with_levels(i, n):
                project(i, between=lambda: level(n - 1, 1))
                level(n, 0)

            def scores(bank, g, keys):
                for h in range(HP):
                    for q in range(2):
                        hd = slice(HD * q, HD * (q + 1))
                        ins = mm(B[bank + q][:, P * h:P * (h + 1)], qT[hd, h, g, :], keys(hd, h), start=True, stop=True)
                return ins

            pe.wait_ge(ev("hT_ready"), 4)
            for i in (Z_F, Z_B, H_Q, H_I):
                project(i)
            pe.wait_ge(ev("early_loaded"), 48)
            for h in range(HP):
                ins = tr(B[6][:, P * h:P * (h + 1)], ck[:, P * h:P * (h + 1)], ident)
            ins.then_inc(ev("early_ps"), 1)
            for g in range(GM):
                ins = tr(B[7][:, P * g:P * (g + 1)], ws[:, g, :], ident)
            ins.then_inc(ev("early_ps"), 1)
            tr(B[2][:, 0:GM], gb_rows, ident[0:GM, 0:GM]).then_inc(ev("early_ps"), 1)
            pe.wait_ge(ev("bias_raw_loaded"), 64)
            pe.wait_ge(ev("flip_ready"), 1)
            for q in range(2):
                ins = mm(B[4 + q], flip, bias_raw[:, HP * q:HP * (q + 1), :], start=True, stop=True)
            ins.then_inc(ev("flip_ps"), 1)
            project(K_0)
            project(Q_0)
            pe.wait_ge(ev("early_out"), 3)
            diagonal()
            project(K_1)
            level(0, 0)
            project_with_levels(Q_1, 1)
            pe.wait_ge(ev("win_out"), K_1 + 1)
            for h in range(HP):
                ins = tr(B[6][:, P * h:P * (h + 1)], kT[:, h, 0, :], ident)
            ins.then_inc(ev("kout_ps"), 1)
            project_with_levels(V_0, 2)
            pe.wait_ge(ev("biasN_ready"), 2)
            pe.wait_ge(ev("win_out"), Q_1 + 1)
            scores(4, 0, lambda hd, h: kT[hd, h, 0, :]).then_inc(ev("score_p"), 1)
            project_with_levels(V_1, 3)
            project_with_levels(G_V, 4)
            pe.wait_ge(ev("exp_p"), NH)
            pe.wait_ge(ev("kout_ready"), 1)
            for q in range(2):
                for h in range(HP):
                    ins = tr(B[6 + q][:, P * h:P * (h + 1)], probs_p[:, q, h, :], ident)
                ins.then_inc(ev("pT_ps"), 1)
            project_with_levels(G_U, 5)
            pe.wait_ge(ev("pT_ready"), 2)
            for h in range(HP):
                for q in range(2):
                    head = 2 * h + q
                    ins = mm(B[4][:, HD * head:HD * (head + 1)], pT_p[:, q, P * h:P * (h + 1)],
                             v[:, 0, HD * head:HD * (head + 1)], start=True, stop=True)
            ins.then_inc(ev("att_p_ps"), 1)
            pe.wait_ge(ev("vg_ready"), 2)
            for g in range(GM):
                ins = mm(B[5][:, P * g:P * (g + 1)], wsT[:, g, :],
                         rows[:, :, 768 + HD * g:768 + HD * (g + 1)], start=True, stop=True)
            ins.then_inc(ev("z_ps"), 1)
            project(H_G, between=lambda: level(5, 1))

            level(6, 0)
            pe.wait_ge(ev("gmlp_ready"), 1)
            scores(4, 1, lambda hd, h: kT[hd, h, 1, :])
            level(6, 1)
            scores(6, 1, lambda hd, h: ckT[hd, h, :]).then_inc(ev("score_s"), 1)
            pe.wait_ge(ev("end_ready"), 4)
            for d in range(2):
                for h in range(RP):
                    ins = tr(B[1][:, P * (2 * d + h):P * (2 * d + h + 1)], Kend[:, d, h, :], ident)
            ins.then_inc(ev("kst_ps"), 1)
            pe.wait_ge(ev("lvl_store"), 30)
            pe.wait_ge(ev("mixer_loaded"), 144)
            for q in range(2):
                if q:
                    pe.wait_ge(ev("ctx_sc"), 2)
                    mod_sums(4)
                for g in range(G):
                    for h in range(RP):
                        out = B[2 + q][:, 256 * g + HD * h:256 * g + HD * (h + 1)]
                        m = 2 * h + g
                        ins = mm(out, AT[:, q, P * m:P * (m + 1)], hi[:, g, HD * (2 * h + q):HD * (2 * h + q + 1)],
                                 start=True, stop=g == 0)
                        for d in range(2 if g else 0):
                            ins = mm(out, Qend[HD * q:HD * (q + 1), d, h, :], s0[HD * q:HD * (q + 1), d, h, :],
                                     start=False, stop=d == 1)
            ins.then_inc(ev("o_ps"), 1)
            mod_sums(5)
            pe.wait_ge(ev("kst_ready"), 1)
            pe.wait_ge(ev("silu_g"), 1)
            for d in range(2):
                for h in range(RH):
                    ins = mm(B[0][0:HD, 256 * d + HD * h:256 * d + HD * (h + 1)],
                             kstT[:, d, h // 2, HD * (h % 2):HD * (h % 2 + 1)], hi[:, 0, HD * h:HD * (h + 1)], start=True, stop=True)
            ins.then_inc(ev("state_ps"), 1)

            def cat_transpose(g, kh, bank):
                for k in range(4):
                    ins = tr(B[bank][:, P * k:P * (k + 1)], rows[:, g, P * (4 * kh + k):P * (4 * kh + k + 1)], ident)
                ins.then_inc(ev("cat_ps"), 1)

            def probs_transpose(q):
                pe.wait_ge(ev("exp_s"), 2 * q + 2)
                for n in range(4 * q, 4 * q + 4):
                    ins = tr(B[4 + q % 2][:, P * (n % 4):P * (n % 4 + 1)], probs[:, n // 2, P * (n % 2):P * (n % 2 + 1)], ident)
                ins.then_inc(ev("sT_ps"), 1)

            def project_out(i):
                slot_wait(AT_WOUT + i)
                w = ring[:, (AT_WOUT + i) % RING, :].rearrange("p (k n) -> p k n", k=2)
                for t in range(2):
                    for kk in range(2):
                        for half in range(2):
                            ins = mm(B[2 * t + half], catT[:, 2 * WOUT[i] + kk, t, :], w[:, kk, 512 * half:512 * (half + 1)],
                                     start=i == 0 and kk == 0, stop=i == 3 and kk == 1)
                    if t == 0 and i == 3:
                        ins.then_inc(ev("wout_ps"), 1)
                ins.then_inc(chunks_used, 1)

            mod_spread(4)
            mod_spread(5)
            pe.wait_ge(ev("state_ready"), 1)
            mod_sums(6)
            mod_sums(7)
            pe.wait_ge(ev("local_sc"), 2)
            pe.wait_ge(ev("hgrn_ready"), 1)
            pe.wait_ge(ev("mod_out"), 4)
            cat_transpose(0, 1, 6)
            cat_transpose(1, 1, 7)
            mod_spread(6)
            mod_spread(7)
            probs_transpose(0)
            probs_transpose(1)
            mod_sums(8)
            mod_sums(9)
            pe.wait_ge(ev("sT_ready"), 1)
            probs_transpose(2)
            pe.wait_ge(ev("sT_ready"), 2)
            probs_transpose(3)
            mod_spread(8)
            mod_spread(9)
            pe.wait_ge(ev("catT_ready"), 2)
            for n in range(16):
                if n % 4 == 0:
                    pe.wait_ge(ev("sT_ready"), n // 4 + 1)
                head = n // 2
                src = (sT_lo if n < 8 else sT_hi)[:, P * (n % 8):P * (n % 8 + 1)]
                val = (cv if n % 2 else v[:, 1, :])[:, HD * head:HD * (head + 1)]
                ins = mm(B[6][:, HD * head:HD * (head + 1)], src, val, start=n % 2 == 0, stop=n % 2 == 1)
            ins.then_inc(ev("att_s_ps"), 1)
            pe.wait_ge(ev("mod_out"), 8)
            pe.wait_ge(ev("o_out"), 2)
            project_out(0)
            cat_transpose(0, 0, 7)
            pe.wait_ge(ev("att_s"), 1)
            cat_transpose(1, 0, 5)
            project_out(1)
            pe.wait_ge(ev("catT_ready"), 4)
            project_out(2)
            project_out(3)
            pe.wait_ge(ev("catT_ready"), 4)
            mod_sums(10)
            mod_sums(11)

            pe.wait_ge(ev("x1_ready"), 4)
            keep_clock(3, B[4])
            for t in range(2):
                pe.wait_ge(ev("h2_ready"), t + 1)
                for q in range(2):
                    if t:
                        pe.wait_ge(ev("h2T_ready"), q + 1)
                    for k in range(4):
                        ins = tr(B[2 + q][:, P * k:P * (k + 1)], rows[:, t, P * (4 * q + k):P * (4 * q + k + 1)], ident)
                    ins.then_inc(ev("h2T_ps"), 1)
                keep_clock(1, B[4])
                pe.wait_ge(ev("h2T_ready"), 2 * t + 2)
                out = B[0][:, NE * t:NE * (t + 1)]
                mm(out, ones_rows, rbias, start=True, stop=False)
                for k in range(KT):
                    ins = mm(out, h2T[:, k, t, :], rw[:, k, :], start=False, stop=k == KT - 1)
            ins.then_inc(ev("logits_ps"), 1)
            mod_spread(10)
            mod_spread(11)
            keep_clock(1, B[2])
            pe.wait_ge(ev("mask_ready"), 1)
            tri = cst[:, C_TRI:C_TRI + P]
            mm(B[1][:, 0:NE], tri, msk[:, 0, :], start=True, stop=True)
            mm(B[1][:, NE:2 * NE], tri, msk[:, 1, :], start=True, stop=False)
            mm(B[1][:, NE:2 * NE], ones[:, 0:1].to_broadcast([P, P]), msk[:, 0, :], start=False, stop=True)
            for t in range(2):
                ins = mm(B[1][:, 64:65], mask4[:, t].rearrange("p r e -> p (r e)"), ones[:, 0:1], start=t == 0, stop=t == 1)
            ins.then_inc(ev("rank_ps"), 1)
            keep_clock(2, B[2])
            pe.wait_ge(ev("rank_ready"), 1)
            pe.wait_ge(ev("gate_ready"), 1)
            pe.wait_ge(ev("flag_ready"), 1)
            for t in range(2):
                tr(B[1][0:NE, P * t:P * (t + 1)], rank[:, t, 0:NE], ident)
                ins = tr(B[1][0:NE, 256 + P * t:256 + P * (t + 1)], gate[:, t, :], ident)
            ins.then_inc(ev("rgT_ps"), 1)
            mm(B[0][:, 64:65], cst[:, C_STRI:C_STRI + P], flag, start=True, stop=True).then_inc(ev("pos_ps"), 1)

            def spread(buf, count):
                pe.wait_ge(ev("route_ready"), count + 1)
                mm(B[3], pick[:, buf, :], rgT, start=True, stop=True).then_inc(ev("bc_ps"), 1)

            def gather(count, between=None):
                pe.wait_ge(ev("gT_ready"), count + 1)
                for k in range(KT):
                    if between and k == KT // 2:
                        between()
                    for t in range(2):
                        ins = mm(B[3][:, CAP * k:CAP * (k + 1)], rows[:, t, P * k:P * (k + 1)], Ptok[:, t, :],
                                 start=t == 0, stop=t == 1)
                ins.then_inc(ev("xe_ps"), 1)

            def product(bank, m, buf, lhsT, count):
                for half in range(2 if m < 2 else 0):
                    cols = slice(512 * half, 512 * (half + 1))
                    mm(bank[CAP * half:CAP * (half + 1), :], pick[:, buf, 0:CAP], mbias[:, m, cols], start=True, stop=False)
                for r in range(4):
                    cidx = 4 * m + r
                    pe.wait_ge(slot_loaded[expert_slot(cidx)], chunk_loads(cidx, count))
                    w = ring[:, expert_slot(cidx), :].rearrange("p (k n) -> p k n", k=2)
                    for kk in range(2):
                        for half in range(2):
                            ins = mm(bank[CAP * half:CAP * (half + 1), :], lhsT(2 * r + kk), w[:, kk, 512 * half:512 * (half + 1)],
                                     start=m == 2 and r == 0 and kk == 0, stop=r == 3 and kk == 1)
                    ins.then_inc(chunks_used, 1)

            def combine(buf, stored):
                pe.wait_ge(ev("y_sb"), stored)
                for t in range(2):
                    for half in range(2):
                        r = slice(CAP * half, CAP * (half + 1))
                        ins = mm(B[4 + 2 * t + half], gT[r, buf, P * t:P * (t + 1)], ysb[r, :], start=False, stop=False)
                ins.then_inc(ev("combined"), 1)

            def xe_tile(k):
                return xe[:, k, :]

            def a_tile(k):
                return aT[:, k % 4, CAP * (k // 4):CAP * (k // 4 + 1)]

            def down(buf, count):
                pe.wait_ge(ev("a_ready"), count + 1)
                for q in range(4):
                    ins = tr(B[2][:, P * q:P * (q + 1)], ab[:, P * q:P * (q + 1)], ident)
                ins.then_inc(ev("aT_ps"), 1)
                pe.wait_ge(ev("aT_ready"), count + 1)
                product(B[2], 2, buf, a_tile, count)

            def open_sums(t):
                for half in range(2):
                    mm(B[4 + 2 * t + half], rgT[:, 256 + P * t:256 + P * (t + 1)], mbias[:, 2, 512 * half:512 * (half + 1)],
                       start=True, stop=False)

            keep_clock(2, B[2])
            pe.wait_ge(ev("rgT_ready"), 1)
            spread(0, 0)
            pe.wait_ge(ev("onehot_ready"), 1)
            mm(B[0][:, 128:144], cst[:, C_OFF:C_OFF + 1].to_broadcast([P, P]), onehot, start=True, stop=True)
            mm(B[0][:, 144:160], cst[:, C_E:C_E + 1].to_broadcast([P, P]), onehot, start=True, stop=True)
            mm(B[0][:, 160:161], ones[:, 0:1].to_broadcast([P, P]), flag, start=True, stop=True).then_inc(ev("list_ps"), 1)
            pe.wait_ge(ev("mbias_loaded"), 48)
            pe.wait_ge(ev("mod_out"), 10)
            open_sums(0)
            gather(0, between=lambda: open_sums(1))
            keep_clock(1, B[2])
            pe.wait_ge(ev("over_list"), 1)
            with pe.Fori(0, NE // 2) as i:
                for u in range(2):
                    e = i * 2 + u
                    pe.wait_ge(ev("xe_ready"), e + 1)
                    product(B[0], 0, u, xe_tile, e)
                    combine(1 - u, e + 1)
                    spread(1 - u, e + 1)
                    product(B[1], 1, u, xe_tile, e)
                    gather(e + 1)
                    down(u, e)
            combine(1, NE + 1)
            n_over = pe.value_load(small_i[0:1, 16:17], min_val=0, max_val=MAX_OVER)
            with pe.If(n_over > 0):
                with pe.Fori(0, MAX_OVER) as j:
                    with pe.If(n_over > j):
                        spread(0, j + (NE + 1))
                        gather(j + (NE + 1))
                        pe.wait_ge(ev("xe_ready"), j + (NE + 2))
                        product(B[0], 0, 0, xe_tile, j + NE)
                        product(B[1], 1, 0, xe_tile, j + NE)
                        down(0, j + NE)
                        combine(0, j + (NE + 2))
            for n in range(4):
                ins = mm(B[4 + n][:, 0:16], zeros, cst[:, 0:16], start=False, stop=True)
            ins.then_inc(ev("moe_done"), 1)


_INS = ['x_prompt', 'x_sample', 'cache_k', 'cache_v', 'state_hgrn_fwd', 'state_hgrn_bwd', 'c', 'c_ctx',
        'w_mod', 'b_mod', 'norm1_g', 'norm2_g', 'w_in', 'na_rel_bias', 'hgrn_lb', 'hgrn_onorm_g',
        'gmlp_vnorm_g', 'gmlp_ws', 'gmlp_b', 'w_out', 'router_w', 'router_b', 'w_gate', 'b_gate',
        'w_up', 'b_up', 'w_down', 'b_down', 'final_g']
_OUTS = [(1, P, D), (1, P, D), (1, 1, P, NH, HD), (1, 1, P, NH, HD), (1, 1, RH, HD, HD), (1, 1, RH, HD, HD)]


def kernel(**inputs):
    import concourse.bacc as bacc
    from concourse.bass_utils import run_bass_kernel_spmd

    nc = bacc.Bacc("TRN2", target_bir_lowering=False, num_devices=1)
    arrays, args = {}, []
    const_f32, const_masks = shape_constants()
    given = [(name, inputs[name]) for name in _INS] + [("const_f32", const_f32), ("const_masks", const_masks)]
    for name, array in given:
        array = np.ascontiguousarray(array)
        arrays[f"in_{name}"] = array
        args.append(nc.dram_tensor(f"in_{name}", array.shape, mybir.dt.from_np(array.dtype), kind="ExternalInput").ap())
    for i, shape in enumerate(_OUTS):
        args.append(nc.dram_tensor(f"out_{i}", shape, F32, kind="ExternalOutput").ap())
    hybrid_layer(nc, *args)
    r = run_bass_kernel_spmd(nc, [arrays], core_ids=[0])
    return tuple(r.results[0][f"out_{i}"] for i in range(len(_OUTS)))
```
